# Optimizing a Trainium2 kernel written in Bass

```python
import jax
import jax.numpy as jnp
from jax import lax
import numpy as np

"""One inference step (DEPTH layers) of a hybrid autoregressive decoder trunk, run for a
prompt group and a sample group with the same parameters.

Per layer (post-norm DeepNorm):
  x <- LayerNorm(ALPHA * x + Mixer(x));  x <- LayerNorm(ALPHA * x + FFN(x))
Mixer: one combined input projection whose columns are split into
  (A) causal multi-scale pooling mixer (4 channel groups, trailing windows 2/4/8/16),
  (B) Conformer convolution module (GLU -> depthwise causal conv width 31 -> LayerNorm -> swish),
  (C) Griffin recurrent branch (width-4 causal conv -> RG-LRU, times GeLU gate branch),
  plus 3 per-channel sigmoid merge gates; each branch is projected to D_MODEL, merged by
  its gate, then one output projection.
FFN: dense SwiGLU on even layers, top-2-of-8 expert SwiGLU on odd layers.

Inputs:
  x_prompt (BATCH, SEQ, D_MODEL), x_sample (DEC_BATCH, DEC_SEQ, D_MODEL)
  state_pool     (DEPTH, DEC_BATCH, POOL_BUF, D_POOL)       last 15 pooling-input rows
  state_conv     (DEPTH, DEC_BATCH, CONV_BUF, D_CONV)       last 30 GLU-output rows
  state_lru_conv (DEPTH, DEC_BATCH, LRU_CONV_BUF, D_LRU)    last 3 pre-conv RG-LRU rows
  state_lru_h    (DEPTH, DEC_BATCH, D_LRU)                  RG-LRU hidden state
Output tuple:
  (y_prompt (BATCH, SEQ, D_MODEL), y_sample (DEC_BATCH, DEC_SEQ, D_MODEL),
   new_state_pool_prompt (DEPTH, BATCH, POOL_BUF, D_POOL),
   new_state_conv_prompt (DEPTH, BATCH, CONV_BUF, D_CONV),
   new_state_lru_conv_prompt (DEPTH, BATCH, LRU_CONV_BUF, D_LRU),
   new_state_lru_h_prompt (DEPTH, BATCH, D_LRU),
   new_state_pool_sample (DEPTH, DEC_BATCH, POOL_BUF, D_POOL),
   new_state_conv_sample (DEPTH, DEC_BATCH, CONV_BUF, D_CONV),
   new_state_lru_conv_sample (DEPTH, DEC_BATCH, LRU_CONV_BUF, D_LRU),
   new_state_lru_h_sample (DEPTH, DEC_BATCH, D_LRU))
"""

D_MODEL = 1024
BATCH = 1
SEQ = 256
DEPTH = 2
DEC_BATCH = 8
DEC_SEQ = 1
PAST_LEN = 2048
PAGE_SIZE = 128

D_POOL = D_MODEL // 2
N_POOL_GROUPS = 4
POOL_GROUP = D_POOL // N_POOL_GROUPS
POOL_WINDOWS = (2, 4, 8, 16)
POOL_BUF = max(POOL_WINDOWS) - 1
D_CONV = D_MODEL // 2
CONV_WIDTH = 31
CONV_BUF = CONV_WIDTH - 1
D_LRU = D_MODEL // 2
N_LRU_BLOCKS = 8
LRU_BLOCK = D_LRU // N_LRU_BLOCKS
LRU_CONV_WIDTH = 4
LRU_CONV_BUF = LRU_CONV_WIDTH - 1
LRU_C = 8.0
N_BRANCH = 3
IN_COLS = D_POOL + 2 * D_CONV + 2 * D_LRU + N_BRANCH * D_MODEL
D_FF = 2816
N_EXPERTS = 8
TOP_K = 2
D_EXPERT = 3584
N_DENSE = (DEPTH + 1) // 2
N_MOE = DEPTH // 2
ALPHA = (2.0 * DEPTH) ** 0.25
BETA = (8.0 * DEPTH) ** -0.25
LN_EPS = 1e-5

kernel_name = "hybrid_pool_conformer_rglru_decoder_step"

def layer_norm(x, g, b):
    xf = x.astype(jnp.float32)
    mu = jnp.mean(xf, axis=-1, keepdims=True)
    var = jnp.mean(jnp.square(xf - mu), axis=-1, keepdims=True)
    y = (xf - mu) * lax.rsqrt(var + LN_EPS) * g.astype(jnp.float32) + b.astype(jnp.float32)
    return y.astype(x.dtype)

def causal_depthwise_conv(u, prev, w, b):
    width = w.shape[0]
    u_ext = jnp.concatenate([prev.astype(u.dtype), u], axis=1)
    y = lax.conv_general_dilated(
        u_ext, w[:, None, :].astype(u.dtype), window_strides=(1,), padding='VALID',
        dimension_numbers=('NWC', 'WIO', 'NWC'), feature_group_count=u.shape[-1])
    return y + b, u_ext[:, u_ext.shape[1] - (width - 1):]

def pool_mixer(u, prev, start_pos, w_pool, scale):
    B, T, _ = u.shape
    u_ext = jnp.concatenate([prev.astype(u.dtype), u], axis=1)
    cs = jnp.cumsum(u_ext.astype(jnp.float32), axis=1)
    cs = jnp.concatenate([jnp.zeros((B, 1, D_POOL), jnp.float32), cs], axis=1)
    end = cs[:, POOL_BUF + 1:]
    pos = (start_pos + jnp.arange(T))[:, None]
    groups = []
    for g, w in enumerate(POOL_WINDOWS):
        sl = slice(g * POOL_GROUP, (g + 1) * POOL_GROUP)
        start = cs[:, POOL_BUF + 1 - w:POOL_BUF + 1 - w + T, sl]
        cnt = jnp.minimum(w, pos + 1).astype(jnp.float32)
        groups.append((end[..., sl] - start) / cnt)
    pooled = jnp.concatenate(groups, axis=-1) - u.astype(jnp.float32)
    pooled = pooled.astype(u.dtype).reshape(B, T, N_POOL_GROUPS, POOL_GROUP)
    mixed = jnp.einsum('btgc,gcd->btgd', pooled, w_pool).reshape(B, T, D_POOL) * scale
    return mixed, u_ext[:, T:]

def rg_lru(xc, h0, start_pos, w_a, b_a, w_x, b_x, lam):
    B, T, _ = xc.shape
    xb = xc.reshape(B, T, N_LRU_BLOCKS, LRU_BLOCK)
    r = jax.nn.sigmoid((jnp.einsum('btnc,ncd->btnd', xb, w_a).reshape(B, T, D_LRU) + b_a).astype(jnp.float32))
    i = jax.nn.sigmoid((jnp.einsum('btnc,ncd->btnd', xb, w_x).reshape(B, T, D_LRU) + b_x).astype(jnp.float32))
    log_a = -LRU_C * r * jax.nn.softplus(-lam.astype(jnp.float32))
    reset = ((start_pos + jnp.arange(T)) == 0)[None, :, None]
    mult = jnp.where(reset, 1.0, jnp.sqrt(-jnp.expm1(2.0 * log_a)))
    a = jnp.where(reset, 0.0, jnp.exp(log_a))
    bterm = mult * i * xc.astype(jnp.float32)
    bterm = bterm.at[:, 0].add(a[:, 0] * h0.astype(jnp.float32))

    def combine(left, right):
        a1, b1 = left
        a2, b2 = right
        return a1 * a2, a2 * b1 + b2

    _, h = lax.associative_scan(combine, (a, bterm), axis=1)
    return h, h[:, -1]

def swiglu(x, w_gate, w_up, w_down):
    return (jax.nn.silu(x @ w_gate) * (x @ w_up)) @ w_down

def moe_swiglu(x, router, w_gate, w_up, w_down):
    B, T, D = x.shape
    xt = x.reshape(B * T, D)
    logits = (xt @ router).astype(jnp.float32)
    top_vals, top_idx = lax.top_k(logits, TOP_K)
    gates = jax.nn.softmax(top_vals, axis=-1)
    combine = jnp.sum(jax.nn.one_hot(top_idx, N_EXPERTS, dtype=jnp.float32) * gates[..., None], axis=1)
    y = jnp.zeros((B * T, D), jnp.float32)
    for e in range(N_EXPERTS):
        y_e = swiglu(xt, w_gate[e], w_up[e], w_down[e])
        y = y + combine[:, e:e + 1] * y_e.astype(jnp.float32)
    return y.astype(x.dtype).reshape(B, T, D)

def setup_inputs(seed: int = 0) -> dict:
    key = jax.random.key(seed)
    ks = list(jax.random.split(key, 40))
    kit = iter(ks)

    def nrm(shape, scale):
        return jax.random.normal(next(kit), shape, jnp.float32) * scale

    def gain(shape):
        return 1.0 + nrm(shape, 0.05)

    x_prompt = nrm((BATCH, SEQ, D_MODEL), 1.0)
    x_sample = nrm((DEC_BATCH, DEC_SEQ, D_MODEL), 1.0)
    state_pool = nrm((DEPTH, DEC_BATCH, POOL_BUF, D_POOL), 1.0)
    state_conv = nrm((DEPTH, DEC_BATCH, CONV_BUF, D_CONV), 0.5)
    state_lru_conv = nrm((DEPTH, DEC_BATCH, LRU_CONV_BUF, D_LRU), 1.0)
    state_lru_h = nrm((DEPTH, DEC_BATCH, D_LRU), 0.5)

    w_in = nrm((DEPTH, D_MODEL, IN_COLS), D_MODEL ** -0.5)
    b_gate = nrm((DEPTH, N_BRANCH * D_MODEL), 0.02)
    w_pool = nrm((DEPTH, N_POOL_GROUPS, POOL_GROUP, POOL_GROUP), POOL_GROUP ** -0.5)
    pool_scale = gain((DEPTH, D_POOL))
    conv_w = nrm((DEPTH, CONV_WIDTH, D_CONV), CONV_WIDTH ** -0.5)
    conv_b = nrm((DEPTH, D_CONV), 0.02)
    conv_ln_g = gain((DEPTH, D_CONV))
    conv_ln_b = nrm((DEPTH, D_CONV), 0.02)
    lru_conv_w = nrm((DEPTH, LRU_CONV_WIDTH, D_LRU), LRU_CONV_WIDTH ** -0.5)
    lru_conv_b = nrm((DEPTH, D_LRU), 0.02)
    lru_wa = nrm((DEPTH, N_LRU_BLOCKS, LRU_BLOCK, LRU_BLOCK), LRU_BLOCK ** -0.5)
    lru_ba = nrm((DEPTH, D_LRU), 0.02)
    lru_wx = nrm((DEPTH, N_LRU_BLOCKS, LRU_BLOCK, LRU_BLOCK), LRU_BLOCK ** -0.5)
    lru_bx = nrm((DEPTH, D_LRU), 0.02)
    a0 = jax.random.uniform(next(kit), (DEPTH, D_LRU), jnp.float32, 0.9, 0.999)
    lru_lambda = jnp.log(a0) - jnp.log1p(-a0)
    w_br_pool = nrm((DEPTH, D_POOL, D_MODEL), D_POOL ** -0.5)
    w_br_conv = nrm((DEPTH, D_CONV, D_MODEL), D_CONV ** -0.5)
    w_br_lru = nrm((DEPTH, D_LRU, D_MODEL), D_LRU ** -0.5)
    w_out = nrm((DEPTH, D_MODEL, D_MODEL), BETA * D_MODEL ** -0.5)
    ln1_g = gain((DEPTH, D_MODEL))
    ln1_b = nrm((DEPTH, D_MODEL), 0.02)
    ln2_g = gain((DEPTH, D_MODEL))
    ln2_b = nrm((DEPTH, D_MODEL), 0.02)
    ffn_w_gate = nrm((N_DENSE, D_MODEL, D_FF), D_MODEL ** -0.5)
    ffn_w_up = nrm((N_DENSE, D_MODEL, D_FF), D_MODEL ** -0.5)
    ffn_w_down = nrm((N_DENSE, D_FF, D_MODEL), BETA * D_FF ** -0.5)
    moe_router = nrm((N_MOE, D_MODEL, N_EXPERTS), D_MODEL ** -0.5)
    moe_w_gate = nrm((N_MOE, N_EXPERTS, D_MODEL, D_EXPERT), D_MODEL ** -0.5)
    moe_w_up = nrm((N_MOE, N_EXPERTS, D_MODEL, D_EXPERT), D_MODEL ** -0.5)
    moe_w_down = nrm((N_MOE, N_EXPERTS, D_EXPERT, D_MODEL), BETA * D_EXPERT ** -0.5)
    return {
        "x_prompt": x_prompt, "x_sample": x_sample,
        "state_pool": state_pool, "state_conv": state_conv,
        "state_lru_conv": state_lru_conv, "state_lru_h": state_lru_h,
        "w_in": w_in, "b_gate": b_gate, "w_pool": w_pool, "pool_scale": pool_scale,
        "conv_w": conv_w, "conv_b": conv_b, "conv_ln_g": conv_ln_g, "conv_ln_b": conv_ln_b,
        "lru_conv_w": lru_conv_w, "lru_conv_b": lru_conv_b, "lru_wa": lru_wa, "lru_ba": lru_ba,
        "lru_wx": lru_wx, "lru_bx": lru_bx, "lru_lambda": lru_lambda,
        "w_br_pool": w_br_pool, "w_br_conv": w_br_conv, "w_br_lru": w_br_lru, "w_out": w_out,
        "ln1_g": ln1_g, "ln1_b": ln1_b, "ln2_g": ln2_g, "ln2_b": ln2_b,
        "ffn_w_gate": ffn_w_gate, "ffn_w_up": ffn_w_up, "ffn_w_down": ffn_w_down,
        "moe_router": moe_router, "moe_w_gate": moe_w_gate, "moe_w_up": moe_w_up,
        "moe_w_down": moe_w_down,
    }

def reference(x_prompt, x_sample, state_pool, state_conv, state_lru_conv, state_lru_h,
              w_in, b_gate, w_pool, pool_scale, conv_w, conv_b, conv_ln_g, conv_ln_b,
              lru_conv_w, lru_conv_b, lru_wa, lru_ba, lru_wx, lru_bx, lru_lambda,
              w_br_pool, w_br_conv, w_br_lru, w_out, ln1_g, ln1_b, ln2_g, ln2_b,
              ffn_w_gate, ffn_w_up, ffn_w_down, moe_router, moe_w_gate, moe_w_up, moe_w_down):

    def mixer(l, x, prev_pool, prev_conv, prev_lru_conv, h0, start_pos):
        B, T, _ = x.shape
        proj = jnp.einsum('btd,dc->btc', x, w_in[l])
        o1 = D_POOL
        o2 = o1 + D_CONV
        o3 = o2 + D_CONV
        o4 = o3 + D_LRU
        o5 = o4 + D_LRU
        u_pool = proj[..., :o1]
        u_val = proj[..., o1:o2]
        u_glu = proj[..., o2:o3]
        u_lru = proj[..., o3:o4]
        u_gelu = proj[..., o4:o5]
        u_gate = proj[..., o5:]
        y_a, new_pool = pool_mixer(u_pool, prev_pool, start_pos, w_pool[l], pool_scale[l])
        y_a = y_a @ w_br_pool[l]
        glu = u_val * jax.nn.sigmoid(u_glu)
        c, new_conv = causal_depthwise_conv(glu, prev_conv, conv_w[l], conv_b[l])
        y_b = jax.nn.silu(layer_norm(c, conv_ln_g[l], conv_ln_b[l])) @ w_br_conv[l]
        xc, new_lru_conv = causal_depthwise_conv(u_lru, prev_lru_conv, lru_conv_w[l], lru_conv_b[l])
        h, h_last = rg_lru(xc, h0, start_pos, lru_wa[l], lru_ba[l], lru_wx[l], lru_bx[l], lru_lambda[l])
        y_c = (h.astype(x.dtype) * jax.nn.gelu(u_gelu)) @ w_br_lru[l]
        gates = jax.nn.sigmoid((u_gate + b_gate[l]).astype(jnp.float32)).astype(x.dtype)
        gates = gates.reshape(B, T, N_BRANCH, D_MODEL)
        merged = gates[:, :, 0] * y_a + gates[:, :, 1] * y_b + gates[:, :, 2] * y_c
        return merged @ w_out[l], new_pool, new_conv, new_lru_conv, h_last.astype(h0.dtype)

    def trunk(x, prev_pool, prev_conv, prev_lru_conv, h0, start_pos):
        pools, convs, lconvs, hs = [], [], [], []
        for l in range(DEPTH):
            m, sp, sc, slc, sh = mixer(l, x, prev_pool[l], prev_conv[l], prev_lru_conv[l], h0[l], start_pos)
            pools.append(sp)
            convs.append(sc)
            lconvs.append(slc)
            hs.append(sh)
            x = layer_norm(ALPHA * x + m, ln1_g[l], ln1_b[l])
            if l % 2 == 0:
                f = swiglu(x, ffn_w_gate[l // 2], ffn_w_up[l // 2], ffn_w_down[l // 2])
            else:
                f = moe_swiglu(x, moe_router[l // 2], moe_w_gate[l // 2], moe_w_up[l // 2], moe_w_down[l // 2])
            x = layer_norm(ALPHA * x + f, ln2_g[l], ln2_b[l])
        return x, jnp.stack(pools), jnp.stack(convs), jnp.stack(lconvs), jnp.stack(hs)

    nb = x_prompt.shape[0]
    dt = x_prompt.dtype
    y_prompt, pool_p, conv_p, lconv_p, h_p = trunk(
        x_prompt,
        jnp.zeros((DEPTH, nb, POOL_BUF, D_POOL), dt),
        jnp.zeros((DEPTH, nb, CONV_BUF, D_CONV), dt),
        jnp.zeros((DEPTH, nb, LRU_CONV_BUF, D_LRU), dt),
        jnp.zeros((DEPTH, nb, D_LRU), state_lru_h.dtype),
        0)
    y_sample, pool_s, conv_s, lconv_s, h_s = trunk(
        x_sample, state_pool, state_conv, state_lru_conv, state_lru_h, PAST_LEN)
    return (y_prompt, y_sample, pool_p, conv_p, lconv_p, h_p, pool_s, conv_s, lconv_s, h_s)


_drawn_inputs = setup_inputs


def setup_inputs(seed=0):
    import zlib

    import numpy as np

    out = dict(_drawn_inputs(seed))
    spreads = {}
    factors = {'b_gate': 8.0,
     'pool_scale': 2.925,
     'conv_b': 5.454,
     'conv_ln_g': 3.665,
     'conv_ln_b': 7.371,
     'lru_ba': 8.0,
     'lru_bx': 7.777}
    for name, (base, spread) in spreads.items():
        noise = np.random.default_rng([zlib.crc32(name.encode()), seed]).standard_normal(out[name].shape)
        drawn = base * np.exp(spread * noise) if base else spread * noise
        out[name] = jnp.asarray(drawn.astype(out[name].dtype))
    for name, factor in factors.items():
        out[name] = (out[name] * factor).astype(out[name].dtype)
    return out
```

```python
from contextlib import ExitStack

import concourse.bass as bass
from concourse import mybir

P = 128
D = 1024
KT = D // P
TP, NS_ = 256, 8
T = TP + NS_
L = 2
C4 = 4
DB = C4 * P
CW, LW, PW = 31, 4, 16
WINDOWS = (2, 4, 8, 16)
IN_COLS = DB * 5 + 3 * D
D_FF, D_EX, NE = 2816, 3584, 8
ALPHA = (2.0 * L) ** 0.25
EPS = 1e-5
WS = 64.0
CAP = 128
SLOTS = 3
PIECE = 4096
AHEAD = 2

F32 = mybir.dt.float32
F16 = mybir.dt.float16
I32 = mybir.dt.int32
ALU = mybir.AluOpType
ACT = mybir.ActivationFunctionType
X = mybir.AxisListType.X

VEC_B = ["pool_scale", "conv_b", "conv_ln_g", "conv_ln_b", "lru_conv_b", "lru_ba", "lru_bx", "lru_lambda"]
NR = len(VEC_B) + CW + LW
VEC_D = ["ln1_g", "ln1_b", "ln2_g", "ln2_b"]
NQ = 3 + len(VEC_D)
C_ID, C_IO, C_TR, C_IC, C_IX, C_ALL = 0, P, P + CAP, 2 * P + CAP, 2 * P + CAP + 64, 2 * P + CAP + 72

IN_ORDER = [("glu", 2), ("val", 1), ("lru", 3), ("pool", 0), ("gelu", 4),
            ("gate", 5, 0, 0), ("gate", 6, 0, 1), ("branch", 0),
            ("gate", 9, 2, 0), ("gate", 10, 2, 1), ("branch", 2),
            ("gate", 7, 1, 0), ("gate", 8, 1, 1), ("branch", 1), ("out", 0), ("out", 1)]
MIX = len(IN_ORDER)
NF = D_FF // P
FG = [4] * (NF // 4) + ([NF % 4] if NF % 4 else [])
DG = [8, 8, NF - 16]
FFN = 2 * len(FG) + 2 * len(DG)
PRE = 2 * MIX + FFN
NC = D_EX // 512
VISIT = 3 * NC
assert VISIT % SLOTS == 0


def visit_order():
    order = []
    for c in range(NC):
        order += [("g", c), ("u", c)]
        if c:
            order.append(("d", c - 1))
    return order + [("d", NC - 1)]


def mixer_piece(l):
    return l * (MIX + FFN)


def psum_plan():
    used = [0] * 8
    place = {}
    turn = [0]

    def put(name, bank=None):
        if bank is None:
            bank = turn[0] % 8
            turn[0] += 1
        place[name] = (bank, used[bank])
        used[bank] += 1

    for k in range(KT):
        put(("xT", k))
    put("par512")
    put("par1024")
    for l in range(L):
        for h in range(2):
            put(("st_conv", l, h))
        put(("st_pool", l))
        put(("st_lru", l))
    for l in range(L):
        for s, what in enumerate(IN_ORDER):
            if what[0] == "branch":
                if what[1] == 1:
                    put(("cmean", l))
                    put(("csq", l))
                for j in range(KT):
                    put(("mix", l, s, j))
            elif what[0] == "out":
                for j in range(4):
                    put(("mix", l, s, j))
                    if what[1] == 0 and j == 1:
                        put(("mean1", l))
                        put(("msq1", l))
            else:
                for j in range(4):
                    put(("mix", l, s, j))
            if s == 5:
                for j in range(C4):
                    put(("ra", l, j))
                for j in range(C4):
                    put(("ri", l, j))
            if s == 6:
                for j in range(C4):
                    put(("pm", l, j))
            if s == 13:
                put(("so", l))
        if l == 0:
            for g, nf in enumerate(FG):
                for j in range(nf):
                    put(("fg", g, j))
                for j in range(nf):
                    put(("fu", g, j))
            for j in range(KT):
                put(("fd", j))
                if j == KT - 1:
                    put(("mean2", 0))
                    put(("msq2", 0))
    put("logits")
    put("ranks")
    for i in range(3):
        for h in range(2):
            put(("xtok", i, h))
    for h in range(2):
        put(("gath_hi", h), 6 + h)
    for h in range(2):
        put(("gath_lo", h), 1 + 2 * h)
    put(("y_init", 0), 4)
    put(("y_init", 1), 5)
    return place, used


PER_VISIT = [4, 4, 4, 4, 1, 1, 5, 6]


def trunk_kernel(nc, A, O):
    place, base = psum_plan()
    order = visit_order()

    with ExitStack() as ctx:
        def sb(name, shape, dt=F32):
            return ctx.enter_context(nc.sbuf_tensor(name, shape, dt))

        def sem(name):
            return ctx.enter_context(nc.semaphore(name))

        stage = sb("stage", [P, SLOTS, PIECE])
        w_hi = sb("w_hi", [P, SLOTS, PIECE], F16)
        w_lo = sb("w_lo", [P, SLOTS, PIECE], F16)
        x = sb("x", [P, KT, T])
        xh = sb("xh", [P, KT, T], F16)
        xl = sb("xl", [P, KT, T], F16)
        z = sb("z", [P, KT, T])
        zsq = sb("zsq", [P, KT, T])
        merged = zsq
        conv_sq = z[:, 0:C4, :]
        rt = z[:, 0:C4, :]
        pooled = z[:, C4:KT, :]
        y_pool = z[:, C4:KT, :]
        win_s = sb("win_s", [P, L, C4, NS_, CW])
        pool_s = sb("pool_s", [P, L, C4, NS_, PW])
        lru_s = sb("lru_s", [P, L, C4, NS_, LW])
        h0_s = sb("h0_s", [P, L, C4, NS_])
        consts = sb("consts", [P, C_ALL])
        ident = consts[:, C_ID:C_ID + P]
        iota = consts[:, C_IO:C_IO + CAP]
        tri = consts[:, C_TR:C_TR + P]
        inv_cnt = consts[:, C_IC:C_IC + 64].rearrange("p (g w) -> p g w", g=4)
        idx_w = consts[:, C_IX:C_IX + NE]
        ones = sb("ones", [P, P])
        ones_d = sb("ones_d", [P, P])
        ones_b = sb("ones_b", [P, P])
        par = sb("par", [P, C4, L * NR])
        par_d = sb("par_d", [P, KT, L * NQ])
        sp4 = sb("sp4", [P, C4, L])
        spt = sb("spt", [P, 6, C4, L])
        w_pool = sb("w_pool", [P, C4, P])
        w_a = sb("w_a", [P, C4, P])
        w_x = sb("w_x", [P, C4, P])
        stat = sb("stat", [P, 3, T])
        w_rt = sb("w_rt", [P, KT, NE])
        visits_i = sb("visits_i", [P, 1], I32)
        route = sb("route", [P, 12, 3, NE])
        route1 = sb("route1", [P, 8, 3])
        rank = sb("rank", [P, 3, NE])
        gate_split = sb("gate_split", [P, 3, NE, 2], F16)
        gate_slot = sb("gate_slot", [P, 1])
        ident16 = sb("ident16", [P, P], F16)

        ARENA = 12600
        arena = sb("arena", [P, ARENA])
        at = [0]

        def carve(shape, dt=F32, start=None):
            n = 1
            for s in shape:
                n *= s
            words = n if dt == F32 else (n + 1) // 2
            o = at[0] if start is None else start
            at[0] = o + words
            assert at[0] <= ARENA
            v = arena[:, o:o + words]
            v = v.bitcast(dt)[:, 0:n] if dt != F32 else v
            if len(shape) == 2:
                v = v.rearrange("p (a b) -> p a b", a=shape[0])
            if len(shape) == 3:
                v = v.rearrange("p (a b c) -> p a b c", a=shape[0], b=shape[1])
            return v

        x_rows = carve([2, D], start=0)
        xs_rows = carve([D])
        conv_rows = carve([L, 2, DB])
        pool_rows = carve([L, DB])
        lru_rows = carve([L, DB])
        par_rows = carve([DB])
        pard_rows = carve([D])
        gates = carve([KT, T], start=0)
        glu = carve([C4, CW - 1 + TP])
        conv = carve([C4, T])
        upool_at = at[0]
        upool = carve([C4, PW - 1 + TP])
        hseq = carve([C4, T], start=upool_at)
        at[0] = upool_at + C4 * (PW - 1 + TP)
        ulru_at = at[0]
        ulru = carve([C4, LW - 1 + TP])
        rq = carve([C4, T], start=ulru_at)
        xc = carve([C4, T])
        ig = carve([C4, T])
        gelu = carve([C4, T])
        sg = carve([C4, T])
        a_lru = sg
        brh = carve([C4, T], F16)
        brl = carve([C4, T], F16)
        so = carve([C4, 81])
        so_out = carve([DB])
        wsum = carve([2, PW - 1 + TP], start=0)
        prod = stat[:, 2, 0:NS_ * CW].rearrange("p (b k) -> p b k", b=NS_)
        hdh = carve([NF, T], F16, start=0)
        hdl = carve([NF, T], F16)
        silu_d = carve([4, T])
        h_d = carve([4, T])
        xth = carve([3, D], F16, start=0)
        xtl = carve([3, D], F16)
        xgh = carve([KT, CAP], F16)
        xgl = carve([KT, CAP], F16)
        silu_e = carve([2, 512])
        h_e = carve([2, 512])
        hh = carve([2, 512], F16)
        hl = carve([2, 512], F16)
        yh = carve([D], F16)
        yl = carve([D], F16)
        onehot = carve([3, CAP], F16)
        onehot_t = carve([T], F16)
        gsel = carve([3, 2], F16)
        y_rows = carve([3, D])

        ps = ctx.enter_context(nc.psum_tensor("ps", [P, 8, 512], F32))

        names = """ld_x ld_const ld_par ld_state ld_small out_dma y_out hi_done lo_done down_used
            x_hi x_split zeroed rows_zeroed dve gates_zeroed xc_ready tanh_ready q_ready root_ready h_ready
            hg_ready br_hi br_ready pooled_ready conv_done csq_done cv_ready silu_ready merge_done
            mg_ready mg_hi mg_split packed zsq_ready m2_ready var_ready std_ready nz_ready norm_ready
            f_hi f_split gd_ready gs_ready mask_ready visits_ready sp_abs sp_exp sp_done
            xt_hi onehot_ready rank_next e_hi e_split y_hi cm2_ready cvar_ready cstd_ready""".split()
        S = {n: sem(n) for n in names}
        stage_full = [sem(f"stage_full{i}") for i in range(SLOTS)]
        bank_full = [sem(f"bank_full{i}") for i in range(8)]
        bank_free = [sem(f"bank_free{i}") for i in range(8)]

        def bank(name):
            return ps[:, place[name][0], :]

        def filled(eng, name):
            b, k = place[name]
            eng.wait_ge(bank_full[b], k + 1)

        def empty(eng, name):
            b, k = place[name]
            if k:
                eng.wait_ge(bank_free[b], k)

        def read_out(eng, name):
            b, k = place[name]
            eng.wait_ge(bank_free[b], k + 1)

        def in_visit(sems, b, v, i):
            return sems[b], v * PER_VISIT[b] + (base[b] + i + 1)

        def free_of(name):
            return bank_free[place[name][0]]

        def full_of(name):
            return bank_full[place[name][0]]

        def vec(name, l, j):
            r = VEC_B.index(name) * L + l
            return par[:, j, r:r + 1]

        def conv_tap(l, j, k, n=1):
            r = len(VEC_B) * L + l * CW + k
            return par[:, j, r:r + n]

        def lru_tap(l, j, k, n=1):
            r = (len(VEC_B) + CW) * L + l * LW + k
            return par[:, j, r:r + n]

        def gate_bias(l, b, d):
            return par_d[:, d, l * 3 + b:l * 3 + b + 1]

        def vec_d(name, l, d):
            r = 3 * L + VEC_D.index(name) * L + l
            return par_d[:, d, r:r + 1]

        def piece_done(eng, n):
            last = last_tile[n]
            if last is None:
                eng.wait_ge(S["down_used"], down_no[n])
            else:
                filled(eng, last)

        def wh(slot, k, c0, c1, width):
            return w_hi[:, slot, k * width + c0:k * width + c1]

        def wl(slot, k, c0, c1, width):
            return w_lo[:, slot, k * width + c0:k * width + c1]

        class Steps:

            def __init__(self, eng, s):
                self.eng, self.sem, self.n = eng, s, 0

            def did(self, ins):
                self.n += 1
                ins.then_inc(self.sem, 1)
                return self.n

            def after(self, n):
                self.eng.wait_ge(self.sem, n)

            def then(self, ins):
                self.after(self.did(ins))

        def pre_piece(n):
            l, s = (0, n) if n < MIX + FFN else (1, n - MIX - FFN)
            if s < MIX:
                what = IN_ORDER[s]
                if what[0] == "branch":
                    w = (A["w_br_pool"], A["w_br_conv"], A["w_br_lru"])[what[1]]
                    return w[l].rearrange("(k p) n -> p k n", p=P), C4, D
                if what[0] == "out":
                    return (A["w_out"][l, :, what[1] * 512:(what[1] + 1) * 512]
                            .rearrange("(k p) n -> p k n", p=P)), KT, 512
                c = what[1] * 512
                return A["w_in"][l, :, c:c + 512].rearrange("(k p) n -> p k n", p=P), KT, 512
            s -= MIX
            if s < 2 * len(FG):
                w = (A["ffn_w_gate"], A["ffn_w_up"])[s % 2]
                f0 = 512 * (s // 2)
                n_ = FG[s // 2] * P
                return w[0, :, f0:f0 + n_].rearrange("(k p) n -> p k n", p=P), KT, n_
            s -= 2 * len(FG)
            half, g = s // len(DG), s % len(DG)
            f0 = sum(DG[:g]) * P
            return (A["ffn_w_down"][0, f0:f0 + DG[g] * P, half * 512:(half + 1) * 512]
                    .rearrange("(k p) n -> p k n", p=P)), DG[g], 512

        def visit_piece(e, m):
            kind, c = order[m]
            if kind == "d":
                return (A["moe_w_down"][0, e, c * 512:(c + 1) * 512, :]
                        .rearrange("a (k p) n -> (a p) k n", p=P)), 4, D
            w = A["moe_w_gate"] if kind == "g" else A["moe_w_up"]
            return w[0, e, :, c * 512:(c + 1) * 512].rearrange("a (k p) n -> (a p) k n", p=P), KT, 512

        last_tile, down_no = {}, {}
        for l in range(L):
            for s, what in enumerate(IN_ORDER):
                last_tile[mixer_piece(l) + s] = ("mix", l, s, (KT if what[0] == "branch" else 4) - 1)
        for g, nf in enumerate(FG):
            last_tile[MIX + 2 * g] = ("fg", g, nf - 1)
            last_tile[MIX + 2 * g + 1] = ("fu", g, nf - 1)
        for half in range(2):
            for g in range(len(DG)):
                n = MIX + 2 * len(FG) + half * len(DG) + g
                last_tile[n] = ("fd", 4 * half + 3) if g == len(DG) - 1 else None
                if g < len(DG) - 1:
                    down_no[n] = len(down_no) + 1
        DOWN0 = len(down_no)

        block = ctx.enter_context(nc.Block())

        @block.sync
        def _(sp):
            sp.dma_start(x_rows, A["x_prompt"][0].rearrange("(a p) n -> p a n", p=P)).then_inc(S["ld_x"], 16)
            sp.dma_start(xs_rows[0:NS_, :], A["x_sample"].rearrange("b s n -> (b s) n")).then_inc(S["ld_x"], 16)

            def load(src, tiles, width, slot):
                dst = stage[:, slot, 0:tiles * width].rearrange("p (k n) -> p k n", k=tiles)
                sp.dma_start(dst, src).then_inc(stage_full[slot], 16)

            for n in range(PRE):
                if n >= SLOTS:
                    sp.wait_ge(S["lo_done"], n - SLOTS + 1)
                load(*pre_piece(n), n % SLOTS)

            def visit(v):
                e = v % NE
                for m in range(VISIT):
                    n = PRE + m
                    sp.wait_ge(S["lo_done"], v * VISIT + (n - SLOTS + 1))
                    load(*visit_piece(bass.ds(e, 1), m), n % SLOTS)

            with sp.Fori(0, NE) as v:
                visit(v)
            sp.wait_ge(S["visits_ready"], 1)
            nv = sp.value_load(visits_i[0:1, 0:1], min_val=NE, max_val=3 * NE)
            with sp.If(nv > NE):
                with sp.Fori(NE, nv) as v:
                    visit(v)
            sp.nop()
            sp.wait_ge(S["out_dma"], 16 * 11 * L)
            sp.wait_ge(S["y_out"], 16 * 3)

        @block.gpsimd
        def _(pool):
            for l in range(L):
                for h in range(2):
                    pool.dma_start(conv_rows[0:4 * (CW - 1), l, h, :],
                                   A["state_conv"][l, 4 * h:4 * h + 4].rearrange("b r n -> (b r) n")
                                   ).then_inc(S["ld_state"], 16)
                pool.dma_start(pool_rows[0:NS_ * (PW - 1), l, :],
                               A["state_pool"][l].rearrange("b r n -> (b r) n")).then_inc(S["ld_state"], 16)
                pool.dma_start(lru_rows[0:NS_ * (LW - 1), l, :],
                               A["state_lru_conv"][l].rearrange("b r n -> (b r) n")).then_inc(S["ld_state"], 16)
                pool.dma_start(lru_rows[24:24 + NS_, l, :], A["state_lru_h"][l]).then_inc(S["ld_state"], 16)
            nc.gpsimd.memset(w_a[:], 0.0).then_inc(S["gates_zeroed"], 1)
            nc.gpsimd.memset(w_x[:], 0.0).then_inc(S["gates_zeroed"], 1)
            pool.wait_ge(S["gates_zeroed"], 2)

            def small(l):
                pool.dma_start(w_pool[:, :, :], A["w_pool"][l].rearrange("g c d -> c g d")).then_inc(S["ld_small"], 16)
                for w, t in ((A["lru_wa"], w_a), (A["lru_wx"], w_x)):
                    for h in range(2):
                        pool.dma_start(t[64 * h:64 * h + 64, :, 64 * h:64 * h + 64],
                                       w[l].rearrange("(j h) c d -> h c j d", h=2)[h]).then_inc(S["ld_small"], 16)

            small(0)
            pool.dma_start(w_rt[:, :, :], A["moe_router"][0].rearrange("(k p) n -> p k n", p=P)
                           ).then_inc(S["ld_small"], 16)
            for l in range(L):
                pool.dma_start(O["conv_s"][l, :, 0:CW - 2, :], A["state_conv"][l, :, 1:CW - 1, :]
                               ).then_inc(S["out_dma"], 16)
                pool.dma_start(O["pool_s"][l, :, 0:PW - 2, :], A["state_pool"][l, :, 1:PW - 1, :]
                               ).then_inc(S["out_dma"], 16)
                pool.dma_start(O["lconv_s"][l, :, 0:LW - 2, :], A["state_lru_conv"][l, :, 1:LW - 1, :]
                               ).then_inc(S["out_dma"], 16)
            for l in range(L):
                for j in range(C4):
                    read_out(pool, ("mix", l, 1, j))
                nc.gpsimd.tensor_copy(so[:, :, 0:30], glu[:, :, TP:TP + 30]).then_inc(S["packed"], 1)
                nc.gpsimd.tensor_copy(so[:, :, 49:57], win_s[:, l, :, :, CW - 1]).then_inc(S["packed"], 1)
                for j in range(C4):
                    read_out(pool, ("mix", l, 2, j))
                nc.gpsimd.tensor_copy(so[:, :, 45:48], ulru[:, :, TP:TP + 3]).then_inc(S["packed"], 1)
                nc.gpsimd.tensor_copy(so[:, :, 65:73], lru_s[:, l, :, :, LW - 1]).then_inc(S["packed"], 1)
                for j in range(C4):
                    read_out(pool, ("mix", l, 3, j))
                nc.gpsimd.tensor_copy(so[:, :, 30:45], upool[:, :, TP:TP + 15]).then_inc(S["packed"], 1)
                nc.gpsimd.tensor_copy(so[:, :, 57:65], pool_s[:, l, :, :, PW - 1]).then_inc(S["packed"], 1)
                pool.wait_ge(S["h_ready"], l + 1)
                nc.gpsimd.tensor_copy(so[:, :, 48:49], hseq[:, :, TP - 1:TP]).then_inc(S["packed"], 1)
                nc.gpsimd.tensor_copy(so[:, :, 73:81], hseq[:, :, TP:T]).then_inc(S["packed"], 1)
                if l + 1 < L:
                    filled(pool, ("pm", l, C4 - 1))
                    small(l + 1)
                read_out(pool, ("so", l))
                for dst, r0, r1 in ((O["conv_p"][l, 0], 0, 30), (O["pool_p"][l, 0], 30, 45), (O["lconv_p"][l, 0], 45, 48),
                                    (O["h_p"][l], 48, 49), (O["conv_s"][l, :, CW - 2, :], 49, 57),
                                    (O["pool_s"][l, :, PW - 2, :], 57, 65), (O["lconv_s"][l, :, LW - 2, :], 65, 73),
                                    (O["h_s"][l], 73, 81)):
                    pool.dma_start(dst, so_out[r0:r1, :]).then_inc(S["out_dma"], 16)

        @block.tensor
        def _(pe):
            mm = nc.tensor.matmul

            def mm3(out, ah, al, bh, bl, start, stop):
                mm(out, ah, bh, start=start, stop=False, skip_group_check=True)
                mm(out, ah, bl, start=False, stop=False, skip_group_check=True)
                return mm(out, al, bh, start=False, stop=stop, skip_group_check=True)

            pe.wait_ge(S["ld_const"], 16)
            pe.wait_ge(S["ld_x"], 32)
            for k in range(KT):
                o = bank(("xT", k))
                for a in range(2):
                    nc.tensor.transpose(o[:, a * P:(a + 1) * P], x_rows[:, a, k * P:(k + 1) * P], ident)
                nc.tensor.transpose(o[:, TP:T], xs_rows[0:NS_, k * P:(k + 1) * P],
                                    ident[0:NS_, 0:NS_]).then_inc(full_of(("xT", k)), 1)
            pe.wait_ge(S["ld_par"], 16 * 15)
            empty(pe, "par512")
            for j in range(C4):
                t = nc.tensor.transpose(bank("par512")[:, j * L * NR:(j + 1) * L * NR],
                                        par_rows[0:L * NR, j * P:(j + 1) * P], ident[0:L * NR, 0:L * NR])
            t.then_inc(full_of("par512"), 1)
            empty(pe, "par1024")
            for j in range(KT):
                t = nc.tensor.transpose(bank("par1024")[:, j * L * NQ:(j + 1) * L * NQ],
                                        pard_rows[0:L * NQ, j * P:(j + 1) * P], ident[0:L * NQ, 0:L * NQ])
            t.then_inc(full_of("par1024"), 1)
            pe.wait_ge(S["ld_state"], 16 * 5 * L)
            for l in range(L):
                R = 4 * (CW - 1)
                for h in range(2):
                    n = ("st_conv", l, h)
                    empty(pe, n)
                    for j in range(C4):
                        t = nc.tensor.transpose(bank(n)[:, j * R:(j + 1) * R],
                                                conv_rows[0:R, l, h, j * P:(j + 1) * P], ident[0:R, 0:R])
                    t.then_inc(full_of(n), 1)
                R = NS_ * (PW - 1)
                n = ("st_pool", l)
                empty(pe, n)
                for j in range(C4):
                    t = nc.tensor.transpose(bank(n)[:, j * R:(j + 1) * R],
                                            pool_rows[0:R, l, j * P:(j + 1) * P], ident[0:R, 0:R])
                t.then_inc(full_of(n), 1)
                n = ("st_lru", l)
                empty(pe, n)
                for j in range(C4):
                    t = nc.tensor.transpose(bank(n)[:, j * 32:j * 32 + 32],
                                            lru_rows[0:32, l, j * P:(j + 1) * P], ident[0:32, 0:32])
                t.then_inc(full_of(n), 1)

            def stats(norm, mean, msq, j, tile):
                read_out(pe, tile)
                if j == 0:
                    empty(pe, mean)
                t = mm(bank(mean)[:, 0:T], ones_d[:, :], z[:, j, :], start=(j == 0), stop=(j == KT - 1),
                       skip_group_check=True)
                if j == KT - 1:
                    t.then_inc(full_of(mean), 1)
                pe.wait_ge(S["zsq_ready"], norm * KT + j + 1)
                if j == 0:
                    empty(pe, msq)
                t = mm(bank(msq)[:, 0:T], ones_d[:, :], zsq[:, j, :], start=(j == 0), stop=(j == KT - 1),
                       skip_group_check=True)
                if j == KT - 1:
                    t.then_inc(full_of(msq), 1)

            for l in range(L):
                b0 = mixer_piece(l)
                for s, what in enumerate(IN_ORDER):
                    n = b0 + s
                    slot = n % SLOTS
                    kind = what[0]
                    if s == 0 and l == 0:
                        for k in range(KT):
                            read_out(pe, ("xT", k))
                    elif s == 0:
                        pe.wait_ge(S["x_split"], 2 * l * KT)
                    if kind == "branch":
                        if what[1] == 1:
                            pe.wait_ge(S["csq_done"], l + 1)
                            empty(pe, ("cmean", l))
                            for j in range(C4):
                                t = mm(bank(("cmean", l))[:, 0:T], ones_b[:, :], conv[:, j, :],
                                       start=(j == 0), stop=(j == C4 - 1))
                            t.then_inc(full_of(("cmean", l)), 1)
                            empty(pe, ("csq", l))
                            for j in range(C4):
                                t = mm(bank(("csq", l))[:, 0:T], ones_b[:, :], conv_sq[:, j, :],
                                       start=(j == 0), stop=(j == C4 - 1))
                            t.then_inc(full_of(("csq", l)), 1)
                        pe.wait_ge(S["br_ready"], (3 * l + {0: 1, 2: 2, 1: 3}[what[1]]) * C4)
                    if kind == "out" and what[1] == 0:
                        pe.wait_ge(S["mg_split"], (l + 1) * KT)
                    pe.wait_ge(S["lo_done"], n + 1)
                    nk, nj, width = (C4, KT, D) if kind == "branch" else (KT, 4, 512)
                    rh, rl = (brh, brl) if kind == "branch" else (xh, xl)
                    for j in range(nj):
                        name = ("mix", l, s, j)
                        empty(pe, name)
                        for k in range(nk):
                            t = mm3(bank(name)[:, 0:T], wh(slot, k, j * P, (j + 1) * P, width),
                                    wl(slot, k, j * P, (j + 1) * P, width), rh[:, k, :], rl[:, k, :],
                                    k == 0, k == nk - 1)
                        t.then_inc(full_of(name), 1)
                        if kind == "out" and what[1] * 4 + j >= 1:
                            d = what[1] * 4 + j - 1
                            stats(2 * l, ("mean1", l), ("msq1", l), d, ("mix", l, 14 + d // 4, d % 4))
                    if s == 5:
                        pe.wait_ge(S["ld_small"], 16 * (6 + 5 * l))
                        for nm, w in (("ra", w_a), ("ri", w_x)):
                            for j in range(C4):
                                pe.wait_ge(S["xc_ready"], l * C4 + j + 1)
                                empty(pe, (nm, l, j))
                                mm(bank((nm, l, j))[:, 0:T], w[:, j, :], xc[:, j, :], start=True,
                                   stop=True).then_inc(full_of((nm, l, j)), 1)
                    if s == 6:
                        for j in range(C4):
                            pe.wait_ge(S["pooled_ready"], l * C4 + j + 1)
                            empty(pe, ("pm", l, j))
                            mm(bank(("pm", l, j))[:, 0:T], w_pool[:, j, :], pooled[:, j, :], start=True,
                               stop=True).then_inc(full_of(("pm", l, j)), 1)
                    if s == 13:
                        pe.wait_ge(S["packed"], 8 * (l + 1))
                        empty(pe, ("so", l))
                        for j in range(C4):
                            t = nc.tensor.transpose(bank(("so", l))[0:81, j * P:(j + 1) * P], so[:, j, 0:81],
                                                    ident)
                        t.then_inc(full_of(("so", l)), 1)
                stats(2 * l, ("mean1", l), ("msq1", l), KT - 1, ("mix", l, 15, 3))
                if l == 0:
                    n = MIX
                    pe.wait_ge(S["x_split"], KT)
                    for g, nf in enumerate(FG):
                        for nm in ("fg", "fu"):
                            pe.wait_ge(S["lo_done"], n + 1)
                            for j in range(nf):
                                name = (nm, g, j)
                                empty(pe, name)
                                for k in range(KT):
                                    t = mm3(bank(name)[:, 0:T], wh(n % SLOTS, k, j * P, (j + 1) * P, nf * P),
                                            wl(n % SLOTS, k, j * P, (j + 1) * P, nf * P), xh[:, k, :], xl[:, k, :],
                                            k == 0, k == KT - 1)
                                t.then_inc(full_of(name), 1)
                            n += 1
                    for half in range(2):
                        f0 = 0
                        for g, nf in enumerate(DG):
                            pe.wait_ge(S["lo_done"], n + 1)
                            pe.wait_ge(S["f_split"], f0 + nf)
                            for j in range(4):
                                name = ("fd", half * 4 + j)
                                if g == 0:
                                    empty(pe, name)
                                for k in range(nf):
                                    t = mm3(bank(name)[:, 0:T], wh(n % SLOTS, k, j * P, (j + 1) * P, 512),
                                            wl(n % SLOTS, k, j * P, (j + 1) * P, 512), hdh[:, f0 + k, :],
                                            hdl[:, f0 + k, :], f0 + k == 0, f0 + k == NF - 1)
                                if g == len(DG) - 1:
                                    t.then_inc(full_of(name), 1)
                            if g < len(DG) - 1:
                                t.then_inc(S["down_used"], 1)
                            f0 += nf
                            n += 1
                            if half == 1 and g == 0:
                                for j in range(4):
                                    stats(1, ("mean2", 0), ("msq2", 0), j, ("fd", j))
                    for j in range(4, KT):
                        stats(1, ("mean2", 0), ("msq2", 0), j, ("fd", j))

            pe.wait_ge(S["norm_ready"], 3 * KT)
            pe.wait_ge(S["ld_small"], 16 * 11)
            empty(pe, "logits")
            for i in range(3):
                n = P if i < 2 else NS_
                for k in range(KT):
                    t = mm(bank("logits")[0:n, i * NE:(i + 1) * NE], x[:, k, i * P:i * P + n], w_rt[:, k, :],
                           start=(k == 0), stop=(k == KT - 1))
            t.then_inc(full_of("logits"), 1)
            for i in range(3):
                n = P if i < 2 else NS_
                for h in range(2):
                    name = ("xtok", i, h)
                    empty(pe, name)
                    for k in range(4):
                        kk = 4 * h + k
                        t = nc.tensor.transpose(bank(name)[0:n, k * P:(k + 1) * P], x[:, kk, i * P:i * P + n],
                                                ident)
                    t.then_inc(full_of(name), 1)
            pe.wait_ge(S["mask_ready"], 1)
            empty(pe, "ranks")
            rk = bank("ranks")
            mask = route[:, 0, :, :]
            for i in range(3):
                n = P if i < 2 else NS_
                for q in range(i):
                    mm(rk[0:n, i * NE:(i + 1) * NE], ones[:, 0:n], mask[:, q, :], start=(q == 0), stop=False)
                mm(rk[0:n, i * NE:(i + 1) * NE], tri[0:n, 0:n], mask[0:n, i, :], start=(i == 0), stop=True)
            for i in range(3):
                n = P if i < 2 else NS_
                t = mm(rk[:, 3 * NE:4 * NE], ones[0:n, :], mask[0:n, i, :], start=(i == 0), stop=(i == 2))
            t.then_inc(full_of("ranks"), 1)

            def gather(v, in_loop):
                pe.wait_ge(S["onehot_ready"], v + 1)
                for part, rows, banks in (("gath_hi", xth, (6, 7)), ("gath_lo", xtl, (1, 3))):
                    for h, b in enumerate(banks):
                        if in_loop is None:
                            empty(pe, (part, h))
                        else:
                            pe.wait_ge(*in_visit(bank_free, b, in_loop, PER_VISIT[b] - 2))
                        for k in range(4):
                            for i in range(3):
                                t = mm(ps[:, b, k * CAP:(k + 1) * CAP],
                                       rows[:, i, (4 * h + k) * P:(4 * h + k + 1) * P],
                                       onehot[:, i, :], start=(i == 0), stop=(i == 2))
                        t.then_inc(bank_full[b], 1)

            def scatter(v):
                for b in (4, 5):
                    pe.wait_ge(*in_visit(bank_free, b, v, -1))
                for d in range(KT):
                    b = 6 + d % 2
                    pe.wait_ge(*in_visit(bank_free, b, v, d // 2 - 1))
                    mm(ps[:, b, 0:T], yh[:, d * P:(d + 1) * P], onehot_t, start=True, stop=False)
                    mm(ps[:, b, 0:T], yl[:, d * P:(d + 1) * P], onehot_t, start=False,
                       stop=True).then_inc(bank_full[b], 1)

            for i in range(3):
                for h in range(2):
                    read_out(pe, ("xtok", i, h))
            gather(0, None)
            pe.wait_ge(S["visits_ready"], 1)
            nv = pe.value_load(visits_i[0:1, 0:1], min_val=NE, max_val=3 * NE)

            with pe.Fori(0, nv) as v:
                def slot_of(m):
                    return (PRE + m) % SLOTS

                def gate_up(c):
                    if c == 0:
                        for b in (6, 7, 1, 3):
                            pe.wait_ge(*in_visit(bank_free, b, v, -1))
                    for kind in "gu":
                        m = order.index((kind, c))
                        pe.wait_ge(S["lo_done"], v * VISIT + (PRE + m + 1))
                        b = c % 2 + (0 if kind == "g" else 2)
                        pe.wait_ge(*in_visit(bank_free, b, v, c // 2 - 1))
                        for j in range(4):
                            for k in range(KT):
                                t = mm3(ps[:, b, j * CAP:(j + 1) * CAP], wh(slot_of(m), k, j * P, (j + 1) * P, 512),
                                        wl(slot_of(m), k, j * P, (j + 1) * P, 512), xgh[:, k, :], xgl[:, k, :],
                                        k == 0, k == KT - 1)
                        t.then_inc(bank_full[b], 1)

                def down(c):
                    m = order.index(("d", c))
                    pe.wait_ge(S["lo_done"], v * VISIT + (PRE + m + 1))
                    pe.wait_ge(S["e_split"], v * NC + (c + 2))
                    for half in range(2):
                        b = 4 + half
                        if c == 0:
                            pe.wait_ge(*in_visit(bank_free, b, v, -1))
                        for k in range(4):
                            t = mm3(ps[:, b, :], hh[:, c % 2, k * P:(k + 1) * P], hl[:, c % 2, k * P:(k + 1) * P],
                                    wh(slot_of(m), k, half * 512, half * 512 + 512, D),
                                    wl(slot_of(m), k, half * 512, half * 512 + 512, D),
                                    c == 0 and k == 0, c == NC - 1 and k == 3)
                        if c == NC - 1:
                            t.then_inc(bank_full[b], 1)
                    if c < NC - 1:
                        t.then_inc(S["down_used"], 1)

                gate_up(0)
                scatter(v)
                gate_up(1)
                pe.wait_ge(*in_visit(bank_free, 7, v, 3))
                st = ps[:, 7, :].bitcast(F16)
                for i in range(3):
                    n = P if i < 2 else NS_
                    nc.tensor.transpose(st[:, i * P:i * P + n], onehot[0:n, i, :], ident16[0:n, 0:n])
                for i in range(3):
                    t = mm(ps[:, 7, 256:258], onehot[:, i, :], gsel[:, i, :], start=(i == 0), stop=(i == 2))
                t.then_inc(bank_full[7], 1)
                down(0)
                for c in range(2, NC):
                    gate_up(c)
                    if c < NC - 1:
                        down(c - 1)
                down(NC - 2)
                gather(v + 1, v)
                down(NC - 1)

            scatter(nv)
            for j in range(KT):
                pe.wait_ge(*in_visit(bank_free, 6 + j % 2, nv, j // 2))
                if j == 0:
                    pe.wait_ge(*in_visit(bank_free, 0, nv, -1))
                t = mm(ps[:, 0, 0:T], ones_d[:, :], z[:, j, :], start=(j == 0), stop=(j == KT - 1),
                       skip_group_check=True)
                if j == KT - 1:
                    t.then_inc(bank_full[0], 1)
                pe.wait_ge(S["zsq_ready"], 3 * KT + j + 1)
                if j == 0:
                    pe.wait_ge(*in_visit(bank_free, 1, nv, -1))
                t = mm(ps[:, 1, 0:T], ones_d[:, :], zsq[:, j, :], start=(j == 0), stop=(j == KT - 1),
                       skip_group_check=True)
                if j == KT - 1:
                    t.then_inc(bank_full[1], 1)
            pe.wait_ge(S["norm_ready"], 4 * KT)
            for i in range(3):
                n = P if i < 2 else NS_
                for h in range(2):
                    b = 2 + h
                    pe.wait_ge(*in_visit(bank_free, b, nv, i - 1))
                    for k in range(4):
                        t = nc.tensor.transpose(ps[0:n, b, k * P:(k + 1) * P], x[:, 4 * h + k, i * P:i * P + n],
                                                ident)
                    t.then_inc(bank_full[b], 1)
        @block.scalar
        def _(act):
            fn = nc.scalar.activation

            def hi(n):
                if n >= PRE:
                    return
                tiles, width = pre_piece(n)[1:]
                act.wait_ge(stage_full[n % SLOTS], 16 * (n // SLOTS + 1))
                if n >= SLOTS:
                    piece_done(act, n - SLOTS)
                fn(w_hi[:, n % SLOTS, 0:tiles * width], stage[:, n % SLOTS, 0:tiles * width], ACT.Copy,
                   scale=WS).then_inc(S["hi_done"], 1)

            def norm(q, mean, l, g, b, split):
                mean_full(act, mean)
                fn(stat[:, 0, :], mean_ap(mean), ACT.Square).then_inc(S["m2_ready"], 1)
                act.wait_ge(S["var_ready"], q + 1)
                fn(stat[:, 2, :], stat[:, 1, :], ACT.Sqrt).then_inc(S["std_ready"], 1)
                for j in range(KT):
                    act.wait_ge(S["nz_ready"], q * KT + j + 1)
                    fn(x[:, j, :], z[:, j, :], ACT.Identity, bias=vec_d(b, l, j),
                       scale=vec_d(g, l, j)).then_inc(S["norm_ready"], 1)
                    if split:
                        fn(xh[:, j, :], z[:, j, :], ACT.Identity, bias=vec_d(b, l, j),
                           scale=vec_d(g, l, j)).then_inc(S["x_hi"], 1)

            def mean_full(eng, mean):
                if mean[0] == "tail":
                    eng.wait_ge(*in_visit(bank_full, 0, mean[2], 0))
                else:
                    filled(eng, mean)

            def mean_ap(mean):
                return ps[:, mean[1], 0:T] if mean[0] == "tail" else bank(mean)[:, 0:T]

            act.dma_start(consts[:, :], A["consts"]).then_inc(S["ld_const"], 16)
            for i, name in enumerate(VEC_B):
                act.dma_start(par_rows[i * L:(i + 1) * L, :], A[name]).then_inc(S["ld_par"], 16)
            r = len(VEC_B) * L
            act.dma_start(par_rows[r:r + L * CW, :], A["conv_w"].rearrange("l k n -> (l k) n")).then_inc(S["ld_par"], 16)
            r += L * CW
            act.dma_start(par_rows[r:r + L * LW, :], A["lru_conv_w"].rearrange("l k n -> (l k) n")
                          ).then_inc(S["ld_par"], 16)
            act.dma_start(pard_rows[0:3 * L, :], A["b_gate"].rearrange("l (b n) -> (l b) n", b=3)
                          ).then_inc(S["ld_par"], 16)
            for i, name in enumerate(VEC_D):
                act.dma_start(pard_rows[(3 + i) * L:(4 + i) * L, :], A[name]).then_inc(S["ld_par"], 16)
            for k in range(KT):
                filled(act, ("xT", k))
                fn(x[:, k, :], bank(("xT", k))[:, 0:T], ACT.Copy)
                fn(xh[:, k, :], bank(("xT", k))[:, 0:T], ACT.Copy).then_inc(S["x_hi"], 1)
            filled(act, "par512")
            fn(par[:, :, :], bank("par512")[:, 0:C4 * L * NR].rearrange("p (j r) -> p j r", j=C4),
               ACT.Copy).then_inc(free_of("par512"), 1)
            filled(act, "par1024")
            fn(par_d[:, :, :], bank("par1024")[:, 0:KT * L * NQ].rearrange("p (j r) -> p j r", j=KT),
               ACT.Copy).then_inc(free_of("par1024"), 1)
            hi(0)
            hi(1)
            read_out(act, "par512")
            read_out(act, "par1024")
            act.wait_ge(S["sp_abs"], 1)
            fn(spt[:, 1], spt[:, 0], ACT.Exp, scale=-1.0).then_inc(S["sp_exp"], 1)

            for l in range(L):
                b0 = mixer_piece(l)
                for s, what in enumerate(IN_ORDER):
                    hi(b0 + s + AHEAD)
                    kind = what[0]
                    for j in range(4):
                        name = ("mix", l, s, j)
                        o = bank(name)
                        if kind == "glu":
                            filled(act, name)
                            fn(sg[:, j, :], o[:, 0:T], ACT.Sigmoid, scale=1 / WS).then_inc(free_of(name), 1)
                        elif kind == "lru":
                            filled(act, name)
                            if j == 0 and l:
                                act.wait_ge(S["zeroed"], l + 1)
                            fn(ulru[:, j, LW - 1:], o[:, 0:TP], ACT.Copy, scale=1 / WS)
                            fn(lru_s[:, l, j, :, LW - 1], o[:, TP:T], ACT.Copy, scale=1 / WS).then_inc(free_of(name), 1)
                        elif kind == "pool":
                            filled(act, name)
                            fn(upool[:, j, PW - 1:], o[:, 0:TP], ACT.Copy, scale=1 / WS)
                            fn(pool_s[:, l, j, :, PW - 1], o[:, TP:T], ACT.Copy, scale=1 / WS).then_inc(free_of(name), 1)
                        elif kind == "gelu":
                            filled(act, name)
                            fn(gelu[:, j, :], o[:, 0:T], ACT.Gelu_apprx_tanh, scale=1 / WS).then_inc(free_of(name), 1)
                        elif kind == "gate":
                            filled(act, name)
                            turn = {0: 0, 2: 1, 1: 2}[what[2]]
                            d = what[3] * 4 + j
                            if turn == 1:
                                read_out(act, ("mix", l, 7, d))
                            elif turn == 2:
                                act.wait_ge(S["merge_done"], l * KT + d + 1)
                            elif d == 0:
                                act.wait_ge(S["pooled_ready"], (l + 1) * C4)
                            fn(gates[:, d, :], o[:, 0:T], ACT.Sigmoid, bias=gate_bias(l, what[2], d),
                               scale=1 / WS).then_inc(free_of(name), 1)
                    if s == 5:
                        for nm, w, out in (("ra", "lru_ba", rt), ("ri", "lru_bx", ig)):
                            for j in range(C4):
                                n = (nm, l, j)
                                filled(act, n)
                                fn(out[:, j, :], bank(n)[:, 0:T], ACT.Sigmoid, bias=vec(w, l, j)).then_inc(free_of(n), 1)
                        filled(act, ("ri", l, C4 - 1))
                        act.wait_ge(S["sp_done"], 1)
                        for j in range(C4):
                            read_out(act, ("ra", l, j))
                            fn(rt[:, j, :], rt[:, j, :], ACT.Tanh, scale=sp4[:, j, l:l + 1]).then_inc(S["tanh_ready"], 1)
                    if s == 6:
                        for j in range(C4):
                            n = ("pm", l, j)
                            filled(act, n)
                            fn(y_pool[:, j, :], bank(n)[:, 0:T], ACT.Copy, scale=vec("pool_scale", l, j))
                            fn(brh[:, j, :], bank(n)[:, 0:T], ACT.Copy, scale=vec("pool_scale", l, j)
                               ).then_inc(free_of(n), 1)
                        act.wait_ge(S["q_ready"], l + 1)
                        fn(rt, rt, ACT.Sqrt).then_inc(S["root_ready"], 1)
                    if s == 8:
                        act.wait_ge(S["hg_ready"], l + 1)
                        piece_done(act, b0 + 7)
                        for j in range(C4):
                            fn(brh[:, j, :], rq[:, j, :], ACT.Copy).then_inc(S["br_hi"], 1)
                    if s == 9:
                        act.wait_ge(S["conv_done"], (l + 1) * C4)
                        fn(conv_sq, conv, ACT.Square).then_inc(S["csq_done"], 1)
                    if s == 12:
                        filled(act, ("cmean", l))
                        fn(stat[:, 0, :], bank(("cmean", l))[:, 0:T], ACT.Square).then_inc(S["cm2_ready"], 1)
                        act.wait_ge(S["cvar_ready"], l + 1)
                        fn(stat[:, 2, :], stat[:, 1, :], ACT.Sqrt).then_inc(S["cstd_ready"], 1)
                        for j in range(C4):
                            act.wait_ge(S["cv_ready"], l * C4 + j + 1)
                            fn(conv_sq[:, j, :], conv[:, j, :], ACT.Silu, bias=vec("conv_ln_b", l, j),
                               scale=vec("conv_ln_g", l, j)).then_inc(S["silu_ready"], 1)
                        for j in range(C4):
                            act.wait_ge(S["silu_ready"], l * C4 + j + 1)
                            fn(brh[:, j, :], conv_sq[:, j, :], ACT.Copy).then_inc(S["br_hi"], 1)
                    if s == 13:
                        for d in range(KT):
                            act.wait_ge(S["mg_ready"], l * KT + d + 1)
                            fn(xh[:, d, :], merged[:, d, :], ACT.Copy).then_inc(S["mg_hi"], 1)
                        n = ("so", l)
                        filled(act, n)
                        if l:
                            act.wait_ge(S["out_dma"], 16 * (3 * L + 8 * l))
                        fn(so_out[0:81, :], bank(n)[0:81, :], ACT.Copy).then_inc(free_of(n), 1)
                    if kind == "out":
                        for j in range(4):
                            d = what[1] * 4 + j
                            read_out(act, ("mix", l, s, j))
                            fn(zsq[:, d, :], z[:, d, :], ACT.Square).then_inc(S["zsq_ready"], 1)
                norm(2 * l, ("mean1", l), l, "ln1_g", "ln1_b", l == 0)
                if l == 0:
                    n = MIX
                    f = 0
                    for g, nf in enumerate(FG):
                        hi(n + AHEAD)
                        hi(n + 1 + AHEAD)
                        for j in range(nf):
                            filled(act, ("fg", g, j))
                            if g:
                                read_out(act, ("fu", g - 1, j))
                            fn(silu_d[:, j, :], bank(("fg", g, j))[:, 0:T], ACT.Silu,
                               scale=1 / WS).then_inc(free_of(("fg", g, j)), 1)
                        for j in range(nf):
                            read_out(act, ("fu", g, j))
                            fn(hdh[:, f + j, :], h_d[:, j, :], ACT.Copy).then_inc(S["f_hi"], 1)
                        n += 2
                        f += nf
                    for half in range(2):
                        for g in range(len(DG)):
                            hi(n + AHEAD)
                            n += 1
                        for j in range(4 * half, 4 * half + 4):
                            read_out(act, ("fd", j))
                            fn(zsq[:, j, :], z[:, j, :], ACT.Square).then_inc(S["zsq_ready"], 1)
                    norm(1, ("mean2", 0), 0, "ln2_g", "ln2_b", True)

            for i in range(3):
                n = P if i < 2 else NS_
                for h in range(2):
                    name = ("xtok", i, h)
                    filled(act, name)
                    if i == 2:
                        act.wait_ge(S["rows_zeroed"], 1)
                    fn(xth[0:n, i, h * 512:(h + 1) * 512], bank(name)[0:n, :], ACT.Copy).then_inc(S["xt_hi"], 1)
            act.wait_ge(S["gd_ready"], 1)
            fn(route1[:, 4, :], route1[:, 3, :], ACT.Sigmoid)
            fn(route1[:, 5, :], route1[:, 3, :], ACT.Sigmoid, scale=-1.0).then_inc(S["gs_ready"], 1)

            def gather_hi(v, wait):
                for h in range(2):
                    wait(act, "gath_hi", h, 6 + h)
                    fn(xgh[:, 4 * h:4 * h + 4, :], ps[:, 6 + h, :].rearrange("p (k c) -> p k c", k=4),
                       ACT.Copy).then_inc(bank_free[6 + h], 1)

            def y_hi(v):
                act.wait_ge(*in_visit(bank_free, 7, v, -2))
                for h in range(2):
                    act.wait_ge(*in_visit(bank_full, 4 + h, v, -1))
                    fn(yh[:, h * 512:(h + 1) * 512], ps[:, 4 + h, :], ACT.Copy,
                       scale=gate_slot[:, 0:1]).then_inc(S["y_hi"], 1)

            gather_hi(0, lambda e, part, h, b: filled(e, (part, h)))
            act.wait_ge(S["visits_ready"], 1)
            nv = act.value_load(visits_i[0:1, 0:1], min_val=NE, max_val=3 * NE)
            def visit_done(m):
                kind, c = order[m % VISIT]
                back = 0 if m >= 0 else 1
                if kind == "d" and c < NC - 1:
                    return S["down_used"], v * (NC - 1) + (DOWN0 - back * (NC - 1) + c + 1)
                b, i = {"g": (c % 2, c // 2), "u": (2 + c % 2, c // 2), "d": (5, 0)}[kind]
                return in_visit(bank_full, b, v, i - back * PER_VISIT[b])

            with act.Fori(0, nv) as v:
                def hi_v(m):
                    if m >= VISIT:
                        return
                    n = PRE + m
                    act.wait_ge(stage_full[n % SLOTS], v * (16 * VISIT // SLOTS) + 16 * (n // SLOTS + 1))
                    act.wait_ge(*visit_done(m - SLOTS))
                    fn(w_hi[:, n % SLOTS, :], stage[:, n % SLOTS, :], ACT.Copy, scale=WS).then_inc(S["hi_done"], 1)

                hi_v(0)
                hi_v(1)
                y_hi(v)
                for m, (kind, c) in enumerate(order):
                    hi_v(m + AHEAD)
                    if kind == "u":
                        b = c % 2
                        act.wait_ge(*in_visit(bank_full, b, v, c // 2))
                        fn(silu_e[:, c % 2, :], ps[:, b, :], ACT.Silu, scale=1 / WS).then_inc(bank_free[b], 1)
                        act.wait_ge(*in_visit(bank_free, 2 + b, v, c // 2))
                        fn(hh[:, c % 2, :], h_e[:, c % 2, :], ACT.Copy).then_inc(S["e_hi"], 1)
                gather_hi(v + 1, lambda e, part, h, b: e.wait_ge(
                    *in_visit(bank_full, b, v, PER_VISIT[b] - 1)))
            y_hi(nv)
            for j in range(KT):
                act.wait_ge(*in_visit(bank_free, 6 + j % 2, nv, j // 2))
                fn(zsq[:, j, :], z[:, j, :], ACT.Square).then_inc(S["zsq_ready"], 1)
            norm(3, ("tail", 0, nv), 1, "ln2_g", "ln2_b", False)
            for i in range(3):
                n = P if i < 2 else NS_
                for h in range(2):
                    b = 2 + h
                    act.wait_ge(*in_visit(bank_full, b, nv, i))
                    fn(y_rows[0:n, i, h * 512:(h + 1) * 512], ps[0:n, b, :], ACT.Copy).then_inc(bank_free[b], 1)
                for b in (2, 3):
                    act.wait_ge(*in_visit(bank_free, b, nv, i))
                dst = (O["y_prompt"][0, i * P:(i + 1) * P, :] if i < 2 else O["y_sample"].rearrange("b s n -> (b s) n"))
                act.dma_start(dst, y_rows[0:n, i, :]).then_inc(S["y_out"], 16)
        @block.vector
        def _(dve):
            V = nc.vector
            own = Steps(dve, S["dve"])

            def lo(n):
                if n >= PRE:
                    return
                tiles, width = pre_piece(n)[1:]
                sl = n % SLOTS
                dve.wait_ge(S["hi_done"], n + 1)
                V.scalar_tensor_tensor(w_lo[:, sl, 0:tiles * width], stage[:, sl, 0:tiles * width], WS,
                                       w_hi[:, sl, 0:tiles * width], ALU.mult, ALU.subtract).then_inc(S["lo_done"], 1)

            def norm(q, mean, msq, scale, split):
                if mean[0] == "tail":
                    waits = [in_visit(bank_full, b, mean[2], 0) for b in (0, 1)]
                    read = [in_visit(bank_free, b, mean[2], 0) for b in (0, 1)]
                    mu, sq = ps[:, 0, 0:T], ps[:, 1, 0:T]
                else:
                    waits = [(full_of(n), place[n][1] + 1) for n in (mean, msq)]
                    read = [(free_of(n), place[n][1] + 1) for n in (mean, msq)]
                    mu, sq = bank(mean)[:, 0:T], bank(msq)[:, 0:T]
                for w in waits:
                    dve.wait_ge(*w)
                dve.wait_ge(S["m2_ready"], q + 1)
                V.tensor_tensor(stat[:, 1, :], sq, stat[:, 0, :], ALU.subtract).then_inc(read[1][0], 1)
                dve.wait_ge(*read[1])
                V.tensor_scalar(stat[:, 1, :], stat[:, 1, :], 0.0, EPS * scale * scale, ALU.max,
                                ALU.add).then_inc(S["var_ready"], 1)
                for j in range(KT):
                    t = V.tensor_tensor(z[:, j, :], z[:, j, :], mu, ALU.subtract)
                t.then_inc(read[0][0], 1)
                dve.wait_ge(S["std_ready"], q + 1)
                own.then(V.reciprocal(stat[:, 0, :], stat[:, 2, :]))
                dve.wait_ge(*read[0])
                for j in range(KT):
                    V.tensor_tensor(z[:, j, :], z[:, j, :], stat[:, 0, :], ALU.mult).then_inc(S["nz_ready"], 1)
                if split:
                    for j in range(KT):
                        dve.wait_ge(S["x_hi"], (q + 1) * KT + j + 1)
                        V.tensor_tensor(xl[:, j, :], x[:, j, :], xh[:, j, :], ALU.subtract).then_inc(S["x_split"], 1)

            V.memset(ones[:], 1.0)
            V.memset(ones_d[:], 1.0 / D)
            own.did(V.memset(ones_b[:], 1.0 / DB))
            for k in range(KT):
                n = ("xT", k)
                dve.wait_ge(S["x_hi"], k + 1)
                V.tensor_tensor(xl[:, k, :], bank(n)[:, 0:T], xh[:, k, :], ALU.subtract).then_inc(free_of(n), 1)
            lo(0)
            for l in range(L):
                for h in range(2):
                    n = ("st_conv", l, h)
                    filled(dve, n)
                    for j in range(C4):
                        r = 4 * (CW - 1)
                        t = V.tensor_copy(win_s[:, l, j, 4 * h:4 * h + 4, 0:CW - 1],
                                          bank(n)[:, j * r:(j + 1) * r].rearrange("p (b r) -> p b r", b=4))
                    t.then_inc(free_of(n), 1)
                n = ("st_pool", l)
                filled(dve, n)
                for j in range(C4):
                    r = NS_ * (PW - 1)
                    t = V.tensor_copy(pool_s[:, l, j, :, 0:PW - 1],
                                      bank(n)[:, j * r:(j + 1) * r].rearrange("p (b r) -> p b r", b=NS_))
                t.then_inc(free_of(n), 1)
                n = ("st_lru", l)
                filled(dve, n)
                for j in range(C4):
                    V.tensor_copy(lru_s[:, l, j, :, 0:LW - 1],
                                  bank(n)[:, j * 32:j * 32 + 24].rearrange("p (b r) -> p b r", b=NS_))
                t = V.tensor_copy(h0_s[:, l, :, :],
                                  bank(n)[:, 0:P].rearrange("p (j r) -> p j r", j=C4)[:, :, 24:32])
                t.then_inc(free_of(n), 1)
            lo(1)
            dve.wait_ge(S["ld_const"], 16)
            own.did(V.tensor_copy(ident16[:, :], ident))
            r = VEC_B.index("lru_lambda") * L
            lam = par[:, :, r:r + L]
            read_out(dve, "par512")
            read_out(dve, "par1024")
            V.scalar_tensor_tensor(spt[:, 0], lam, -1.0, lam, ALU.mult, ALU.max).then_inc(S["sp_abs"], 1)
            dve.wait_ge(S["sp_exp"], 1)
            own.then(V.tensor_scalar(spt[:, 2], spt[:, 1], 2.0, None, ALU.add))
            own.then(V.reciprocal(spt[:, 3], spt[:, 2]))
            own.then(V.tensor_tensor(spt[:, 2], spt[:, 1], spt[:, 3], ALU.mult))
            own.then(V.tensor_tensor(spt[:, 3], spt[:, 2], spt[:, 2], ALU.mult))
            own.then(V.tensor_scalar(spt[:, 4], spt[:, 3], 1.0 / 15, 1.0 / 13, ALU.mult, ALU.add))
            for k in (11, 9, 7, 5, 3, 1):
                own.then(V.tensor_tensor(spt[:, 4], spt[:, 4], spt[:, 3], ALU.mult))
                own.then(V.tensor_scalar(spt[:, 4], spt[:, 4], 1.0 / k, None, ALU.add))
            own.then(V.tensor_tensor(spt[:, 4], spt[:, 4], spt[:, 2], ALU.mult))
            own.then(V.tensor_scalar(spt[:, 5], lam, -1.0, 0.0, ALU.mult, ALU.max))
            own.then(V.scalar_tensor_tensor(spt[:, 3], spt[:, 4], 2.0, spt[:, 5], ALU.mult, ALU.add))
            V.tensor_scalar(sp4[:, :, :], spt[:, 3], 4.0, None, ALU.mult).then_inc(S["sp_done"], 1)

            for l in range(L):
                b0 = mixer_piece(l)
                tap_at = [0] * C4

                def conv_taps(k0, k1):
                    for k in range(k0, k1):
                        for j in range(C4):
                            w = conv_tap(l, j, k)
                            src = glu[:, j, k:k + TP]
                            if k == 0:
                                i = V.tensor_scalar(conv[:, j, 0:TP], src, w, vec("conv_b", l, j), ALU.mult, ALU.add)
                            else:
                                own.after(tap_at[j])
                                i = V.scalar_tensor_tensor(conv[:, j, 0:TP], src, w, conv[:, j, 0:TP],
                                                           ALU.mult, ALU.add)
                            tap_at[j] = own.did(i)

                def window_conv(win, taps, width, out, bias, done):
                    for j in range(C4):
                        w = taps(l, j, 0, width).unsqueeze(1).to_broadcast([P, NS_, width])
                        own.then(V.tensor_tensor(prod[:, :, 0:width], win[:, l, j, :, :], w, ALU.mult))
                        own.then(V.tensor_reduce(out[:, j, TP:T], prod[:, :, 0:width], X, ALU.add))
                        V.tensor_scalar(out[:, j, TP:T], out[:, j, TP:T], vec(bias, l, j), None,
                                        ALU.add).then_inc(S[done], 1)

                def merge(s, done):
                    for d in range(KT):
                        name = ("mix", l, s, d)
                        read_out(dve, ("mix", l, s - 2 + d // 4, d % 4))
                        filled(dve, name)
                        out = gates if done else merged
                        V.scalar_tensor_tensor(out[:, d, :], bank(name)[:, 0:T], 1 / WS, gates[:, d, :], ALU.mult,
                                               ALU.mult).then_inc(free_of(name), 1)
                        if done and d:
                            merge_sum(s, d - 1, done)
                    if done:
                        merge_sum(s, KT - 1, done)

                def merge_sum(s, d, done):
                    read_out(dve, ("mix", l, s, d))
                    V.tensor_tensor(merged[:, d, :], merged[:, d, :], gates[:, d, :], ALU.add).then_inc(S[done], 1)

                if l:
                    dve.wait_ge(S["packed"], 8 * l)
                V.memset(glu[:, :, 0:CW - 1], 0.0)
                V.memset(upool[:, :, 0:PW - 1], 0.0)
                V.memset(ulru[:, :, 0:LW - 1], 0.0).then_inc(S["zeroed"], 1)

                for s, what in enumerate(IN_ORDER):
                    lo(b0 + s + AHEAD)
                    kind = what[0]
                    if kind == "val":
                        for j in range(4):
                            name = ("mix", l, s, j)
                            gl = ("mix", l, 0, j)
                            read_out(dve, gl)
                            filled(dve, name)
                            o = bank(name)
                            V.scalar_tensor_tensor(glu[:, j, CW - 1:], o[:, 0:TP], 1 / WS, sg[:, j, 0:TP], ALU.mult,
                                                   ALU.mult)
                            V.scalar_tensor_tensor(win_s[:, l, j, :, CW - 1], o[:, TP:T], 1 / WS, sg[:, j, TP:T],
                                                   ALU.mult, ALU.mult).then_inc(free_of(name), 1)
                        for j in range(4):
                            read_out(dve, ("mix", l, s, j))
                    if s == 2:
                        dve.wait_ge(S["zeroed"], l + 1)
                        for k in range(LW):
                            for j in range(C4):
                                src = ulru[:, j, k:k + TP]
                                if k == 0:
                                    read_out(dve, ("mix", l, s, j))
                                    i = V.tensor_scalar(xc[:, j, 0:TP], src, lru_tap(l, j, k), vec("lru_conv_b", l, j),
                                                        ALU.mult, ALU.add)
                                else:
                                    own.after(tap_at[j])
                                    i = V.scalar_tensor_tensor(xc[:, j, 0:TP], src, lru_tap(l, j, k),
                                                               xc[:, j, 0:TP], ALU.mult, ALU.add)
                                tap_at[j] = own.did(i)
                        window_conv(lru_s, lru_tap, LW, xc, "lru_conv_b", "xc_ready")
                        conv_taps(0, 3)
                    if s == 3:
                        conv_taps(3, 10)
                    if s == 4:
                        for j in range(C4):
                            read_out(dve, ("mix", l, 3, j))
                            src, w = upool[:, j, :], 1
                            E_ = PW - 1 + TP
                            while w < WINDOWS[j]:
                                dst = wsum[:, (w.bit_length() - 1) % 2, :]
                                lo_ = 2 * w - 1
                                own.then(V.tensor_tensor(dst[:, lo_:E_], src[:, lo_:E_], src[:, lo_ - w:E_ - w],
                                                         ALU.add))
                                src, w = dst, 2 * w
                            own.then(V.scalar_tensor_tensor(pooled[:, j, 0:TP], src[:, PW - 1:], 1.0 / w,
                                                            upool[:, j, PW - 1:], ALU.mult, ALU.subtract))
                            o2 = wsum[:, w.bit_length() % 2, 0:PW]
                            own.then(V.tensor_tensor(o2, src[:, PW - 1:2 * PW - 1], inv_cnt[:, j, :], ALU.mult))
                            own.then(V.tensor_tensor(pooled[:, j, 0:PW], o2, upool[:, j, PW - 1:2 * PW - 1],
                                                     ALU.subtract))
                            own.then(V.tensor_reduce(pooled[:, j, TP:T], pool_s[:, l, j, :, PW - w:PW], X, ALU.add))
                            V.scalar_tensor_tensor(pooled[:, j, TP:T], pooled[:, j, TP:T], 1.0 / w,
                                                   pool_s[:, l, j, :, PW - 1], ALU.mult,
                                                   ALU.subtract).then_inc(S["pooled_ready"], 1)
                        conv_taps(10, 13)
                    if s == 5:
                        conv_taps(13, 19)
                    if s == 6:
                        for j in range(C4):
                            read_out(dve, ("pm", l, j))
                            V.tensor_tensor(brl[:, j, :], y_pool[:, j, :], brh[:, j, :],
                                            ALU.subtract).then_inc(S["br_ready"], 1)
                        dve.wait_ge(S["tanh_ready"], (l + 1) * C4)
                        dve.wait_ge(S["packed"], 8 * l + 4)
                        own.then(V.tensor_scalar(rq, rt, 1.0, None, ALU.add))
                        n = own.did(V.reciprocal(rq, rq))
                        own.after(n)
                        V.tensor_scalar(a_lru, rq, 2.0, -1.0, ALU.mult, ALU.add).then_inc(S["q_ready"], 1)
                        dve.wait_ge(S["q_ready"], l + 1)
                        own.did(V.memset(a_lru[:, :, 0:1], 0.0))
                        own.then(V.tensor_tensor(ig, ig, xc, ALU.mult))
                        dve.wait_ge(S["root_ready"], l + 1)
                        own.then(V.tensor_tensor(rq, rq, rt, ALU.mult))
                        own.then(V.memset(rq[:, :, 0:1], 0.5))
                        own.then(V.scalar_tensor_tensor(ig, ig, 2.0, rq, ALU.mult, ALU.mult))
                    if s == 7:
                        merge(s, None)
                        dve.wait_ge(S["packed"], 8 * l + 6)
                        for j in range(C4):
                            V.tensor_tensor_scan(hseq[:, j, 0:TP], a_lru[:, j, 0:TP], ig[:, j, 0:TP], 0.0, ALU.mult,
                                                 ALU.add)
                        own.then(V.tensor_tensor(a_lru[:, :, TP:T], a_lru[:, :, TP:T], h0_s[:, l, :, :], ALU.mult))
                        V.tensor_tensor(hseq[:, :, TP:T], a_lru[:, :, TP:T], ig[:, :, TP:T],
                                        ALU.add).then_inc(S["h_ready"], 1)
                        dve.wait_ge(S["h_ready"], l + 1)
                        for j in range(C4):
                            read_out(dve, ("mix", l, 4, j))
                        V.tensor_tensor(rq, hseq, gelu, ALU.mult).then_inc(S["hg_ready"], 1)
                        conv_taps(19, 23)
                    if s == 8:
                        for j in range(C4):
                            dve.wait_ge(S["br_hi"], 2 * l * C4 + j + 1)
                            V.tensor_tensor(brl[:, j, :], rq[:, j, :], brh[:, j, :],
                                            ALU.subtract).then_inc(S["br_ready"], 1)
                        conv_taps(23, 28)
                    if s == 9:
                        conv_taps(28, CW)
                        window_conv(win_s, conv_tap, CW, conv, "conv_b", "conv_done")
                    if s == 10:
                        merge(s, "merge_done")
                    if s == 12:
                        filled(dve, ("cmean", l))
                        filled(dve, ("csq", l))
                        dve.wait_ge(S["cm2_ready"], l + 1)
                        mu = bank(("cmean", l))[:, 0:T]
                        V.tensor_tensor(stat[:, 1, :], bank(("csq", l))[:, 0:T], stat[:, 0, :],
                                        ALU.subtract).then_inc(free_of(("csq", l)), 1)
                        read_out(dve, ("csq", l))
                        V.tensor_scalar(stat[:, 1, :], stat[:, 1, :], 0.0, EPS, ALU.max, ALU.add
                                        ).then_inc(S["cvar_ready"], 1)
                        for j in range(C4):
                            t = V.tensor_tensor(conv[:, j, :], conv[:, j, :], mu, ALU.subtract)
                        t.then_inc(free_of(("cmean", l)), 1)
                        dve.wait_ge(S["cstd_ready"], l + 1)
                        read_out(dve, ("cmean", l))
                        own.then(V.reciprocal(stat[:, 0, :], stat[:, 2, :]))
                        for j in range(C4):
                            V.tensor_tensor(conv[:, j, :], conv[:, j, :], stat[:, 0, :],
                                            ALU.mult).then_inc(S["cv_ready"], 1)
                        for j in range(C4):
                            dve.wait_ge(S["br_hi"], (2 * l + 1) * C4 + j + 1)
                            V.tensor_tensor(brl[:, j, :], conv_sq[:, j, :], brh[:, j, :],
                                            ALU.subtract).then_inc(S["br_ready"], 1)
                    if s == 13:
                        merge(s, "mg_ready")
                        for d in range(KT):
                            dve.wait_ge(S["mg_hi"], l * KT + d + 1)
                            V.tensor_tensor(xl[:, d, :], merged[:, d, :], xh[:, d, :],
                                            ALU.subtract).then_inc(S["mg_split"], 1)
                    if kind == "out":
                        for j in range(4):
                            name = ("mix", l, s, j)
                            d = what[1] * 4 + j
                            filled(dve, name)
                            V.scalar_tensor_tensor(z[:, d, :], x[:, d, :], WS * ALPHA, bank(name)[:, 0:T], ALU.mult,
                                                   ALU.add).then_inc(free_of(name), 1)
                norm(2 * l, ("mean1", l), ("msq1", l), WS, l == 0)
                if l == 0:
                    n = MIX
                    f = 0
                    for g, nf in enumerate(FG):
                        lo(n + AHEAD)
                        lo(n + 1 + AHEAD)
                        for j in range(nf):
                            fg, fu = ("fg", g, j), ("fu", g, j)
                            read_out(dve, fg)
                            if g:
                                dve.wait_ge(S["f_split"], f - 4 + j + 1)
                            filled(dve, fu)
                            V.scalar_tensor_tensor(h_d[:, j, :], bank(fu)[:, 0:T], 1 / WS, silu_d[:, j, :], ALU.mult,
                                                   ALU.mult).then_inc(free_of(fu), 1)
                        for j in range(nf):
                            dve.wait_ge(S["f_hi"], f + j + 1)
                            V.tensor_tensor(hdl[:, f + j, :], h_d[:, j, :], hdh[:, f + j, :],
                                            ALU.subtract).then_inc(S["f_split"], 1)
                        n += 2
                        f += nf
                    for half in range(2):
                        for g in range(len(DG)):
                            lo(n + AHEAD)
                            n += 1
                        for j in range(4 * half, 4 * half + 4):
                            name = ("fd", j)
                            filled(dve, name)
                            V.scalar_tensor_tensor(z[:, j, :], x[:, j, :], WS * ALPHA, bank(name)[:, 0:T], ALU.mult,
                                                   ALU.add).then_inc(free_of(name), 1)
                    norm(1, ("mean2", 0), ("msq2", 0), WS, True)

            own.did(V.memset(yh[:, :], 0.0))
            own.did(V.memset(yl[:, :], 0.0))
            own.did(V.memset(onehot_t, 0.0))
            own.did(V.memset(gate_slot[:, :], 0.0))
            own.did(V.memset(xtl[:, 2, :], 0.0))
            V.memset(xth[:, 2, :], 0.0).then_inc(S["rows_zeroed"], 1)
            V.memset(gsel[:, :, :], 0.0).then_inc(S["e_split"], 1)
            lg = route[:, 1]
            own.then(V.memset(lg, 0.0))
            filled(dve, "logits")
            own.did(V.tensor_copy(lg[:, 0:2, :], bank("logits")[:, 0:2 * NE].rearrange("p (i e) -> p i e", i=2)))
            V.tensor_copy(lg[0:NS_, 2, :], bank("logits")[0:NS_, 2 * NE:3 * NE]).then_inc(free_of("logits"), 1)
            read_out(dve, "logits")
            big = [P, 3, NE]

            def largest(src, sel, m):
                own.then(V.tensor_reduce(m, src, X, ALU.max))
                own.then(V.tensor_tensor(route[:, 8], src, m.unsqueeze(2).to_broadcast(big), ALU.is_equal))
                own.then(V.tensor_tensor(route[:, 8], route[:, 8], idx_w.unsqueeze(1).to_broadcast(big), ALU.mult))
                own.then(V.tensor_reduce(route1[:, 7, :], route[:, 8], X, ALU.max))
                own.then(V.tensor_tensor(sel, route[:, 8], route1[:, 7, :].unsqueeze(2).to_broadcast(big),
                                         ALU.is_equal))

            largest(lg, route[:, 2], route1[:, 0, :])
            own.then(V.scalar_tensor_tensor(route[:, 3], route[:, 2], -1e30, lg, ALU.mult, ALU.add))
            largest(route[:, 3], route[:, 4], route1[:, 1, :])
            V.tensor_tensor(route[:, 0], route[:, 2], route[:, 4], ALU.add).then_inc(S["mask_ready"], 1)
            V.tensor_tensor(route1[:, 3, :], route1[:, 0, :], route1[:, 1, :], ALU.subtract).then_inc(S["gd_ready"], 1)
            dve.wait_ge(S["gs_ready"], 1)
            own.then(V.tensor_tensor(route[:, 5], route[:, 2], route1[:, 4, :].unsqueeze(2).to_broadcast(big), ALU.mult))
            own.then(V.tensor_tensor(route[:, 6], route[:, 4], route1[:, 5, :].unsqueeze(2).to_broadcast(big), ALU.mult))
            own.then(V.tensor_tensor(route[:, 7], route[:, 5], route[:, 6], ALU.add))
            own.then(V.tensor_copy(gate_split[:, :, :, 0], route[:, 7]))
            own.did(V.tensor_tensor(gate_split[:, :, :, 1], route[:, 7], gate_split[:, :, :, 0], ALU.subtract))
            dve.wait_ge(S["mask_ready"], 1)
            own.then(V.memset(rank[:, :, :], -1.0))
            filled(dve, "ranks")
            rk = bank("ranks")
            own.did(V.tensor_tensor(route[:, 9, 0:2, :], rk[:, 0:2 * NE].rearrange("p (i e) -> p i e", i=2),
                                    route[:, 0, 0:2, :], ALU.mult))
            own.then(V.tensor_tensor(route[0:NS_, 9, 2, :], rk[0:NS_, 2 * NE:3 * NE], route[0:NS_, 0, 2, :], ALU.mult))
            own.did(V.tensor_scalar(rank[:, 0:2, :], route[:, 9, 0:2, :], 1.0, None, ALU.subtract))
            own.then(V.tensor_scalar(rank[0:NS_, 2, :], route[0:NS_, 9, 2, :], 1.0, None, ALU.subtract))
            V.tensor_reduce(route1[:, 6, 0:1], rk[:, 3 * NE:4 * NE], X, ALU.max).then_inc(free_of("ranks"), 1)
            read_out(dve, "ranks")
            own.then(V.tensor_scalar(route1[:, 6, 1:2], route1[:, 6, 0:1], float(CAP), float(NE), ALU.is_gt, ALU.mult))
            own.then(V.tensor_scalar(route1[:, 6, 2:3], route1[:, 6, 0:1], float(2 * CAP), float(NE), ALU.is_gt,
                                     ALU.mult))
            own.then(V.tensor_tensor(route1[:, 6, 1:2], route1[:, 6, 1:2], route1[:, 6, 2:3], ALU.add))
            V.tensor_scalar(visits_i[:, :], route1[:, 6, 1:2], float(NE), None, ALU.add).then_inc(S["visits_ready"], 1)
            for i in range(3):
                n = P if i < 2 else NS_
                for h in range(2):
                    name = ("xtok", i, h)
                    q = 2 * i + h + 1
                    dve.wait_ge(S["xt_hi"], q)
                    V.tensor_tensor(xtl[0:n, i, h * 512:(h + 1) * 512], bank(name)[0:n, :],
                                    xth[0:n, i, h * 512:(h + 1) * 512], ALU.subtract).then_inc(free_of(name), 1)

            def select(v, col):
                dve.wait_ge(S["rank_next"], v)
                for i in range(3):
                    V.tensor_scalar(onehot[:, i, :], iota, rank[:, i, col], None, ALU.is_equal)
                t = V.tensor_copy(gsel, gate_split[:, :, col, :])
                t.then_inc(S["onehot_ready"], 1)
                dve.wait_ge(S["onehot_ready"], v + 1)
                V.tensor_scalar(rank[:, :, col], rank[:, :, col], float(CAP), None, ALU.subtract
                                ).then_inc(S["rank_next"], 1)

            def gather_lo(wait):
                for h in range(2):
                    b = 1 + 2 * h
                    wait(dve, "gath_lo", h, b)
                    V.tensor_copy(xgl[:, 4 * h:4 * h + 4, :], ps[:, b, :].rearrange("p (k c) -> p k c", k=4)
                                  ).then_inc(bank_free[b], 1)

            def y_lo(v):
                for h in range(2):
                    dve.wait_ge(S["y_hi"], 2 * v + (h + 1))
                    V.scalar_tensor_tensor(yl[:, h * 512:(h + 1) * 512], ps[:, 4 + h, :], gate_slot[:, 0:1],
                                           yh[:, h * 512:(h + 1) * 512], ALU.mult, ALU.subtract
                                           ).then_inc(bank_free[4 + h], 1)

            select(0, slice(0, 1))
            for j in range(KT):
                n = own.did(V.tensor_scalar(z[:, j, :], x[:, j, :], WS * ALPHA, None, ALU.mult))
            for h in range(2):
                empty(dve, ("y_init", h))
                V.memset(ps[:, 4 + h, :], 0.0).then_inc(bank_full[4 + h], 1)
            own.after(n)
            gather_lo(lambda e, part, h, b: filled(e, (part, h)))
            nv = dve.value_load(visits_i[0:1, 0:1], min_val=NE, max_val=3 * NE)

            def scatter_add(v):
                for d in range(KT):
                    b = 6 + d % 2
                    dve.wait_ge(*in_visit(bank_full, b, v, d // 2))
                    t = V.tensor_tensor(z[:, d, :], z[:, d, :], ps[:, b, 0:T], ALU.add)
                    t.then_inc(bank_free[b], 1)

            with dve.Fori(0, nv) as v:
                def lo_v(m):
                    if m >= VISIT:
                        return
                    n = PRE + m
                    dve.wait_ge(S["hi_done"], v * VISIT + (n + 1))
                    V.scalar_tensor_tensor(w_lo[:, n % SLOTS, :], stage[:, n % SLOTS, :], WS, w_hi[:, n % SLOTS, :],
                                           ALU.mult, ALU.subtract).then_inc(S["lo_done"], 1)

                lo_v(0)
                lo_v(1)
                y_lo(v)
                for m, (kind, c) in enumerate(order):
                    lo_v(m + AHEAD)
                    if kind == "u":
                        b = 2 + c % 2
                        dve.wait_ge(*in_visit(bank_free, b - 2, v, c // 2))
                        dve.wait_ge(*in_visit(bank_full, b, v, c // 2))
                        dve.wait_ge(S["e_split"], v * NC + max(c, 1))
                        V.scalar_tensor_tensor(h_e[:, c % 2, :], ps[:, b, :], 1 / WS, silu_e[:, c % 2, :], ALU.mult,
                                               ALU.mult).then_inc(bank_free[b], 1)
                        dve.wait_ge(S["e_hi"], v * NC + (c + 1))
                        V.tensor_tensor(hl[:, c % 2, :], h_e[:, c % 2, :], hh[:, c % 2, :],
                                        ALU.subtract).then_inc(S["e_split"], 1)
                        if c == 0:
                            scatter_add(v)
                        if c == 1:
                            dve.wait_ge(*in_visit(bank_full, 7, v, 4))
                            V.tensor_copy(onehot_t, ps[:, 7, :].bitcast(F16)[:, 0:T])
                            V.tensor_reduce(gate_slot[:, 0:1], ps[:, 7, 256:258], X, ALU.add
                                            ).then_inc(bank_free[7], 1)
                    if kind == "d" and c == 3:
                        select(v + 1, bass.ds((v + 1) % NE, 1))
                gather_lo(lambda e, part, h, b: e.wait_ge(*in_visit(bank_full, b, v, PER_VISIT[b] - 1)))
            y_lo(nv)
            scatter_add(nv)
            norm(3, ("tail", 0, nv), None, WS, False)


def constants():
    import numpy as np

    c = np.zeros((P, C_ALL), np.float32)
    c[:, C_ID:C_ID + P] = np.eye(P)
    c[:, C_IO:C_IO + CAP] = np.arange(CAP)
    c[:, C_TR:C_TR + P] = np.triu(np.ones((P, P)))
    for g, w in enumerate(WINDOWS):
        c[:, C_IC + g * PW:C_IC + (g + 1) * PW] = 1.0 / np.minimum(w, np.arange(PW) + 1)
    c[:, C_IX:C_IX + NE] = NE - np.arange(NE)
    return c


_INS = ["x_prompt", "x_sample", "state_pool", "state_conv", "state_lru_conv", "state_lru_h", "w_in", "b_gate",
        "w_pool", "pool_scale", "conv_w", "conv_b", "conv_ln_g", "conv_ln_b", "lru_conv_w", "lru_conv_b", "lru_wa",
        "lru_ba", "lru_wx", "lru_bx", "lru_lambda", "w_br_pool", "w_br_conv", "w_br_lru", "w_out", "ln1_g", "ln1_b",
        "ln2_g", "ln2_b", "ffn_w_gate", "ffn_w_up", "ffn_w_down", "moe_router", "moe_w_gate", "moe_w_up",
        "moe_w_down"]
_OUTS = {"y_prompt": (1, TP, D), "y_sample": (NS_, 1, D), "pool_p": (L, 1, PW - 1, DB), "conv_p": (L, 1, CW - 1, DB),
         "lconv_p": (L, 1, LW - 1, DB), "h_p": (L, 1, DB), "pool_s": (L, NS_, PW - 1, DB),
         "conv_s": (L, NS_, CW - 1, DB), "lconv_s": (L, NS_, LW - 1, DB), "h_s": (L, NS_, DB)}


def kernel(**inputs):
    import numpy as np
    import concourse.bacc as bacc
    from concourse.bass_utils import run_bass_kernel_spmd

    nc = bacc.Bacc("TRN2", target_bir_lowering=False, num_devices=1)
    arrays, ins, outs = {}, {}, {}
    for name in _INS:
        arrays[f"in_{name}"] = np.ascontiguousarray(inputs[name])
        ins[name] = nc.dram_tensor(f"in_{name}", arrays[f"in_{name}"].shape, F32, kind="ExternalInput").ap()
    arrays["in_consts"] = constants()
    ins["consts"] = nc.dram_tensor("in_consts", (P, C_ALL), F32, kind="ExternalInput").ap()
    for name, shape in _OUTS.items():
        outs[name] = nc.dram_tensor(f"out_{name}", shape, F32, kind="ExternalOutput").ap()
    trunk_kernel(nc, ins, outs)
    r = run_bass_kernel_spmd(nc, [arrays], core_ids=[0])
    return tuple(r.results[0][f"out_{name}"] for name in _OUTS)
```

```python
from contextlib import ExitStack

import concourse.bass as bass
from concourse import mybir

P = 128
D = 1024
KT = D // P
TP, NS_ = 256, 8
T = TP + NS_
L = 2
C4 = 4
DB = C4 * P
CW, LW, PW = 31, 4, 16
WINDOWS = (2, 4, 8, 16)
IN_COLS = DB * 5 + 3 * D
D_FF, D_EX, NE = 2816, 3584, 8
ALPHA = (2.0 * L) ** 0.25
EPS = 1e-5
WS = 64.0
CAP = 128
SLOTS = 6
PIECE = 2048
AHEAD = 5

F32 = mybir.dt.float32
F16 = mybir.dt.float16
I32 = mybir.dt.int32
ALU = mybir.AluOpType
ACT = mybir.ActivationFunctionType
X = mybir.AxisListType.X

VEC_B = ["pool_scale", "conv_b", "conv_ln_g", "conv_ln_b", "lru_conv_b", "lru_ba", "lru_bx", "lru_lambda"]
NR = len(VEC_B) + CW + LW
VEC_D = ["ln1_g", "ln1_b", "ln2_g", "ln2_b"]
NQ = 3 + len(VEC_D)
C_ID, C_IO, C_TR, C_IC, C_IX, C_ALL = 0, P, P + CAP, 2 * P + CAP, 2 * P + CAP + 64, 2 * P + CAP + 72

IN_ORDER = [("glu", 2), ("val", 1), ("lru", 3), ("pool", 0), ("gelu", 4),
            ("gate", 5, 0, 0), ("gate", 6, 0, 1), ("branch", 0),
            ("gate", 9, 2, 0), ("gate", 10, 2, 1), ("branch", 2),
            ("gate", 7, 1, 0), ("gate", 8, 1, 1), ("branch", 1), ("out", 0), ("out", 1)]
MIX = 2 * len(IN_ORDER)
NF = D_FF // P
FG = [4] * (NF // 4) + ([NF % 4] if NF % 4 else [])
FFN = 4 * len(FG) + 2 * len(FG)
PRE = 2 * MIX + FFN
NC = D_EX // 512
VISIT = 6 * NC
assert VISIT % SLOTS == 0


def visit_order():
    order = []
    for c in range(NC):
        order += [(kind, c, h) for kind in "gu" for h in range(2)]
        if c:
            order += [("d", c - 1, h) for h in range(2)]
    return order + [("d", NC - 1, h) for h in range(2)]


def mixer_piece(l):
    return l * (MIX + FFN)


def psum_plan():
    used = [0] * 8
    place = {}
    turn = [0]

    def put(name, bank=None):
        if bank is None:
            bank = turn[0] % 8
            turn[0] += 1
        place[name] = (bank, used[bank])
        used[bank] += 1

    for k in range(KT):
        put(("xT", k))
    put("par512")
    put("par1024")
    for l in range(L):
        for h in range(2):
            put(("st_conv", l, h))
        put(("st_pool", l))
        put(("st_lru", l))
    for l in range(L):
        for s, what in enumerate(IN_ORDER):
            if what[0] == "branch":
                for j in range(KT):
                    put(("mix", l, s, j))
            elif what[0] == "out":
                for j in range(4):
                    put(("mix", l, s, j))
                if what[1] == 1:
                    put(("mean", 2 * l))
                    put(("msq", 2 * l))
            else:
                for j in range(4):
                    put(("mix", l, s, j))
            if s == 5:
                for j in range(C4):
                    put(("ra", l, j))
                for j in range(C4):
                    put(("ri", l, j))
            if s == 6:
                for j in range(C4):
                    put(("pm", l, j))
            if s == 11:
                put(("cmean", l))
                put(("csq", l))
            if s == 13:
                put(("so", l))
        if l == 0:
            for g, nf in enumerate(FG):
                for j in range(nf):
                    put(("fg", g, j))
                for j in range(nf):
                    put(("fu", g, j))
            for j in range(KT):
                put(("fd", j))
            put(("mean", 1))
            put(("msq", 1))
    put("logits")
    put("ranks")
    for i in range(3):
        for h in range(2):
            put(("xtok", i, h))
    for h in range(2):
        put(("gath_hi", h), 6 + h)
    for h in range(2):
        put(("gath_lo", h), 1 + 2 * h)
    put(("y_init", 0), 4)
    put(("y_init", 1), 5)
    return place, used


PER_VISIT = [4, 4, 4, 4, 3, 3, 3, 4]


def trunk_kernel(nc, A, O):
    place, base = psum_plan()
    order = visit_order()

    with ExitStack() as ctx:
        def sb(name, shape, dt=F32):
            return ctx.enter_context(nc.sbuf_tensor(name, shape, dt))

        def sem(name):
            return ctx.enter_context(nc.semaphore(name))

        stage = sb("stage", [P, SLOTS, PIECE])
        w_hi = sb("w_hi", [P, SLOTS, PIECE], F16)
        w_lo = sb("w_lo", [P, SLOTS, PIECE], F16)
        x = sb("x", [P, KT, T])
        xh = sb("xh", [P, KT, T], F16)
        xl = sb("xl", [P, KT, T], F16)
        z = sb("z", [P, KT, T])
        zsq = sb("zsq", [P, KT, T])
        merged = zsq
        conv_sq = z[:, 0:C4, :]
        rt = z[:, 0:C4, :]
        pooled = z[:, C4:KT, :]
        y_pool = z[:, C4:KT, :]
        win_s = sb("win_s", [P, L, C4, NS_, CW])
        pool_s = sb("pool_s", [P, L, C4, NS_, PW])
        lru_s = sb("lru_s", [P, L, C4, NS_, LW])
        h0_s = sb("h0_s", [P, L, C4, NS_])
        consts = sb("consts", [P, C_ALL])
        ident = consts[:, C_ID:C_ID + P]
        iota = consts[:, C_IO:C_IO + CAP]
        tri = consts[:, C_TR:C_TR + P]
        inv_cnt = consts[:, C_IC:C_IC + 64].rearrange("p (g w) -> p g w", g=4)
        idx_w = consts[:, C_IX:C_IX + NE]
        ones_d = sb("ones_d", [P, P])
        ones_b = sb("ones_b", [P, P])
        par = sb("par", [P, C4, L * NR])
        par_d = sb("par_d", [P, KT, L * NQ])
        sp4 = sb("sp4", [P, C4, L])
        spt = sb("spt", [P, 6, C4, L])
        w_pool = sb("w_pool", [P, C4, P])
        w_a = sb("w_a", [P, C4, P])
        w_x = sb("w_x", [P, C4, P])
        stat = sb("stat", [P, 3, T])
        warm = sb("warm", [P, 1])
        zsum, zsqsum = stat[:, 0, :], stat[:, 1, :]
        w_rt = sb("w_rt", [P, KT, NE])
        visits_i = sb("visits_i", [P, 1], I32)
        route = sb("route", [P, 10, 3, NE])
        route1 = sb("route1", [P, 8, 3])
        rank = sb("rank", [P, 3, NE])
        gate_split = sb("gate_split", [P, 3, NE, 2], F16)
        gate_slot = sb("gate_slot", [P, 1])
        ident16 = sb("ident16", [P, P], F16)

        ARENA = 12600
        arena = sb("arena", [P, ARENA])
        at = [0]

        def carve(shape, dt=F32, start=None):
            n = 1
            for s in shape:
                n *= s
            words = n if dt == F32 else (n + 1) // 2
            o = at[0] if start is None else start
            at[0] = o + words
            assert at[0] <= ARENA
            v = arena[:, o:o + words]
            v = v.bitcast(dt)[:, 0:n] if dt != F32 else v
            if len(shape) == 2:
                v = v.rearrange("p (a b) -> p a b", a=shape[0])
            if len(shape) == 3:
                v = v.rearrange("p (a b c) -> p a b c", a=shape[0], b=shape[1])
            return v

        x_rows = carve([2, D], start=0)
        xs_rows = carve([D])
        conv_rows = carve([L, 2, DB])
        pool_rows = carve([L, DB])
        lru_rows = carve([L, DB])
        par_rows = carve([DB])
        pard_rows = carve([D])
        gates = carve([KT, T], start=0)
        glu = carve([C4, CW - 1 + TP])
        conv = carve([C4, T])
        upool_at = at[0]
        upool = carve([C4, PW - 1 + TP])
        hseq = carve([C4, T], start=upool_at)
        at[0] = upool_at + C4 * (PW - 1 + TP)
        ulru_at = at[0]
        ulru = carve([C4, LW - 1 + TP])
        rq = carve([C4, T], start=ulru_at)
        xc = carve([C4, T])
        ig = carve([C4, T])
        gelu = carve([C4, T])
        sg = carve([C4, T])
        a_lru = sg
        brh = carve([C4, T], F16)
        brl = carve([C4, T], F16)
        so = carve([C4, 81])
        so_out = carve([DB])
        wsum = carve([2, PW - 1 + TP], start=0)
        prod = stat[:, 2, 0:NS_ * CW].rearrange("p (b k) -> p b k", b=NS_)
        hdh = carve([NF, T], F16, start=0)
        hdl = carve([NF, T], F16)
        silu_d = carve([4, T])
        h_d = carve([4, T])
        xth = carve([3, D], F16, start=0)
        xtl = carve([3, D], F16)
        xgh = carve([KT, CAP], F16)
        xgl = carve([KT, CAP], F16)
        silu_e = carve([2, 512])
        h_e = carve([2, 512])
        hh = carve([2, 512], F16)
        hl = carve([2, 512], F16)
        yh = carve([D], F16)
        yl = carve([D], F16)
        onehot = carve([3, CAP], F16)
        onehot_t = carve([T], F16)
        gsel = carve([3, 2], F16)
        y_rows = carve([3, D])

        ps = ctx.enter_context(nc.psum_tensor("ps", [P, 8, 512], F32))

        names = """ld_x ld_const ld_par ld_state ld_small out_dma y_out hi_done lo_done part_used
            x_hi x_split zeroed rows_zeroed dve gates_zeroed xc_ready tanh_ready q_ready root_ready h_ready
            hg_ready br_hi br_ready pooled_ready conv_done csq_done cv_ready silu_ready merge_done
            mg_ready mg_hi mg_split packed zsq_ready m2_ready var_ready std_ready nz_ready norm_ready
            f_hi f_split gd_ready gs_ready mask_ready visits_ready sp_abs sp_exp sp_done x_pool zadd
            xt_hi onehot_ready rank_next e_hi e_split y_hi cm2_ready cvar_ready cstd_ready""".split()
        S = {n: sem(n) for n in names}
        stage_full = [sem(f"stage_full{i}") for i in range(SLOTS)]
        bank_full = [sem(f"bank_full{i}") for i in range(8)]
        bank_free = [sem(f"bank_free{i}") for i in range(8)]

        def bank(name):
            return ps[:, place[name][0], :]

        def filled(eng, name):
            b, k = place[name]
            eng.wait_ge(bank_full[b], k + 1)

        def empty(eng, name):
            b, k = place[name]
            if k:
                eng.wait_ge(bank_free[b], k)

        def read_out(eng, name):
            b, k = place[name]
            eng.wait_ge(bank_free[b], k + 1)

        def in_visit(sems, b, v, i):
            return sems[b], v * PER_VISIT[b] + (base[b] + i + 1)

        def free_of(name):
            return bank_free[place[name][0]]

        def full_of(name):
            return bank_full[place[name][0]]

        def vec(name, l, j):
            r = VEC_B.index(name) * L + l
            return par[:, j, r:r + 1]

        def conv_tap(l, j, k, n=1):
            r = len(VEC_B) * L + l * CW + k
            return par[:, j, r:r + n]

        def lru_tap(l, j, k, n=1):
            r = (len(VEC_B) + CW) * L + l * LW + k
            return par[:, j, r:r + n]

        def gate_bias(l, b, d):
            return par_d[:, d, l * 3 + b:l * 3 + b + 1]

        def vec_d(name, l, d):
            r = 3 * L + VEC_D.index(name) * L + l
            return par_d[:, d, r:r + 1]

        def piece_done(eng, n):
            last = last_tile[n]
            if last is None:
                eng.wait_ge(S["part_used"], part_no[n])
            else:
                filled(eng, last)

        def wh(slot, k, c0, c1, width=512):
            return w_hi[:, slot, k * width + c0:k * width + c1]

        def wl(slot, k, c0, c1, width=512):
            return w_lo[:, slot, k * width + c0:k * width + c1]

        class Steps:

            def __init__(self, eng, s):
                self.eng, self.sem, self.n = eng, s, 0

            def did(self, ins):
                self.n += 1
                ins.then_inc(self.sem, 1)
                return self.n

            def after(self, n):
                self.eng.wait_ge(self.sem, n)

            def then(self, ins):
                self.after(self.did(ins))

        def pre_piece(n):
            if n >= PRE:
                return visit_piece(slice(0, 1), n - PRE)
            l, s = (0, n) if n < MIX + FFN else (1, n - MIX - FFN)
            if s < MIX:
                s, half = s // 2, s % 2
                what = IN_ORDER[s]
                if what[0] == "branch":
                    w = (A["w_br_pool"], A["w_br_conv"], A["w_br_lru"])[what[1]]
                    return w[l, :, half * 512:half * 512 + 512].rearrange("(k p) n -> p k n", p=P), C4, 512
                w = A["w_out"] if what[0] == "out" else A["w_in"]
                c = what[1] * 512
                return w[l, half * 512:half * 512 + 512, c:c + 512].rearrange("(k p) n -> p k n", p=P), 4, 512
            s -= MIX
            if s < 4 * len(FG):
                g, up, half = s // 4, s // 2 % 2, s % 2
                w = (A["ffn_w_gate"], A["ffn_w_up"])[up]
                n_ = FG[g] * P
                return (w[0, half * 512:half * 512 + 512, 512 * g:512 * g + n_]
                        .rearrange("(k p) n -> p k n", p=P)), 4, n_
            s -= 4 * len(FG)
            half, g = s // len(FG), s % len(FG)
            return (A["ffn_w_down"][0, 512 * g:512 * g + FG[g] * P, half * 512:half * 512 + 512]
                    .rearrange("(k p) n -> p k n", p=P)), FG[g], 512

        def visit_piece(e, m):
            kind, c, h = order[m]
            if kind == "d":
                return (A["moe_w_down"][0, e, c * 512 + h * 256:c * 512 + h * 256 + 256, :]
                        .rearrange("a (k p) n -> (a p) k n", p=P)), 2, D
            w = A["moe_w_gate"] if kind == "g" else A["moe_w_up"]
            return (w[0, e, h * 512:h * 512 + 512, c * 512:(c + 1) * 512]
                    .rearrange("a (k p) n -> (a p) k n", p=P)), 4, 512

        last_tile, part_no = {}, {}

        def ends(n, tile):
            last_tile[n] = tile
            if tile is None:
                part_no[n] = len(part_no) + 1

        for l in range(L):
            for s, what in enumerate(IN_ORDER):
                n = mixer_piece(l) + 2 * s
                branch = what[0] == "branch"
                ends(n, ("mix", l, s, 3) if branch else None)
                ends(n + 1, ("mix", l, s, KT - 1 if branch else 3))
            if l == 0:
                for g, nf in enumerate(FG):
                    for i, nm in enumerate(("fg", "fu")):
                        ends(MIX + 4 * g + 2 * i, None)
                        ends(MIX + 4 * g + 2 * i + 1, (nm, g, nf - 1))
                for half in range(2):
                    for g in range(len(FG)):
                        ends(MIX + 4 * len(FG) + half * len(FG) + g,
                             ("fd", 4 * half + 3) if g == len(FG) - 1 else None)
        PART0 = len(part_no)
        part_in_visit = [m for m, (kind, c, h) in enumerate(order) if h == 0 or (kind == "d" and c < NC - 1)]
        NPART = len(part_in_visit)
        GATHER_AT = VISIT - 2

        block = ctx.enter_context(nc.Block())

        @block.sync
        def _(sp):
            sp.dma_start(x_rows, A["x_prompt"][0].rearrange("(a p) n -> p a n", p=P)).then_inc(S["ld_x"], 16)
            sp.dma_start(xs_rows[0:NS_, :], A["x_sample"].rearrange("b s n -> (b s) n")).then_inc(S["ld_x"], 16)

            def load(src, tiles, width, slot):
                dst = stage[:, slot, 0:tiles * width].rearrange("p (k n) -> p k n", k=tiles)
                sp.dma_start(dst, src).then_inc(stage_full[slot], 16)

            for n in range(PRE):
                if n >= SLOTS:
                    sp.wait_ge(S["lo_done"], n - SLOTS + 1)
                load(*pre_piece(n), n % SLOTS)

            def visit(v):
                e = v % NE
                for m in range(VISIT):
                    n = PRE + m
                    sp.wait_ge(S["lo_done"], v * VISIT + (n - SLOTS + 1))
                    load(*visit_piece(bass.ds(e, 1), m), n % SLOTS)

            with sp.Fori(0, NE) as v:
                visit(v)
            sp.wait_ge(S["visits_ready"], 1)
            nv = sp.value_load(visits_i[0:1, 0:1], min_val=NE, max_val=3 * NE)
            with sp.If(nv > NE):
                with sp.Fori(NE, nv) as v:
                    visit(v)
            sp.nop()
            sp.wait_ge(S["out_dma"], 16 * 11 * L)
            sp.wait_ge(S["y_out"], 16 * 3)

        @block.gpsimd
        def _(pool):
            for l in range(L):
                for h in range(2):
                    pool.dma_start(conv_rows[0:4 * (CW - 1), l, h, :],
                                   A["state_conv"][l, 4 * h:4 * h + 4].rearrange("b r n -> (b r) n")
                                   ).then_inc(S["ld_state"], 16)
                pool.dma_start(pool_rows[0:NS_ * (PW - 1), l, :],
                               A["state_pool"][l].rearrange("b r n -> (b r) n")).then_inc(S["ld_state"], 16)
                pool.dma_start(lru_rows[0:NS_ * (LW - 1), l, :],
                               A["state_lru_conv"][l].rearrange("b r n -> (b r) n")).then_inc(S["ld_state"], 16)
                pool.dma_start(lru_rows[24:24 + NS_, l, :], A["state_lru_h"][l]).then_inc(S["ld_state"], 16)
            nc.gpsimd.memset(w_a[:], 0.0).then_inc(S["gates_zeroed"], 1)
            nc.gpsimd.memset(w_x[:], 0.0).then_inc(S["gates_zeroed"], 1)
            pool.wait_ge(S["gates_zeroed"], 2)

            def small(l):
                pool.dma_start(w_pool[:, :, :], A["w_pool"][l].rearrange("g c d -> c g d")).then_inc(S["ld_small"], 16)
                for w, t in ((A["lru_wa"], w_a), (A["lru_wx"], w_x)):
                    for h in range(2):
                        pool.dma_start(t[64 * h:64 * h + 64, :, 64 * h:64 * h + 64],
                                       w[l].rearrange("(j h) c d -> h c j d", h=2)[h]).then_inc(S["ld_small"], 16)

            small(0)
            pool.dma_start(w_rt[:, :, :], A["moe_router"][0].rearrange("(k p) n -> p k n", p=P)
                           ).then_inc(S["ld_small"], 16)
            for l in range(L):
                pool.dma_start(O["conv_s"][l, :, 0:CW - 2, :], A["state_conv"][l, :, 1:CW - 1, :]
                               ).then_inc(S["out_dma"], 16)
                pool.dma_start(O["pool_s"][l, :, 0:PW - 2, :], A["state_pool"][l, :, 1:PW - 1, :]
                               ).then_inc(S["out_dma"], 16)
                pool.dma_start(O["lconv_s"][l, :, 0:LW - 2, :], A["state_lru_conv"][l, :, 1:LW - 1, :]
                               ).then_inc(S["out_dma"], 16)
            def norm(q, tiles, l, g):
                for j in range(1, KT - 1):
                    for i, (src, dst) in enumerate(((z, zsum), (zsq, zsqsum))):
                        if i == 0:
                            for jj in ((0, 1) if j == 1 else (j,)):
                                read_out(pool, tiles[jj])
                        else:
                            pool.wait_ge(S["zsq_ready"], q * KT + j + 1)
                        if j > 1:
                            pool.wait_ge(S["zadd"], 2 * (q * (KT - 2) + j - 2) + i + 1)
                        nc.gpsimd.tensor_tensor(dst, src[:, 0, :] if j == 1 else dst, src[:, j, :],
                                                ALU.add).then_inc(S["zadd"], 1)
                if q < 2:
                    for j in range(KT):
                        pool.wait_ge(S["nz_ready"], q * KT + j + 1)
                        nc.gpsimd.tensor_scalar(x[:, j, :], z[:, j, :], 1.0, vec_d(g, l, j), ALU.mult,
                                                ALU.add).then_inc(S["x_pool"], 1)

            for l in range(L):
                for j in range(C4):
                    read_out(pool, ("mix", l, 1, j))
                nc.gpsimd.tensor_copy(so[:, :, 0:30], glu[:, :, TP:TP + 30]).then_inc(S["packed"], 1)
                nc.gpsimd.tensor_copy(so[:, :, 49:57], win_s[:, l, :, :, CW - 1]).then_inc(S["packed"], 1)
                for j in range(C4):
                    read_out(pool, ("mix", l, 2, j))
                nc.gpsimd.tensor_copy(so[:, :, 45:48], ulru[:, :, TP:TP + 3]).then_inc(S["packed"], 1)
                nc.gpsimd.tensor_copy(so[:, :, 65:73], lru_s[:, l, :, :, LW - 1]).then_inc(S["packed"], 1)
                for j in range(C4):
                    read_out(pool, ("mix", l, 3, j))
                nc.gpsimd.tensor_copy(so[:, :, 30:45], upool[:, :, TP:TP + 15]).then_inc(S["packed"], 1)
                nc.gpsimd.tensor_copy(so[:, :, 57:65], pool_s[:, l, :, :, PW - 1]).then_inc(S["packed"], 1)
                pool.wait_ge(S["h_ready"], l + 1)
                nc.gpsimd.tensor_copy(so[:, :, 48:49], hseq[:, :, TP - 1:TP]).then_inc(S["packed"], 1)
                nc.gpsimd.tensor_copy(so[:, :, 73:81], hseq[:, :, TP:T]).then_inc(S["packed"], 1)
                if l + 1 < L:
                    filled(pool, ("pm", l, C4 - 1))
                    small(l + 1)
                read_out(pool, ("so", l))
                for dst, r0, r1 in ((O["conv_p"][l, 0], 0, 30), (O["pool_p"][l, 0], 30, 45), (O["lconv_p"][l, 0], 45, 48),
                                    (O["h_p"][l], 48, 49), (O["conv_s"][l, :, CW - 2, :], 49, 57),
                                    (O["pool_s"][l, :, PW - 2, :], 57, 65), (O["lconv_s"][l, :, LW - 2, :], 65, 73),
                                    (O["h_s"][l], 73, 81)):
                    pool.dma_start(dst, so_out[r0:r1, :]).then_inc(S["out_dma"], 16)
                norm(2 * l, [("mix", l, 14 + j // 4, j % 4) for j in range(KT)], l, "ln1_b")
                if l == 0:
                    norm(1, [("fd", j) for j in range(KT)], l, "ln2_b")

        @block.tensor
        def _(pe):
            mm = nc.tensor.matmul

            def mm3(out, ah, al, bh, bl, start, stop):
                mm(out, ah, bh, start=start, stop=False, skip_group_check=True)
                mm(out, ah, bl, start=False, stop=False, skip_group_check=True)
                return mm(out, al, bh, start=False, stop=stop, skip_group_check=True)

            pe.wait_ge(S["ld_const"], 16)
            pe.wait_ge(S["ld_x"], 32)
            for k in range(KT):
                o = bank(("xT", k))
                for a in range(2):
                    nc.tensor.transpose(o[:, a * P:(a + 1) * P], x_rows[:, a, k * P:(k + 1) * P], ident)
                nc.tensor.transpose(o[:, TP:T], xs_rows[0:NS_, k * P:(k + 1) * P],
                                    ident[0:NS_, 0:NS_]).then_inc(full_of(("xT", k)), 1)
            pe.wait_ge(S["ld_par"], 16 * 15)
            empty(pe, "par512")
            for j in range(C4):
                t = nc.tensor.transpose(bank("par512")[:, j * L * NR:(j + 1) * L * NR],
                                        par_rows[0:L * NR, j * P:(j + 1) * P], ident[0:L * NR, 0:L * NR])
            t.then_inc(full_of("par512"), 1)
            empty(pe, "par1024")
            for j in range(KT):
                t = nc.tensor.transpose(bank("par1024")[:, j * L * NQ:(j + 1) * L * NQ],
                                        pard_rows[0:L * NQ, j * P:(j + 1) * P], ident[0:L * NQ, 0:L * NQ])
            t.then_inc(full_of("par1024"), 1)
            pe.wait_ge(S["ld_state"], 16 * 5 * L)
            for l in range(L):
                R = 4 * (CW - 1)
                for h in range(2):
                    n = ("st_conv", l, h)
                    empty(pe, n)
                    for j in range(C4):
                        t = nc.tensor.transpose(bank(n)[:, j * R:(j + 1) * R],
                                                conv_rows[0:R, l, h, j * P:(j + 1) * P], ident[0:R, 0:R])
                    t.then_inc(full_of(n), 1)
                R = NS_ * (PW - 1)
                n = ("st_pool", l)
                empty(pe, n)
                for j in range(C4):
                    t = nc.tensor.transpose(bank(n)[:, j * R:(j + 1) * R],
                                            pool_rows[0:R, l, j * P:(j + 1) * P], ident[0:R, 0:R])
                t.then_inc(full_of(n), 1)
                n = ("st_lru", l)
                empty(pe, n)
                for j in range(C4):
                    t = nc.tensor.transpose(bank(n)[:, j * 32:j * 32 + 32],
                                            lru_rows[0:32, l, j * P:(j + 1) * P], ident[0:32, 0:32])
                t.then_inc(full_of(n), 1)

            def stats(q, last):
                mean, msq = ("mean", q), ("msq", q)
                pe.wait_ge(S["zadd"], 2 * (q + 1) * (KT - 2))
                empty(pe, mean)
                mm(bank(mean)[:, 0:T], ones_d[:, :], zsum, start=True, stop=False, skip_group_check=True)
                empty(pe, msq)
                mm(bank(msq)[:, 0:T], ones_d[:, :], zsqsum, start=True, stop=False, skip_group_check=True)
                read_out(pe, last)
                mm(bank(mean)[:, 0:T], ones_d[:, :], z[:, KT - 1, :], start=False, stop=True,
                   skip_group_check=True).then_inc(full_of(mean), 1)
                pe.wait_ge(S["zsq_ready"], (q + 1) * KT)
                mm(bank(msq)[:, 0:T], ones_d[:, :], zsq[:, KT - 1, :], start=False, stop=True,
                   skip_group_check=True).then_inc(full_of(msq), 1)

            for l in range(L):
                b0 = mixer_piece(l)
                for s, what in enumerate(IN_ORDER):
                    kind = what[0]
                    if s == 0 and l == 0:
                        for k in range(KT):
                            read_out(pe, ("xT", k))
                    if kind == "branch":
                        pe.wait_ge(S["br_ready"], (3 * l + {0: 1, 2: 2, 1: 3}[what[1]]) * C4)
                    for half in range(2):
                        n = b0 + 2 * s + half
                        slot = n % SLOTS
                        if s == 0 and l:
                            pe.wait_ge(S["x_split"], KT + 4 * (half + 1))
                        if s == 14:
                            pe.wait_ge(S["mg_split"], l * KT + 4 * (half + 1))
                        pe.wait_ge(S["lo_done"], n + 1)
                        for j in range(4):
                            if kind == "branch":
                                name = ("mix", l, s, 4 * half + j)
                                empty(pe, name)
                                for k in range(C4):
                                    t = mm3(bank(name)[:, 0:T], wh(slot, k, j * P, (j + 1) * P),
                                            wl(slot, k, j * P, (j + 1) * P), brh[:, k, :], brl[:, k, :],
                                            k == 0, k == C4 - 1)
                                t.then_inc(full_of(name), 1)
                            else:
                                name = ("mix", l, s, j)
                                if half == 0:
                                    empty(pe, name)
                                for k in range(4):
                                    kk = 4 * half + k
                                    t = mm3(bank(name)[:, 0:T], wh(slot, k, j * P, (j + 1) * P),
                                            wl(slot, k, j * P, (j + 1) * P), xh[:, kk, :], xl[:, kk, :],
                                            kk == 0, kk == KT - 1)
                                if half:
                                    t.then_inc(full_of(name), 1)
                        if last_tile[n] is None:
                            t.then_inc(S["part_used"], 1)
                    if s == 5:
                        pe.wait_ge(S["ld_small"], 16 * (6 + 5 * l))
                        for nm, w in (("ra", w_a), ("ri", w_x)):
                            for j in range(C4):
                                pe.wait_ge(S["xc_ready"], l * C4 + j + 1)
                                empty(pe, (nm, l, j))
                                mm(bank((nm, l, j))[:, 0:T], w[:, j, :], xc[:, j, :], start=True,
                                   stop=True).then_inc(full_of((nm, l, j)), 1)
                    if s == 6:
                        for j in range(C4):
                            pe.wait_ge(S["pooled_ready"], l * C4 + j + 1)
                            empty(pe, ("pm", l, j))
                            mm(bank(("pm", l, j))[:, 0:T], w_pool[:, j, :], pooled[:, j, :], start=True,
                               stop=True).then_inc(full_of(("pm", l, j)), 1)
                    if s == 11:
                        pe.wait_ge(S["csq_done"], l + 1)
                        for nm, src in (("cmean", conv), ("csq", conv_sq)):
                            empty(pe, (nm, l))
                            for j in range(C4):
                                t = mm(bank((nm, l))[:, 0:T], ones_b[:, :], src[:, j, :],
                                       start=(j == 0), stop=(j == C4 - 1))
                            t.then_inc(full_of((nm, l)), 1)
                    if s == 13:
                        pe.wait_ge(S["packed"], 8 * (l + 1))
                        empty(pe, ("so", l))
                        for j in range(C4):
                            t = nc.tensor.transpose(bank(("so", l))[0:81, j * P:(j + 1) * P], so[:, j, 0:81],
                                                    ident)
                        t.then_inc(full_of(("so", l)), 1)
                stats(2 * l, ("mix", l, 15, 3))
                if l == 0:
                    n = MIX
                    for g, nf in enumerate(FG):
                        for nm in ("fg", "fu"):
                            for half in range(2):
                                if n < MIX + 2:
                                    pe.wait_ge(S["x_split"], 4 * (half + 1))
                                pe.wait_ge(S["lo_done"], n + 1)
                                for j in range(nf):
                                    name = (nm, g, j)
                                    if half == 0:
                                        empty(pe, name)
                                    for k in range(4):
                                        kk = 4 * half + k
                                        t = mm3(bank(name)[:, 0:T], wh(n % SLOTS, k, j * P, (j + 1) * P, nf * P),
                                                wl(n % SLOTS, k, j * P, (j + 1) * P, nf * P), xh[:, kk, :],
                                                xl[:, kk, :], kk == 0, kk == KT - 1)
                                    if half:
                                        t.then_inc(full_of(name), 1)
                                if half == 0:
                                    t.then_inc(S["part_used"], 1)
                                n += 1
                    for half in range(2):
                        for g, nf in enumerate(FG):
                            pe.wait_ge(S["lo_done"], n + 1)
                            pe.wait_ge(S["f_split"], 4 * g + nf)
                            for j in range(4):
                                name = ("fd", half * 4 + j)
                                if g == 0:
                                    empty(pe, name)
                                for k in range(nf):
                                    f = 4 * g + k
                                    t = mm3(bank(name)[:, 0:T], wh(n % SLOTS, k, j * P, (j + 1) * P),
                                            wl(n % SLOTS, k, j * P, (j + 1) * P), hdh[:, f, :],
                                            hdl[:, f, :], f == 0, f == NF - 1)
                                if g == len(FG) - 1:
                                    t.then_inc(full_of(name), 1)
                            if g < len(FG) - 1:
                                t.then_inc(S["part_used"], 1)
                            n += 1
                    stats(1, ("fd", KT - 1))

            pe.wait_ge(S["norm_ready"], KT)
            pe.wait_ge(S["ld_small"], 16 * 11)
            empty(pe, "logits")
            for i in range(3):
                n = P if i < 2 else NS_
                for k in range(KT):
                    t = mm(bank("logits")[0:n, i * NE:(i + 1) * NE], x[:, k, i * P:i * P + n], w_rt[:, k, :],
                           start=(k == 0), stop=(k == KT - 1))
            t.then_inc(full_of("logits"), 1)
            for i in range(3):
                n = P if i < 2 else NS_
                for h in range(2):
                    name = ("xtok", i, h)
                    empty(pe, name)
                    for k in range(4):
                        kk = 4 * h + k
                        t = nc.tensor.transpose(bank(name)[0:n, k * P:(k + 1) * P], x[:, kk, i * P:i * P + n],
                                                ident)
                    t.then_inc(full_of(name), 1)
            pe.wait_ge(S["mask_ready"], 1)
            empty(pe, "ranks")
            rk = bank("ranks")
            mask = route[:, 0, :, :]
            for i in range(3):
                n = P if i < 2 else NS_
                for q in range(i):
                    mm(rk[0:n, i * NE:(i + 1) * NE], ones_d[:, 0:n], mask[:, q, :], start=(q == 0), stop=False)
                mm(rk[0:n, i * NE:(i + 1) * NE], tri[0:n, 0:n], mask[0:n, i, :], start=(i == 0), stop=True)
            for i in range(3):
                n = P if i < 2 else NS_
                t = mm(rk[:, 3 * NE:4 * NE], ones_d[0:n, :], mask[0:n, i, :], start=(i == 0), stop=(i == 2))
            t.then_inc(full_of("ranks"), 1)

            def gather(v, in_loop):
                pe.wait_ge(S["onehot_ready"], v + 1)
                for part, rows, banks in (("gath_hi", xth, (6, 7)), ("gath_lo", xtl, (1, 3))):
                    for h, b in enumerate(banks):
                        if in_loop is None:
                            empty(pe, (part, h))
                        else:
                            pe.wait_ge(*in_visit(bank_free, b, in_loop, PER_VISIT[b] - 2))
                        for k in range(4):
                            for i in range(3):
                                t = mm(ps[:, b, k * CAP:(k + 1) * CAP],
                                       rows[:, i, (4 * h + k) * P:(4 * h + k + 1) * P],
                                       onehot[:, i, :], start=(i == 0), stop=(i == 2))
                        t.then_inc(bank_full[b], 1)

            def scatter(v, batch):
                if batch == 0:
                    for b in (4, 5):
                        pe.wait_ge(*in_visit(bank_free, b, v, -1))
                for b in range(4, 8):
                    d = 4 * batch + b - 4
                    pe.wait_ge(*in_visit(bank_free, b, v, batch - 1))
                    mm(ps[:, b, 0:T], yh[:, d * P:(d + 1) * P], onehot_t, start=True, stop=False)
                    mm(ps[:, b, 0:T], yl[:, d * P:(d + 1) * P], onehot_t, start=False,
                       stop=True).then_inc(bank_full[b], 1)

            for i in range(3):
                for h in range(2):
                    read_out(pe, ("xtok", i, h))
            gather(0, None)
            pe.wait_ge(S["visits_ready"], 1)
            nv = pe.value_load(visits_i[0:1, 0:1], min_val=NE, max_val=3 * NE)

            with pe.Fori(0, nv) as v:
                def slot_of(m):
                    return (PRE + m) % SLOTS

                def half_piece(c, kind, h):
                    m = order.index((kind, c, h))
                    slot = slot_of(m)
                    b = c % 2 + (0 if kind == "g" else 2)
                    pe.wait_ge(S["lo_done"], v * VISIT + (PRE + m + 1))
                    if h == 0:
                        pe.wait_ge(*in_visit(bank_free, b, v, c // 2 - 1))
                    for j in range(4):
                        for k in range(4):
                            kk = 4 * h + k
                            t = mm3(ps[:, b, j * CAP:(j + 1) * CAP], wh(slot, k, j * P, (j + 1) * P),
                                    wl(slot, k, j * P, (j + 1) * P), xgh[:, kk, :], xgl[:, kk, :],
                                    kk == 0 and j == 0, kk == KT - 1)
                    t.then_inc(bank_full[b] if h else S["part_used"], 1)

                def gate_up(c, kinds="gu"):
                    if c == 0:
                        for b in (6, 7, 1, 3):
                            pe.wait_ge(*in_visit(bank_free, b, v, -1))
                    for kind in kinds:
                        for h in range(2):
                            half_piece(c, kind, h)

                def down(c):
                    pe.wait_ge(S["e_split"], v * NC + (c + 2))
                    for h in range(2):
                        m = order.index(("d", c, h))
                        slot = slot_of(m)
                        pe.wait_ge(S["lo_done"], v * VISIT + (PRE + m + 1))
                        for half in range(2):
                            b = 4 + half
                            if c == 0 and h == 0:
                                pe.wait_ge(*in_visit(bank_free, b, v, 1))
                            for k in range(2):
                                f = 2 * h + k
                                t = mm3(ps[:, b, :], hh[:, c % 2, f * P:(f + 1) * P], hl[:, c % 2, f * P:(f + 1) * P],
                                        wh(slot, k, half * 512, half * 512 + 512, D),
                                        wl(slot, k, half * 512, half * 512 + 512, D),
                                        c == 0 and f == 0, c == NC - 1 and f == 3)
                            if c == NC - 1 and h:
                                t.then_inc(bank_full[b], 1)
                        if not (c == NC - 1 and h):
                            t.then_inc(S["part_used"], 1)

                gate_up(0)
                scatter(v, 0)
                gate_up(1, "g")
                scatter(v, 1)
                gate_up(1, "u")
                pe.wait_ge(*in_visit(bank_free, 7, v, 1))
                st = ps[:, 7, :].bitcast(F16)
                for i in range(3):
                    n = P if i < 2 else NS_
                    nc.tensor.transpose(st[:, i * P:i * P + n], onehot[0:n, i, :], ident16[0:n, 0:n])
                for i in range(3):
                    t = mm(ps[:, 7, 256:258], onehot[:, i, :], gsel[:, i, :], start=(i == 0), stop=(i == 2))
                t.then_inc(bank_full[7], 1)
                down(0)
                for c in range(2, NC):
                    gate_up(c)
                    if c < NC - 1:
                        down(c - 1)
                down(NC - 2)
                gather(v + 1, v)
                down(NC - 1)

            scatter(nv, 0)
            scatter(nv, 1)
            for j in range(KT):
                pe.wait_ge(*in_visit(bank_free, 4 + j % 4, nv, j // 4))
                if j == 0:
                    pe.wait_ge(*in_visit(bank_free, 0, nv, -1))
                t = mm(ps[:, 0, 0:T], ones_d[:, :], z[:, j, :], start=(j == 0), stop=(j == KT - 1),
                       skip_group_check=True)
                if j == KT - 1:
                    t.then_inc(bank_full[0], 1)
                pe.wait_ge(S["zsq_ready"], 3 * KT + j + 1)
                if j == 0:
                    pe.wait_ge(*in_visit(bank_free, 1, nv, -1))
                t = mm(ps[:, 1, 0:T], ones_d[:, :], zsq[:, j, :], start=(j == 0), stop=(j == KT - 1),
                       skip_group_check=True)
                if j == KT - 1:
                    t.then_inc(bank_full[1], 1)
            pe.wait_ge(S["norm_ready"], 2 * KT)
            for i in range(3):
                n = P if i < 2 else NS_
                for h in range(2):
                    b = 2 + h
                    pe.wait_ge(*in_visit(bank_free, b, nv, i - 1))
                    for k in range(4):
                        t = nc.tensor.transpose(ps[0:n, b, k * P:(k + 1) * P], x[:, 4 * h + k, i * P:i * P + n],
                                                ident)
                    t.then_inc(bank_full[b], 1)
        @block.scalar
        def _(act):
            fn = nc.scalar.activation

            def hi(n):
                tiles, width = pre_piece(n)[1:]
                act.wait_ge(stage_full[n % SLOTS], 16 * (n // SLOTS + 1))
                if n >= SLOTS:
                    piece_done(act, n - SLOTS)
                fn(w_hi[:, n % SLOTS, 0:tiles * width], stage[:, n % SLOTS, 0:tiles * width], ACT.Copy,
                   scale=WS).then_inc(S["hi_done"], 1)

            def norm(q, mean, l, b):
                mean_full(act, mean)
                fn(stat[:, 0, :], mean_ap(mean), ACT.Square).then_inc(S["m2_ready"], 1)
                act.wait_ge(S["var_ready"], q + 1)
                fn(stat[:, 2, :], stat[:, 1, :], ACT.Sqrt).then_inc(S["std_ready"], 1)
                for j in range(KT):
                    act.wait_ge(S["nz_ready"], q * KT + j + 1)
                    if q < 2:
                        fn(xh[:, j, :], z[:, j, :], ACT.Identity, bias=vec_d(b, l, j)).then_inc(S["x_hi"], 1)
                    else:
                        fn(x[:, j, :], z[:, j, :], ACT.Identity, bias=vec_d(b, l, j)).then_inc(S["norm_ready"], 1)

            def root_table():
                fn(warm[:, :], ones_d[:, 0:1], ACT.Sqrt)

            def mean_full(eng, mean):
                if mean[0] == "tail":
                    eng.wait_ge(*in_visit(bank_full, 0, mean[2], 0))
                else:
                    filled(eng, mean)

            def mean_ap(mean):
                return ps[:, mean[1], 0:T] if mean[0] == "tail" else bank(mean)[:, 0:T]

            act.dma_start(consts[:, :], A["consts"]).then_inc(S["ld_const"], 16)
            for i, name in enumerate(VEC_B):
                act.dma_start(par_rows[i * L:(i + 1) * L, :], A[name]).then_inc(S["ld_par"], 16)
            r = len(VEC_B) * L
            act.dma_start(par_rows[r:r + L * CW, :], A["conv_w"].rearrange("l k n -> (l k) n")).then_inc(S["ld_par"], 16)
            r += L * CW
            act.dma_start(par_rows[r:r + L * LW, :], A["lru_conv_w"].rearrange("l k n -> (l k) n")
                          ).then_inc(S["ld_par"], 16)
            act.dma_start(pard_rows[0:3 * L, :], A["b_gate"].rearrange("l (b n) -> (l b) n", b=3)
                          ).then_inc(S["ld_par"], 16)
            for i, name in enumerate(VEC_D):
                act.dma_start(pard_rows[(3 + i) * L:(4 + i) * L, :], A[name]).then_inc(S["ld_par"], 16)
            for k in range(KT):
                filled(act, ("xT", k))
                fn(x[:, k, :], bank(("xT", k))[:, 0:T], ACT.Copy)
                fn(xh[:, k, :], bank(("xT", k))[:, 0:T], ACT.Copy).then_inc(S["x_hi"], 1)
            hi(0)
            hi(1)
            filled(act, "par512")
            fn(par[:, :, :], bank("par512")[:, 0:C4 * L * NR].rearrange("p (j r) -> p j r", j=C4),
               ACT.Copy).then_inc(free_of("par512"), 1)
            filled(act, "par1024")
            fn(par_d[:, :, :], bank("par1024")[:, 0:KT * L * NQ].rearrange("p (j r) -> p j r", j=KT),
               ACT.Copy).then_inc(free_of("par1024"), 1)
            for n in range(2, AHEAD):
                hi(n)
            read_out(act, "par512")
            read_out(act, "par1024")
            act.wait_ge(S["sp_abs"], 1)
            fn(spt[:, 1], spt[:, 0], ACT.Exp, scale=-1.0).then_inc(S["sp_exp"], 1)

            for l in range(L):
                b0 = mixer_piece(l)
                for s, what in enumerate(IN_ORDER):
                    hi(b0 + 2 * s + AHEAD)
                    hi(b0 + 2 * s + 1 + AHEAD)
                    kind = what[0]
                    if s == 14:
                        root_table()
                    for j in range(4):
                        name = ("mix", l, s, j)
                        o = bank(name)
                        if kind == "glu":
                            filled(act, name)
                            fn(sg[:, j, :], o[:, 0:T], ACT.Sigmoid, scale=1 / WS).then_inc(free_of(name), 1)
                        elif kind == "lru":
                            filled(act, name)
                            if j == 0 and l:
                                act.wait_ge(S["zeroed"], l + 1)
                            fn(ulru[:, j, LW - 1:], o[:, 0:TP], ACT.Copy, scale=1 / WS)
                            fn(lru_s[:, l, j, :, LW - 1], o[:, TP:T], ACT.Copy, scale=1 / WS).then_inc(free_of(name), 1)
                        elif kind == "pool":
                            filled(act, name)
                            fn(upool[:, j, PW - 1:], o[:, 0:TP], ACT.Copy, scale=1 / WS)
                            fn(pool_s[:, l, j, :, PW - 1], o[:, TP:T], ACT.Copy, scale=1 / WS).then_inc(free_of(name), 1)
                        elif kind == "gelu":
                            filled(act, name)
                            fn(gelu[:, j, :], o[:, 0:T], ACT.Gelu_apprx_tanh, scale=1 / WS).then_inc(free_of(name), 1)
                        elif kind == "gate":
                            filled(act, name)
                            turn = {0: 0, 2: 1, 1: 2}[what[2]]
                            d = what[3] * 4 + j
                            if turn == 1:
                                read_out(act, ("mix", l, 7, d))
                            elif turn == 2:
                                act.wait_ge(S["merge_done"], l * KT + d + 1)
                            elif d == 0:
                                act.wait_ge(S["pooled_ready"], (l + 1) * C4)
                            fn(gates[:, d, :], o[:, 0:T], ACT.Sigmoid, bias=gate_bias(l, what[2], d),
                               scale=1 / WS).then_inc(free_of(name), 1)
                    if s == 5:
                        if l:
                            act.wait_ge(S["x_pool"], 2 * KT)
                        for nm, w, out in (("ra", "lru_ba", rt), ("ri", "lru_bx", ig)):
                            for j in range(C4):
                                n = (nm, l, j)
                                filled(act, n)
                                fn(out[:, j, :], bank(n)[:, 0:T], ACT.Sigmoid, bias=vec(w, l, j)).then_inc(free_of(n), 1)
                        filled(act, ("ri", l, C4 - 1))
                        act.wait_ge(S["sp_done"], 1)
                        for j in range(C4):
                            read_out(act, ("ra", l, j))
                            fn(rt[:, j, :], rt[:, j, :], ACT.Tanh, scale=sp4[:, j, l:l + 1]).then_inc(S["tanh_ready"], 1)
                    if s == 6:
                        for j in range(C4):
                            n = ("pm", l, j)
                            filled(act, n)
                            fn(y_pool[:, j, :], bank(n)[:, 0:T], ACT.Copy, scale=vec("pool_scale", l, j))
                            fn(brh[:, j, :], bank(n)[:, 0:T], ACT.Copy, scale=vec("pool_scale", l, j)
                               ).then_inc(free_of(n), 1)
                        act.wait_ge(S["q_ready"], l + 1)
                        fn(rt, rt, ACT.Sqrt).then_inc(S["root_ready"], 1)
                    if s == 8:
                        act.wait_ge(S["hg_ready"], l + 1)
                        piece_done(act, b0 + 15)
                        for j in range(C4):
                            fn(brh[:, j, :], rq[:, j, :], ACT.Copy).then_inc(S["br_hi"], 1)
                    if s == 9:
                        act.wait_ge(S["conv_done"], (l + 1) * C4)
                        fn(conv_sq, conv, ACT.Square).then_inc(S["csq_done"], 1)
                    if s == 11:
                        filled(act, ("cmean", l))
                        fn(stat[:, 0, :], bank(("cmean", l))[:, 0:T], ACT.Square).then_inc(S["cm2_ready"], 1)
                        act.wait_ge(S["cvar_ready"], l + 1)
                        fn(stat[:, 2, :], stat[:, 1, :], ACT.Sqrt).then_inc(S["cstd_ready"], 1)
                        for j in range(C4):
                            act.wait_ge(S["cv_ready"], l * C4 + j + 1)
                            fn(conv_sq[:, j, :], conv[:, j, :], ACT.Silu, bias=vec("conv_ln_b", l, j),
                               scale=vec("conv_ln_g", l, j)).then_inc(S["silu_ready"], 1)
                        for j in range(C4):
                            act.wait_ge(S["silu_ready"], l * C4 + j + 1)
                            fn(brh[:, j, :], conv_sq[:, j, :], ACT.Copy).then_inc(S["br_hi"], 1)
                    if s == 13:
                        for d in range(KT):
                            act.wait_ge(S["mg_ready"], l * KT + d + 1)
                            fn(xh[:, d, :], merged[:, d, :], ACT.Copy).then_inc(S["mg_hi"], 1)
                        n = ("so", l)
                        filled(act, n)
                        if l:
                            act.wait_ge(S["out_dma"], 16 * (3 * L + 8 * l))
                        fn(so_out[0:81, :], bank(n)[0:81, :], ACT.Copy).then_inc(free_of(n), 1)
                    if kind == "out":
                        for j in range(4):
                            d = what[1] * 4 + j
                            read_out(act, ("mix", l, s, j))
                            fn(zsq[:, d, :], z[:, d, :], ACT.Square).then_inc(S["zsq_ready"], 1)
                norm(2 * l, ("mean", 2 * l), l, "ln1_b")
                if l == 0:
                    n = MIX
                    f = 0
                    for g, nf in enumerate(FG):
                        hi(n + AHEAD)
                        hi(n + 1 + AHEAD)
                        for j in range(nf):
                            filled(act, ("fg", g, j))
                            if g:
                                read_out(act, ("fu", g - 1, j))
                            fn(silu_d[:, j, :], bank(("fg", g, j))[:, 0:T], ACT.Silu,
                               scale=1 / WS).then_inc(free_of(("fg", g, j)), 1)
                        hi(n + 2 + AHEAD)
                        hi(n + 3 + AHEAD)
                        for j in range(nf):
                            read_out(act, ("fu", g, j))
                            fn(hdh[:, f + j, :], h_d[:, j, :], ACT.Copy).then_inc(S["f_hi"], 1)
                        n += 4
                        f += nf
                    for half in range(2):
                        for g in range(len(FG)):
                            hi(n + AHEAD)
                            n += 1
                        if half == 0:
                            root_table()
                        for j in range(4 * half, 4 * half + 4):
                            read_out(act, ("fd", j))
                            fn(zsq[:, j, :], z[:, j, :], ACT.Square).then_inc(S["zsq_ready"], 1)
                    norm(1, ("mean", 1), 0, "ln2_b")

            for i in range(3):
                n = P if i < 2 else NS_
                for h in range(2):
                    name = ("xtok", i, h)
                    filled(act, name)
                    if i == 2:
                        act.wait_ge(S["rows_zeroed"], 1)
                    fn(xth[0:n, i, h * 512:(h + 1) * 512], bank(name)[0:n, :], ACT.Copy).then_inc(S["xt_hi"], 1)
            act.wait_ge(S["gd_ready"], 1)
            fn(route1[:, 4, :], route1[:, 3, :], ACT.Sigmoid)
            fn(route1[:, 5, :], route1[:, 3, :], ACT.Sigmoid, scale=-1.0).then_inc(S["gs_ready"], 1)

            def gather_hi(v, wait):
                for h in range(2):
                    wait(act, "gath_hi", h, 6 + h)
                    fn(xgh[:, 4 * h:4 * h + 4, :], ps[:, 6 + h, :].rearrange("p (k c) -> p k c", k=4),
                       ACT.Copy).then_inc(bank_free[6 + h], 1)

            def y_hi(v):
                act.wait_ge(*in_visit(bank_free, 7, v, -2))
                for h in range(2):
                    act.wait_ge(*in_visit(bank_full, 4 + h, v, -1))
                    fn(yh[:, h * 512:(h + 1) * 512], ps[:, 4 + h, :], ACT.Copy,
                       scale=gate_slot[:, 0:1]).then_inc(S["y_hi"], 1)

            gather_hi(0, lambda e, part, h, b: filled(e, (part, h)))
            act.wait_ge(S["visits_ready"], 1)
            nv = act.value_load(visits_i[0:1, 0:1], min_val=NE, max_val=3 * NE)
            def visit_done(m):
                back = 0 if m >= 0 else 1
                m %= VISIT
                kind, c, h = order[m]
                if m in part_in_visit:
                    return S["part_used"], v * NPART + (PART0 - back * NPART + part_in_visit.index(m) + 1)
                b, i = {"g": (c % 2, c // 2), "u": (2 + c % 2, c // 2), "d": (5, 2)}[kind]
                return in_visit(bank_full, b, v, i - back * PER_VISIT[b])

            with act.Fori(0, nv) as v:
                def hi_v(m):
                    n = PRE + m
                    act.wait_ge(stage_full[n % SLOTS], v * (16 * VISIT // SLOTS) + 16 * (n // SLOTS + 1))
                    act.wait_ge(*visit_done(m - SLOTS))
                    fn(w_hi[:, n % SLOTS, :], stage[:, n % SLOTS, :], ACT.Copy, scale=WS).then_inc(S["hi_done"], 1)

                for q, (kind, c, h) in enumerate(order):
                    if q + AHEAD < VISIT:
                        hi_v(q + AHEAD)
                    else:
                        with act.If(v < nv - 1):
                            hi_v(q + AHEAD)
                    if q == 0:
                        y_hi(v)
                    if q and order[q - 1] == ("g", order[q - 1][1], 1):
                        c, b = order[q - 1][1], order[q - 1][1] % 2
                        act.wait_ge(*in_visit(bank_full, b, v, c // 2))
                        fn(silu_e[:, b, :], ps[:, b, :], ACT.Silu, scale=1 / WS).then_inc(bank_free[b], 1)
                    if q > 1 and order[q - 2] == ("u", order[q - 2][1], 1):
                        c, b = order[q - 2][1], order[q - 2][1] % 2
                        act.wait_ge(*in_visit(bank_free, 2 + b, v, c // 2))
                        fn(hh[:, b, :], h_e[:, b, :], ACT.Copy).then_inc(S["e_hi"], 1)
                    if q == GATHER_AT:
                        gather_hi(v + 1, lambda e, part, hf, bk: e.wait_ge(
                            *in_visit(bank_full, bk, v, PER_VISIT[bk] - 1)))
            y_hi(nv)
            root_table()
            for j in range(KT):
                act.wait_ge(*in_visit(bank_free, 4 + j % 4, nv, j // 4))
                fn(zsq[:, j, :], z[:, j, :], ACT.Square).then_inc(S["zsq_ready"], 1)
            norm(3, ("tail", 0, nv), 1, "ln2_b")
            for i in range(3):
                n = P if i < 2 else NS_
                for h in range(2):
                    b = 2 + h
                    act.wait_ge(*in_visit(bank_full, b, nv, i))
                    fn(y_rows[0:n, i, h * 512:(h + 1) * 512], ps[0:n, b, :], ACT.Copy).then_inc(bank_free[b], 1)
                for b in (2, 3):
                    act.wait_ge(*in_visit(bank_free, b, nv, i))
                dst = (O["y_prompt"][0, i * P:(i + 1) * P, :] if i < 2 else O["y_sample"].rearrange("b s n -> (b s) n"))
                act.dma_start(dst, y_rows[0:n, i, :]).then_inc(S["y_out"], 16)
        @block.vector
        def _(dve):
            V = nc.vector
            own = Steps(dve, S["dve"])

            def lo(n):
                tiles, width = pre_piece(n)[1:]
                sl = n % SLOTS
                dve.wait_ge(S["hi_done"], n + 1)
                V.scalar_tensor_tensor(w_lo[:, sl, 0:tiles * width], stage[:, sl, 0:tiles * width], WS,
                                       w_hi[:, sl, 0:tiles * width], ALU.mult, ALU.subtract).then_inc(S["lo_done"], 1)

            def norm(q, mean, msq, scale, l, g, bias):
                if mean[0] == "tail":
                    waits = [in_visit(bank_full, b, mean[2], 0) for b in (0, 1)]
                    read = [in_visit(bank_free, b, mean[2], 0) for b in (0, 1)]
                    mu, sq = ps[:, 0, 0:T], ps[:, 1, 0:T]
                else:
                    waits = [(full_of(n), place[n][1] + 1) for n in (mean, msq)]
                    read = [(free_of(n), place[n][1] + 1) for n in (mean, msq)]
                    mu, sq = bank(mean)[:, 0:T], bank(msq)[:, 0:T]
                for w in waits:
                    dve.wait_ge(*w)
                dve.wait_ge(S["m2_ready"], q + 1)
                V.tensor_tensor(stat[:, 1, :], sq, stat[:, 0, :], ALU.subtract).then_inc(read[1][0], 1)
                dve.wait_ge(*read[1])
                V.tensor_scalar(stat[:, 1, :], stat[:, 1, :], 0.0, EPS * scale * scale, ALU.max,
                                ALU.add).then_inc(S["var_ready"], 1)
                for j in range(KT):
                    t = V.tensor_tensor(z[:, j, :], z[:, j, :], mu, ALU.subtract)
                t.then_inc(read[0][0], 1)
                dve.wait_ge(S["std_ready"], q + 1)
                own.then(V.reciprocal(stat[:, 0, :], stat[:, 2, :]))
                dve.wait_ge(*read[0])
                for j in range(KT):
                    V.scalar_tensor_tensor(z[:, j, :], z[:, j, :], vec_d(g, l, j), stat[:, 0, :], ALU.mult,
                                           ALU.mult).then_inc(S["nz_ready"], 1)
                    if q < 2 and j:
                        x_lo(q, l, bias, j - 1)
                if q < 2:
                    x_lo(q, l, bias, KT - 1)

            def x_lo(q, l, bias, j):
                dve.wait_ge(S["x_hi"], (q + 1) * KT + j + 1)
                V.scalar_tensor_tensor(xl[:, j, :], z[:, j, :], vec_d(bias, l, j), xh[:, j, :], ALU.add,
                                       ALU.subtract).then_inc(S["x_split"], 1)

            V.memset(ones_d[:], 1.0 / D)
            own.did(V.memset(ones_b[:], 1.0 / DB))
            for k in range(KT):
                n = ("xT", k)
                dve.wait_ge(S["x_hi"], k + 1)
                V.tensor_tensor(xl[:, k, :], bank(n)[:, 0:T], xh[:, k, :], ALU.subtract).then_inc(free_of(n), 1)
            lo(0)
            lo(1)
            for l in range(L):
                for h in range(2):
                    n = ("st_conv", l, h)
                    filled(dve, n)
                    for j in range(C4):
                        r = 4 * (CW - 1)
                        t = V.tensor_copy(win_s[:, l, j, 4 * h:4 * h + 4, 0:CW - 1],
                                          bank(n)[:, j * r:(j + 1) * r].rearrange("p (b r) -> p b r", b=4))
                    t.then_inc(free_of(n), 1)
                n = ("st_pool", l)
                filled(dve, n)
                for j in range(C4):
                    r = NS_ * (PW - 1)
                    t = V.tensor_copy(pool_s[:, l, j, :, 0:PW - 1],
                                      bank(n)[:, j * r:(j + 1) * r].rearrange("p (b r) -> p b r", b=NS_))
                t.then_inc(free_of(n), 1)
                n = ("st_lru", l)
                filled(dve, n)
                for j in range(C4):
                    V.tensor_copy(lru_s[:, l, j, :, 0:LW - 1],
                                  bank(n)[:, j * 32:j * 32 + 24].rearrange("p (b r) -> p b r", b=NS_))
                t = V.tensor_copy(h0_s[:, l, :, :],
                                  bank(n)[:, 0:P].rearrange("p (j r) -> p j r", j=C4)[:, :, 24:32])
                t.then_inc(free_of(n), 1)
            for n in range(2, AHEAD):
                lo(n)
            dve.wait_ge(S["ld_const"], 16)
            own.did(V.tensor_copy(ident16[:, :], ident))
            r = VEC_B.index("lru_lambda") * L
            lam = par[:, :, r:r + L]
            read_out(dve, "par512")
            read_out(dve, "par1024")
            V.scalar_tensor_tensor(spt[:, 0], lam, -1.0, lam, ALU.mult, ALU.max).then_inc(S["sp_abs"], 1)
            dve.wait_ge(S["sp_exp"], 1)
            own.then(V.tensor_scalar(spt[:, 2], spt[:, 1], 2.0, None, ALU.add))
            own.then(V.reciprocal(spt[:, 3], spt[:, 2]))
            own.then(V.tensor_tensor(spt[:, 2], spt[:, 1], spt[:, 3], ALU.mult))
            own.then(V.tensor_tensor(spt[:, 3], spt[:, 2], spt[:, 2], ALU.mult))
            own.then(V.tensor_scalar(spt[:, 4], spt[:, 3], 1.0 / 15, 1.0 / 13, ALU.mult, ALU.add))
            for k in (11, 9, 7, 5, 3, 1):
                own.then(V.tensor_tensor(spt[:, 4], spt[:, 4], spt[:, 3], ALU.mult))
                own.then(V.tensor_scalar(spt[:, 4], spt[:, 4], 1.0 / k, None, ALU.add))
            own.then(V.tensor_tensor(spt[:, 4], spt[:, 4], spt[:, 2], ALU.mult))
            own.then(V.tensor_scalar(spt[:, 5], lam, -1.0, 0.0, ALU.mult, ALU.max))
            own.then(V.scalar_tensor_tensor(spt[:, 3], spt[:, 4], 2.0, spt[:, 5], ALU.mult, ALU.add))
            V.tensor_scalar(sp4[:, :, :], spt[:, 3], 4.0, None, ALU.mult).then_inc(S["sp_done"], 1)

            for l in range(L):
                b0 = mixer_piece(l)
                tap_at = [0] * C4

                def conv_taps(k0, k1):
                    for k in range(k0, k1):
                        for j in range(C4):
                            w = conv_tap(l, j, k)
                            src = glu[:, j, k:k + TP]
                            if k == 0:
                                i = V.tensor_scalar(conv[:, j, 0:TP], src, w, vec("conv_b", l, j), ALU.mult, ALU.add)
                            else:
                                own.after(tap_at[j])
                                i = V.scalar_tensor_tensor(conv[:, j, 0:TP], src, w, conv[:, j, 0:TP],
                                                           ALU.mult, ALU.add)
                            tap_at[j] = own.did(i)

                def window_conv(win, taps, width, out, bias, done):
                    for j in range(C4):
                        w = taps(l, j, 0, width).unsqueeze(1).to_broadcast([P, NS_, width])
                        own.then(V.tensor_tensor(prod[:, :, 0:width], win[:, l, j, :, :], w, ALU.mult))
                        own.then(V.tensor_reduce(out[:, j, TP:T], prod[:, :, 0:width], X, ALU.add))
                        V.tensor_scalar(out[:, j, TP:T], out[:, j, TP:T], vec(bias, l, j), None,
                                        ALU.add).then_inc(S[done], 1)

                def merge(s, done):
                    for d in range(KT):
                        name = ("mix", l, s, d)
                        read_out(dve, ("mix", l, s - 2 + d // 4, d % 4))
                        filled(dve, name)
                        out = gates if done else merged
                        V.scalar_tensor_tensor(out[:, d, :], bank(name)[:, 0:T], 1 / WS, gates[:, d, :], ALU.mult,
                                               ALU.mult).then_inc(free_of(name), 1)
                        if done and d:
                            merge_sum(s, d - 1, done)
                    if done:
                        merge_sum(s, KT - 1, done)

                def merge_sum(s, d, done):
                    read_out(dve, ("mix", l, s, d))
                    V.tensor_tensor(merged[:, d, :], merged[:, d, :], gates[:, d, :], ALU.add).then_inc(S[done], 1)

                if l:
                    dve.wait_ge(S["packed"], 8 * l)
                V.memset(glu[:, :, 0:CW - 1], 0.0)
                V.memset(upool[:, :, 0:PW - 1], 0.0)
                V.memset(ulru[:, :, 0:LW - 1], 0.0).then_inc(S["zeroed"], 1)

                for s, what in enumerate(IN_ORDER):
                    lo(b0 + 2 * s + AHEAD)
                    lo(b0 + 2 * s + 1 + AHEAD)
                    kind = what[0]
                    if kind == "val":
                        for j in range(4):
                            name = ("mix", l, s, j)
                            gl = ("mix", l, 0, j)
                            read_out(dve, gl)
                            filled(dve, name)
                            o = bank(name)
                            V.scalar_tensor_tensor(glu[:, j, CW - 1:], o[:, 0:TP], 1 / WS, sg[:, j, 0:TP], ALU.mult,
                                                   ALU.mult)
                            V.scalar_tensor_tensor(win_s[:, l, j, :, CW - 1], o[:, TP:T], 1 / WS, sg[:, j, TP:T],
                                                   ALU.mult, ALU.mult).then_inc(free_of(name), 1)
                        for j in range(4):
                            read_out(dve, ("mix", l, s, j))
                    if s == 2:
                        dve.wait_ge(S["zeroed"], l + 1)
                        for k in range(LW):
                            for j in range(C4):
                                src = ulru[:, j, k:k + TP]
                                if k == 0:
                                    read_out(dve, ("mix", l, s, j))
                                    i = V.tensor_scalar(xc[:, j, 0:TP], src, lru_tap(l, j, k), vec("lru_conv_b", l, j),
                                                        ALU.mult, ALU.add)
                                else:
                                    own.after(tap_at[j])
                                    i = V.scalar_tensor_tensor(xc[:, j, 0:TP], src, lru_tap(l, j, k),
                                                               xc[:, j, 0:TP], ALU.mult, ALU.add)
                                tap_at[j] = own.did(i)
                        window_conv(lru_s, lru_tap, LW, xc, "lru_conv_b", "xc_ready")
                        conv_taps(0, 3)
                    if s == 3:
                        conv_taps(3, 10)
                    if s == 4:
                        if l:
                            dve.wait_ge(S["x_pool"], 2 * KT)
                        for j in range(C4):
                            read_out(dve, ("mix", l, 3, j))
                            src, w = upool[:, j, :], 1
                            E_ = PW - 1 + TP
                            while w < WINDOWS[j]:
                                dst = wsum[:, (w.bit_length() - 1) % 2, :]
                                lo_ = 2 * w - 1
                                own.then(V.tensor_tensor(dst[:, lo_:E_], src[:, lo_:E_], src[:, lo_ - w:E_ - w],
                                                         ALU.add))
                                src, w = dst, 2 * w
                            own.then(V.scalar_tensor_tensor(pooled[:, j, 0:TP], src[:, PW - 1:], 1.0 / w,
                                                            upool[:, j, PW - 1:], ALU.mult, ALU.subtract))
                            o2 = wsum[:, w.bit_length() % 2, 0:PW]
                            own.then(V.tensor_tensor(o2, src[:, PW - 1:2 * PW - 1], inv_cnt[:, j, :], ALU.mult))
                            own.then(V.tensor_tensor(pooled[:, j, 0:PW], o2, upool[:, j, PW - 1:2 * PW - 1],
                                                     ALU.subtract))
                            own.then(V.tensor_reduce(pooled[:, j, TP:T], pool_s[:, l, j, :, PW - w:PW], X, ALU.add))
                            V.scalar_tensor_tensor(pooled[:, j, TP:T], pooled[:, j, TP:T], 1.0 / w,
                                                   pool_s[:, l, j, :, PW - 1], ALU.mult,
                                                   ALU.subtract).then_inc(S["pooled_ready"], 1)
                        conv_taps(10, 13)
                    if s == 5:
                        conv_taps(13, 19)
                    if s == 6:
                        for j in range(C4):
                            read_out(dve, ("pm", l, j))
                            V.tensor_tensor(brl[:, j, :], y_pool[:, j, :], brh[:, j, :],
                                            ALU.subtract).then_inc(S["br_ready"], 1)
                        dve.wait_ge(S["tanh_ready"], (l + 1) * C4)
                        dve.wait_ge(S["packed"], 8 * l + 4)
                        own.then(V.tensor_scalar(rq, rt, 1.0, None, ALU.add))
                        n = own.did(V.reciprocal(rq, rq))
                        own.after(n)
                        V.tensor_scalar(a_lru, rq, 2.0, -1.0, ALU.mult, ALU.add).then_inc(S["q_ready"], 1)
                        dve.wait_ge(S["q_ready"], l + 1)
                        own.did(V.memset(a_lru[:, :, 0:1], 0.0))
                        own.then(V.tensor_tensor(ig, ig, xc, ALU.mult))
                        dve.wait_ge(S["root_ready"], l + 1)
                        own.then(V.tensor_tensor(rq, rq, rt, ALU.mult))
                        own.then(V.memset(rq[:, :, 0:1], 0.5))
                        own.then(V.scalar_tensor_tensor(ig, ig, 2.0, rq, ALU.mult, ALU.mult))
                    if s == 7:
                        merge(s, None)
                        dve.wait_ge(S["packed"], 8 * l + 6)
                        for j in range(C4):
                            V.tensor_tensor_scan(hseq[:, j, 0:TP], a_lru[:, j, 0:TP], ig[:, j, 0:TP], 0.0, ALU.mult,
                                                 ALU.add)
                        own.then(V.tensor_tensor(a_lru[:, :, TP:T], a_lru[:, :, TP:T], h0_s[:, l, :, :], ALU.mult))
                        V.tensor_tensor(hseq[:, :, TP:T], a_lru[:, :, TP:T], ig[:, :, TP:T],
                                        ALU.add).then_inc(S["h_ready"], 1)
                        dve.wait_ge(S["h_ready"], l + 1)
                        for j in range(C4):
                            read_out(dve, ("mix", l, 4, j))
                        V.tensor_tensor(rq, hseq, gelu, ALU.mult).then_inc(S["hg_ready"], 1)
                        conv_taps(19, 23)
                    if s == 8:
                        for j in range(C4):
                            dve.wait_ge(S["br_hi"], 2 * l * C4 + j + 1)
                            V.tensor_tensor(brl[:, j, :], rq[:, j, :], brh[:, j, :],
                                            ALU.subtract).then_inc(S["br_ready"], 1)
                        conv_taps(23, 28)
                    if s == 9:
                        conv_taps(28, CW)
                        window_conv(win_s, conv_tap, CW, conv, "conv_b", "conv_done")
                    if s == 10:
                        merge(s, "merge_done")
                    if s == 11:
                        filled(dve, ("cmean", l))
                        filled(dve, ("csq", l))
                        dve.wait_ge(S["cm2_ready"], l + 1)
                        mu = bank(("cmean", l))[:, 0:T]
                        V.tensor_tensor(stat[:, 1, :], bank(("csq", l))[:, 0:T], stat[:, 0, :],
                                        ALU.subtract).then_inc(free_of(("csq", l)), 1)
                        read_out(dve, ("csq", l))
                        V.tensor_scalar(stat[:, 1, :], stat[:, 1, :], 0.0, EPS, ALU.max, ALU.add
                                        ).then_inc(S["cvar_ready"], 1)
                        for j in range(C4):
                            t = V.tensor_tensor(conv[:, j, :], conv[:, j, :], mu, ALU.subtract)
                        t.then_inc(free_of(("cmean", l)), 1)
                        dve.wait_ge(S["cstd_ready"], l + 1)
                        read_out(dve, ("cmean", l))
                        own.then(V.reciprocal(stat[:, 0, :], stat[:, 2, :]))
                        for j in range(C4):
                            V.tensor_tensor(conv[:, j, :], conv[:, j, :], stat[:, 0, :],
                                            ALU.mult).then_inc(S["cv_ready"], 1)
                        for j in range(C4):
                            dve.wait_ge(S["br_hi"], (2 * l + 1) * C4 + j + 1)
                            V.tensor_tensor(brl[:, j, :], conv_sq[:, j, :], brh[:, j, :],
                                            ALU.subtract).then_inc(S["br_ready"], 1)
                    if s == 13:
                        merge(s, "mg_ready")
                        for d in range(KT):
                            dve.wait_ge(S["mg_hi"], l * KT + d + 1)
                            V.tensor_tensor(xl[:, d, :], merged[:, d, :], xh[:, d, :],
                                            ALU.subtract).then_inc(S["mg_split"], 1)
                    if kind == "out":
                        for j in range(4):
                            name = ("mix", l, s, j)
                            d = what[1] * 4 + j
                            filled(dve, name)
                            if l:
                                dve.wait_ge(S["x_pool"], KT + d + 1)
                            V.scalar_tensor_tensor(z[:, d, :], x[:, d, :], WS * ALPHA, bank(name)[:, 0:T], ALU.mult,
                                                   ALU.add).then_inc(free_of(name), 1)
                norm(2 * l, ("mean", 2 * l), ("msq", 2 * l), WS, l, "ln1_g", "ln1_b")
                if l == 0:
                    n = MIX
                    f = 0
                    for g, nf in enumerate(FG):
                        for i in range(4):
                            lo(n + i + AHEAD)
                        for j in range(nf):
                            fg, fu = ("fg", g, j), ("fu", g, j)
                            read_out(dve, fg)
                            if g:
                                dve.wait_ge(S["f_split"], f - 4 + j + 1)
                            filled(dve, fu)
                            V.scalar_tensor_tensor(h_d[:, j, :], bank(fu)[:, 0:T], 1 / WS, silu_d[:, j, :], ALU.mult,
                                                   ALU.mult).then_inc(free_of(fu), 1)
                        for j in range(nf):
                            dve.wait_ge(S["f_hi"], f + j + 1)
                            V.tensor_tensor(hdl[:, f + j, :], h_d[:, j, :], hdh[:, f + j, :],
                                            ALU.subtract).then_inc(S["f_split"], 1)
                        n += 4
                        f += nf
                    for half in range(2):
                        for g in range(len(FG)):
                            lo(n + AHEAD)
                            n += 1
                        for j in range(4 * half, 4 * half + 4):
                            name = ("fd", j)
                            filled(dve, name)
                            dve.wait_ge(S["x_pool"], j + 1)
                            V.scalar_tensor_tensor(z[:, j, :], x[:, j, :], WS * ALPHA, bank(name)[:, 0:T], ALU.mult,
                                                   ALU.add).then_inc(free_of(name), 1)
                    norm(1, ("mean", 1), ("msq", 1), WS, 0, "ln2_g", "ln2_b")

            own.did(V.memset(yh[:, :], 0.0))
            own.did(V.memset(yl[:, :], 0.0))
            own.did(V.memset(onehot_t, 0.0))
            own.did(V.memset(gate_slot[:, :], 0.0))
            own.did(V.memset(xtl[:, 2, :], 0.0))
            V.memset(xth[:, 2, :], 0.0).then_inc(S["rows_zeroed"], 1)
            V.memset(gsel[:, :, :], 0.0).then_inc(S["e_split"], 1)
            lg = route[:, 1]
            own.then(V.memset(lg, 0.0))
            filled(dve, "logits")
            own.did(V.tensor_copy(lg[:, 0:2, :], bank("logits")[:, 0:2 * NE].rearrange("p (i e) -> p i e", i=2)))
            V.tensor_copy(lg[0:NS_, 2, :], bank("logits")[0:NS_, 2 * NE:3 * NE]).then_inc(free_of("logits"), 1)
            read_out(dve, "logits")
            big = [P, 3, NE]

            def largest(src, sel, m):
                own.then(V.tensor_reduce(m, src, X, ALU.max))
                own.then(V.tensor_tensor(route[:, 8], src, m.unsqueeze(2).to_broadcast(big), ALU.is_equal))
                own.then(V.tensor_tensor(route[:, 8], route[:, 8], idx_w.unsqueeze(1).to_broadcast(big), ALU.mult))
                own.then(V.tensor_reduce(route1[:, 7, :], route[:, 8], X, ALU.max))
                own.then(V.tensor_tensor(sel, route[:, 8], route1[:, 7, :].unsqueeze(2).to_broadcast(big),
                                         ALU.is_equal))

            largest(lg, route[:, 2], route1[:, 0, :])
            own.then(V.scalar_tensor_tensor(route[:, 3], route[:, 2], -1e30, lg, ALU.mult, ALU.add))
            largest(route[:, 3], route[:, 4], route1[:, 1, :])
            V.tensor_tensor(route[:, 0], route[:, 2], route[:, 4], ALU.add).then_inc(S["mask_ready"], 1)
            V.tensor_tensor(route1[:, 3, :], route1[:, 0, :], route1[:, 1, :], ALU.subtract).then_inc(S["gd_ready"], 1)
            dve.wait_ge(S["gs_ready"], 1)
            own.then(V.tensor_tensor(route[:, 5], route[:, 2], route1[:, 4, :].unsqueeze(2).to_broadcast(big), ALU.mult))
            own.then(V.tensor_tensor(route[:, 6], route[:, 4], route1[:, 5, :].unsqueeze(2).to_broadcast(big), ALU.mult))
            own.then(V.tensor_tensor(route[:, 7], route[:, 5], route[:, 6], ALU.add))
            own.then(V.tensor_copy(gate_split[:, :, :, 0], route[:, 7]))
            own.did(V.tensor_tensor(gate_split[:, :, :, 1], route[:, 7], gate_split[:, :, :, 0], ALU.subtract))
            dve.wait_ge(S["mask_ready"], 1)
            own.then(V.memset(rank[:, :, :], -1.0))
            filled(dve, "ranks")
            rk = bank("ranks")
            own.did(V.tensor_tensor(route[:, 9, 0:2, :], rk[:, 0:2 * NE].rearrange("p (i e) -> p i e", i=2),
                                    route[:, 0, 0:2, :], ALU.mult))
            own.then(V.tensor_tensor(route[0:NS_, 9, 2, :], rk[0:NS_, 2 * NE:3 * NE], route[0:NS_, 0, 2, :], ALU.mult))
            own.did(V.tensor_scalar(rank[:, 0:2, :], route[:, 9, 0:2, :], float(D), 1.0, ALU.mult, ALU.subtract))
            own.then(V.tensor_scalar(rank[0:NS_, 2, :], route[0:NS_, 9, 2, :], float(D), 1.0, ALU.mult, ALU.subtract))
            V.tensor_reduce(route1[:, 6, 0:1], rk[:, 3 * NE:4 * NE], X, ALU.max).then_inc(free_of("ranks"), 1)
            read_out(dve, "ranks")
            own.then(V.tensor_scalar(route1[:, 6, 1:2], route1[:, 6, 0:1], CAP / D, float(NE), ALU.is_gt, ALU.mult))
            own.then(V.tensor_scalar(route1[:, 6, 2:3], route1[:, 6, 0:1], 2 * CAP / D, float(NE), ALU.is_gt,
                                     ALU.mult))
            own.then(V.tensor_tensor(route1[:, 6, 1:2], route1[:, 6, 1:2], route1[:, 6, 2:3], ALU.add))
            V.tensor_scalar(visits_i[:, :], route1[:, 6, 1:2], float(NE), None, ALU.add).then_inc(S["visits_ready"], 1)
            for i in range(3):
                n = P if i < 2 else NS_
                for h in range(2):
                    name = ("xtok", i, h)
                    q = 2 * i + h + 1
                    dve.wait_ge(S["xt_hi"], q)
                    V.tensor_tensor(xtl[0:n, i, h * 512:(h + 1) * 512], bank(name)[0:n, :],
                                    xth[0:n, i, h * 512:(h + 1) * 512], ALU.subtract).then_inc(free_of(name), 1)

            def select(v, col):
                dve.wait_ge(S["rank_next"], v)
                for i in range(3):
                    V.tensor_scalar(onehot[:, i, :], iota, rank[:, i, col], None, ALU.is_equal)
                t = V.tensor_copy(gsel, gate_split[:, :, col, :])
                t.then_inc(S["onehot_ready"], 1)
                dve.wait_ge(S["onehot_ready"], v + 1)
                V.tensor_scalar(rank[:, :, col], rank[:, :, col], float(CAP), None, ALU.subtract
                                ).then_inc(S["rank_next"], 1)

            def gather_lo(wait):
                for h in range(2):
                    b = 1 + 2 * h
                    wait(dve, "gath_lo", h, b)
                    V.tensor_copy(xgl[:, 4 * h:4 * h + 4, :], ps[:, b, :].rearrange("p (k c) -> p k c", k=4)
                                  ).then_inc(bank_free[b], 1)

            def y_lo(v):
                for h in range(2):
                    dve.wait_ge(S["y_hi"], 2 * v + (h + 1))
                    V.scalar_tensor_tensor(yl[:, h * 512:(h + 1) * 512], ps[:, 4 + h, :], gate_slot[:, 0:1],
                                           yh[:, h * 512:(h + 1) * 512], ALU.mult, ALU.subtract
                                           ).then_inc(bank_free[4 + h], 1)

            select(0, slice(0, 1))
            dve.wait_ge(S["norm_ready"], KT)
            for j in range(KT):
                n = own.did(V.tensor_scalar(z[:, j, :], x[:, j, :], WS * ALPHA, None, ALU.mult))
            for h in range(2):
                empty(dve, ("y_init", h))
                V.memset(ps[:, 4 + h, :], 0.0).then_inc(bank_full[4 + h], 1)
            own.after(n)
            gather_lo(lambda e, part, h, b: filled(e, (part, h)))
            nv = dve.value_load(visits_i[0:1, 0:1], min_val=NE, max_val=3 * NE)

            def scatter_add(v, batch):
                for b in range(4, 8):
                    d = 4 * batch + b - 4
                    dve.wait_ge(*in_visit(bank_full, b, v, batch))
                    V.tensor_tensor(z[:, d, :], z[:, d, :], ps[:, b, 0:T], ALU.add).then_inc(bank_free[b], 1)

            with dve.Fori(0, nv) as v:
                def lo_v(m):
                    n = PRE + m
                    dve.wait_ge(S["hi_done"], v * VISIT + (n + 1))
                    V.scalar_tensor_tensor(w_lo[:, n % SLOTS, :], stage[:, n % SLOTS, :], WS, w_hi[:, n % SLOTS, :],
                                           ALU.mult, ALU.subtract).then_inc(S["lo_done"], 1)

                for q in range(VISIT):
                    if q + AHEAD < VISIT:
                        lo_v(q + AHEAD)
                    else:
                        with dve.If(v < nv - 1):
                            lo_v(q + AHEAD)
                    if q == 0:
                        y_lo(v)
                    kind, c, h = order[q - 1] if q else ("", 0, 0)
                    if (kind, h) == ("u", 1):
                        b = 2 + c % 2
                        dve.wait_ge(*in_visit(bank_free, b - 2, v, c // 2))
                        dve.wait_ge(*in_visit(bank_full, b, v, c // 2))
                        dve.wait_ge(S["e_split"], v * NC + max(c, 1))
                        V.scalar_tensor_tensor(h_e[:, c % 2, :], ps[:, b, :], 1 / WS, silu_e[:, c % 2, :], ALU.mult,
                                               ALU.mult).then_inc(bank_free[b], 1)
                        if c == 0:
                            scatter_add(v, 0)
                        if c == 1:
                            dve.wait_ge(*in_visit(bank_full, 7, v, 2))
                            V.tensor_copy(onehot_t, ps[:, 7, :].bitcast(F16)[:, 0:T])
                            V.tensor_reduce(gate_slot[:, 0:1], ps[:, 7, 256:258], X, ALU.add
                                            ).then_inc(bank_free[7], 1)
                    if (kind, c, h) == ("g", 1, 1):
                        scatter_add(v, 1)
                    if (kind, c, h) == ("d", 3, 0):
                        select(v + 1, bass.ds((v + 1) % NE, 1))
                    kind, c, h = order[q - 2] if q > 1 else ("", 0, 0)
                    if (kind, h) == ("u", 1):
                        dve.wait_ge(S["e_hi"], v * NC + (c + 1))
                        V.tensor_tensor(hl[:, c % 2, :], h_e[:, c % 2, :], hh[:, c % 2, :],
                                        ALU.subtract).then_inc(S["e_split"], 1)
                    if q == GATHER_AT:
                        gather_lo(lambda e, part, hf, bk: e.wait_ge(
                            *in_visit(bank_full, bk, v, PER_VISIT[bk] - 1)))
            y_lo(nv)
            scatter_add(nv, 0)
            scatter_add(nv, 1)
            norm(3, ("tail", 0, nv), None, WS, 1, "ln2_g", "ln2_b")


def constants():
    import numpy as np

    c = np.zeros((P, C_ALL), np.float32)
    c[:, C_ID:C_ID + P] = np.eye(P)
    c[:, C_IO:C_IO + CAP] = np.arange(CAP)
    c[:, C_TR:C_TR + P] = np.triu(np.ones((P, P))) / D
    for g, w in enumerate(WINDOWS):
        c[:, C_IC + g * PW:C_IC + (g + 1) * PW] = 1.0 / np.minimum(w, np.arange(PW) + 1)
    c[:, C_IX:C_IX + NE] = NE - np.arange(NE)
    return c


_INS = ["x_prompt", "x_sample", "state_pool", "state_conv", "state_lru_conv", "state_lru_h", "w_in", "b_gate",
        "w_pool", "pool_scale", "conv_w", "conv_b", "conv_ln_g", "conv_ln_b", "lru_conv_w", "lru_conv_b", "lru_wa",
        "lru_ba", "lru_wx", "lru_bx", "lru_lambda", "w_br_pool", "w_br_conv", "w_br_lru", "w_out", "ln1_g", "ln1_b",
        "ln2_g", "ln2_b", "ffn_w_gate", "ffn_w_up", "ffn_w_down", "moe_router", "moe_w_gate", "moe_w_up",
        "moe_w_down"]
_OUTS = {"y_prompt": (1, TP, D), "y_sample": (NS_, 1, D), "pool_p": (L, 1, PW - 1, DB), "conv_p": (L, 1, CW - 1, DB),
         "lconv_p": (L, 1, LW - 1, DB), "h_p": (L, 1, DB), "pool_s": (L, NS_, PW - 1, DB),
         "conv_s": (L, NS_, CW - 1, DB), "lconv_s": (L, NS_, LW - 1, DB), "h_s": (L, NS_, DB)}


def kernel(**inputs):
    import numpy as np
    import concourse.bacc as bacc
    from concourse.bass_utils import run_bass_kernel_spmd

    nc = bacc.Bacc("TRN2", target_bir_lowering=False, num_devices=1)
    arrays, ins, outs = {}, {}, {}
    for name in _INS:
        arrays[f"in_{name}"] = np.ascontiguousarray(inputs[name])
        ins[name] = nc.dram_tensor(f"in_{name}", arrays[f"in_{name}"].shape, F32, kind="ExternalInput").ap()
    arrays["in_consts"] = constants()
    ins["consts"] = nc.dram_tensor("in_consts", (P, C_ALL), F32, kind="ExternalInput").ap()
    for name, shape in _OUTS.items():
        outs[name] = nc.dram_tensor(f"out_{name}", shape, F32, kind="ExternalOutput").ap()
    trunk_kernel(nc, ins, outs)
    r = run_bass_kernel_spmd(nc, [arrays], core_ids=[0])
    return tuple(r.results[0][f"out_{name}"] for name in _OUTS)
```

```python
from contextlib import ExitStack

import concourse.bass as bass
from concourse import mybir

P = 128
D = 1024
KT = D // P
TP, NS_ = 256, 8
T = TP + NS_
L = 2
C4 = 4
DB = C4 * P
CW, LW, PW = 31, 4, 16
WINDOWS = (2, 4, 8, 16)
D_FF, D_EX, NE = 2816, 3584, 8
ALPHA = (2.0 * L) ** 0.25
EPS = 1e-5
WS = 64.0
CAP = 128
SLOTS = 6
PIECE = 2048
TAPS_AT = [(0, 0), (0, 2), (2, 3), (3, 8), (8, 13), (13, 17), (17, 18), (18, 18), (18, 22), (22, 27), (27, 31)] + [(0, 0)] * 5
AHEAD = 5

F32 = mybir.dt.float32
F16 = mybir.dt.float16
I32 = mybir.dt.int32
ALU = mybir.AluOpType
ACT = mybir.ActivationFunctionType
X = mybir.AxisListType.X

VEC_B = ["pool_scale", "conv_b", "conv_ln_g", "conv_ln_b", "lru_conv_b", "lru_ba", "lru_bx", "lru_lambda"]
NR = len(VEC_B) + CW + LW
VEC_D = ["ln1_g", "ln1_b", "ln2_g", "ln2_b"]
NQ = 3 + len(VEC_D)
C_ID, C_IO, C_TR, C_IC, C_IX, C_ALL = 0, P, P + CAP, 2 * P + CAP, 2 * P + CAP + 64, 2 * P + CAP + 72

IN_ORDER = [("glu", 2), ("val", 1), ("lru", 3), ("pool", 0), ("gelu", 4),
            ("gate", 5, 0, 0), ("gate", 6, 0, 1), ("branch", 0),
            ("gate", 9, 2, 0), ("gate", 10, 2, 1), ("branch", 2),
            ("gate", 7, 1, 0), ("gate", 8, 1, 1), ("branch", 1), ("out", 0), ("out", 1)]
MIX = 2 * len(IN_ORDER)
NF = D_FF // P
FG = [4] * (NF // 4) + ([NF % 4] if NF % 4 else [])
FFN = 4 * len(FG) + 2 * len(FG)
PRE = 2 * MIX + FFN
NC = D_EX // 512
VISIT = 6 * NC
assert VISIT % SLOTS == 0


def visit_order():
    order = []
    for c in range(NC):
        order += [(kind, c, h) for kind in "gu" for h in range(2)]
        if c:
            order += [("d", c - 1, h) for h in range(2)]
    return order + [("d", NC - 1, h) for h in range(2)]


def mixer_piece(l):
    return l * (MIX + FFN)


def psum_plan():
    used = [0] * 8
    place = {}
    turn = [0]

    def put(name, bank=None):
        if bank is None:
            bank = turn[0] % 8
            turn[0] += 1
        place[name] = (bank, used[bank])
        used[bank] += 1

    for k in range(KT):
        put(("xT", k))
    for l in range(L):
        for s, what in enumerate(IN_ORDER):
            if what[0] == "branch":
                for j in range(KT):
                    put(("mix", l, s, j))
            elif what[0] == "out":
                for j in range(4):
                    put(("mix", l, s, j))
                if what[1] == 1:
                    put(("mean", 2 * l))
                    put(("msq", 2 * l))
            else:
                for j in range(4):
                    put(("mix", l, s, j))
            if l == 0 and s == 0:
                put("par512")
                put("par1024")
            if l == 0 and s == 1:
                for l_ in range(L):
                    for h in range(2):
                        put(("st_conv", l_, h))
                    put(("st_pool", l_))
                    put(("st_lru", l_))
            if s == 4:
                for j in range(C4):
                    put(("ra", l, j))
            if s == 5:
                for j in range(C4):
                    put(("ri", l, j))
            if s == 6:
                for j in range(C4):
                    put(("pm", l, j))
            if s == 11:
                put(("cmean", l))
                put(("csq", l))
            if s == 13:
                put(("so", l))
        if l == 0:
            for g, nf in enumerate(FG):
                for j in range(nf):
                    put(("fg", g, j))
                for j in range(nf):
                    put(("fu", g, j))
            for j in range(KT):
                put(("fd", j))
            put(("mean", 1))
            put(("msq", 1))
    put("logits_t")
    put("logits")
    for i in range(2):
        for h in range(2):
            put(("xtok", i, h))
    put("ranks")
    for h in range(2):
        put(("xtok", 2, h))
    for h in range(2):
        put(("gath_hi", h), 6 + h)
    for h in range(2):
        put(("gath_lo", h), 1 + 2 * h)
    put(("y_init", 0), 4)
    put(("y_init", 1), 5)
    return place, used


PER_VISIT = [4, 4, 4, 4, 3, 3, 3, 4]


def trunk_kernel(nc, A, O):
    place, base = psum_plan()
    order = visit_order()

    with ExitStack() as ctx:
        def sb(name, shape, dt=F32):
            return ctx.enter_context(nc.sbuf_tensor(name, shape, dt))

        def sem(name):
            return ctx.enter_context(nc.semaphore(name))

        stage = sb("stage", [P, SLOTS, PIECE])
        w_hi = sb("w_hi", [P, SLOTS, PIECE], F16)
        w_lo = sb("w_lo", [P, SLOTS, PIECE], F16)
        x = sb("x", [P, KT, T])
        xh = sb("xh", [P, KT, T], F16)
        xl = sb("xl", [P, KT, T], F16)
        z = sb("z", [P, KT, T])
        zsq = sb("zsq", [P, KT, T])
        merged = zsq
        conv_sq = z[:, 0:C4, :]
        rt = z[:, 0:C4, :]
        pooled = z[:, C4:KT, :]
        win_s = sb("win_s", [P, L, C4, NS_, CW])
        pool_s = sb("pool_s", [P, L, C4, NS_, PW])
        lru_s = sb("lru_s", [P, L, C4, NS_, LW])
        h0_s = sb("h0_s", [P, L, C4, NS_])
        consts = sb("consts", [P, C_ALL])
        ident = consts[:, C_ID:C_ID + P]
        iota = consts[:, C_IO:C_IO + CAP]
        tri = consts[:, C_TR:C_TR + P]
        inv_cnt = consts[:, C_IC:C_IC + 64].rearrange("p (g w) -> p g w", g=4)
        idx_w = consts[:, C_IX:C_IX + NE]
        ones_d = sb("ones_d", [P, P])
        ones_b = sb("ones_b", [P, P])
        par = sb("par", [P, C4, L * NR])
        par_d = sb("par_d", [P, KT, L * NQ])
        sp4 = sb("sp4", [P, C4, L])
        spt = sb("spt", [P, 6, C4, L])
        sp8n = spt[:, 0]
        w_pool = sb("w_pool", [P, C4, P])
        w_a = sb("w_a", [P, C4, P])
        w_x = sb("w_x", [P, C4, P])
        stat = sb("stat", [P, 3, T])
        warm = sb("warm", [P, 24])
        logit_rows = stat[0:NE, 1, :]
        zsum, zsqsum = stat[:, 0, :], stat[:, 1, :]
        w_rt = sb("w_rt", [P, KT, NE])
        visits_i = sb("visits_i", [P, 1], I32)
        route = sb("route", [P, 10, 3, NE])
        route1 = sb("route1", [P, 8, 3])
        rank = sb("rank", [P, 3, NE])
        gate_split = sb("gate_split", [P, 3, NE, 2], F16)
        gate_slot = sb("gate_slot", [P, 1])
        ident16 = sb("ident16", [P, P], F16)

        ARENA = 12600
        arena = sb("arena", [P, ARENA])
        at = [0]

        def carve(shape, dt=F32, start=None):
            n = 1
            for s in shape:
                n *= s
            words = n if dt == F32 else (n + 1) // 2
            o = at[0] if start is None else start
            at[0] = o + words
            assert at[0] <= ARENA
            v = arena[:, o:o + words]
            v = v.bitcast(dt)[:, 0:n] if dt != F32 else v
            if len(shape) == 2:
                v = v.rearrange("p (a b) -> p a b", a=shape[0])
            if len(shape) == 3:
                v = v.rearrange("p (a b c) -> p a b c", a=shape[0], b=shape[1])
            return v

        gates = carve([KT, T], start=0)
        glu = carve([C4, CW - 1 + TP])
        conv_at = at[0]
        conv = carve([C4, T])
        upool_at = at[0]
        upool = carve([C4, PW - 1 + TP])
        hseq = carve([C4, T], start=upool_at)
        at[0] = upool_at + C4 * (PW - 1 + TP)
        ulru_at = at[0]
        ulru = carve([C4, LW - 1 + TP])
        rq = carve([C4, T], start=ulru_at)
        xc = carve([C4, T])
        ig = carve([C4, T])
        gelu = carve([C4, T])
        sg = carve([C4, T])
        a_lru = sg
        brh_at = at[0]
        brh = carve([C4, T], F16)
        brl = carve([C4, T], F16)
        so = carve([C4, 81])
        so_out = carve([DB])
        wsum = carve([2, PW - 1 + TP], start=0)
        prod = stat[:, 2, 0:NS_ * 32].rearrange("p (b k) -> p b k", b=NS_)
        x_rows = carve([2, D], start=0)
        conv_rows = carve([L, 2, DB], start=conv_at)
        pool_rows = carve([L, DB])
        lru_rows = carve([L, DB])
        par_rows = carve([DB])
        pard_rows = carve([D])
        xs_rows = carve([D], start=brh_at)
        hdh = carve([NF, T], F16, start=0)
        hdl = carve([NF, T], F16)
        silu_d = carve([4, T])
        h_d = carve([4, T])
        xth = carve([3, D], F16, start=0)
        xtl = carve([3, D], F16)
        xgh = carve([KT, CAP], F16)
        xgl = carve([KT, CAP], F16)
        silu_e = carve([2, 4 * CAP])
        h_e = carve([2, 4 * CAP])
        hh = carve([2, 4 * CAP], F16)
        hl = carve([2, 4 * CAP], F16)
        yh = carve([D], F16)
        yl = carve([D], F16)
        onehot = carve([3, CAP], F16)
        onehot_t = carve([T], F16)
        gsel = carve([3, 2], F16)
        y_rows = carve([3, D])

        ps = ctx.enter_context(nc.psum_tensor("ps", [P, 8, 512], F32))

        names = """ld_x ld_const ld_par ld_state ld_small out_dma y_out hi_done lo_done part_used
            x_hi x_split zeroed rows_zeroed dve gates_zeroed xc_ready xw_ready cw_ready cp_ready tanh_ready root_ready h_ready
            hg_ready br_hi bp_hi br_ready pooled_ready conv_done csq_done cv_ready silu_ready merge_done
            mg_ready mg_hi mg_split packed zsq_ready m2_ready var_ready std_ready nz_ready norm_ready
            f_hi f_split gd_ready gs_ready mask_ready visits_ready sp_abs sp_exp sp_done x_pool zadd zsum_ready ld_x2 pool
            xt_hi onehot_ready rank_next e_hi e_split y_hi cm2_ready cvar_ready cstd_ready""".split()
        S = {n: sem(n) for n in names}
        stage_full = [sem(f"stage_full{i}") for i in range(SLOTS)]
        bank_full = [sem(f"bank_full{i}") for i in range(8)]
        bank_free = [sem(f"bank_free{i}") for i in range(8)]

        def bank(name):
            return ps[:, place[name][0], :]

        def filled(eng, name):
            b, k = place[name]
            eng.wait_ge(bank_full[b], k + 1)

        def empty(eng, name):
            b, k = place[name]
            if k:
                eng.wait_ge(bank_free[b], k)

        def read_out(eng, name):
            b, k = place[name]
            eng.wait_ge(bank_free[b], k + 1)

        def in_visit(sems, b, v, i):
            return sems[b], v * PER_VISIT[b] + (base[b] + i + 1)

        def free_of(name):
            return bank_free[place[name][0]]

        def full_of(name):
            return bank_full[place[name][0]]

        def vec(name, l, j):
            r = VEC_B.index(name) * L + l
            return par[:, j, r:r + 1]

        def conv_tap(l, j, k, n=1):
            r = len(VEC_B) * L + l * CW + k
            return par[:, j, r:r + n]

        def lru_tap(l, j, k, n=1):
            r = (len(VEC_B) + CW) * L + l * LW + k
            return par[:, j, r:r + n]

        def gate_bias(l, b, d):
            return par_d[:, d, l * 3 + b:l * 3 + b + 1]

        def vec_d(name, l, d):
            r = 3 * L + VEC_D.index(name) * L + l
            return par_d[:, d, r:r + 1]

        def piece_done(eng, n):
            last = last_tile[n]
            if last is None:
                eng.wait_ge(S["part_used"], part_no[n])
            else:
                filled(eng, last)

        def wh(slot, k, c0, c1, width=512):
            return w_hi[:, slot, k * width + c0:k * width + c1]

        def wl(slot, k, c0, c1, width=512):
            return w_lo[:, slot, k * width + c0:k * width + c1]

        class Steps:

            def __init__(self, eng, s):
                self.eng, self.sem, self.n = eng, s, 0

            def did(self, ins):
                self.n += 1
                ins.then_inc(self.sem, 1)
                return self.n

            def after(self, n):
                self.eng.wait_ge(self.sem, n)

            def then(self, ins):
                self.after(self.did(ins))

        def pre_piece(n):
            if n >= PRE:
                return visit_piece(slice(0, 1), n - PRE)
            l, s = (0, n) if n < MIX + FFN else (1, n - MIX - FFN)
            if s < MIX:
                s, half = s // 2, s % 2
                what = IN_ORDER[s]
                if what[0] == "branch":
                    w = (A["w_br_pool"], A["w_br_conv"], A["w_br_lru"])[what[1]]
                    return w[l, :, half * 512:half * 512 + 512].rearrange("(k p) n -> p k n", p=P), C4, 512
                w = A["w_out"] if what[0] == "out" else A["w_in"]
                c = what[1] * 512
                return w[l, half * 512:half * 512 + 512, c:c + 512].rearrange("(k p) n -> p k n", p=P), 4, 512
            s -= MIX
            if s < 4 * len(FG):
                g, up, half = s // 4, s // 2 % 2, s % 2
                w = (A["ffn_w_gate"], A["ffn_w_up"])[up]
                n_ = FG[g] * P
                return (w[0, half * 512:half * 512 + 512, 512 * g:512 * g + n_]
                        .rearrange("(k p) n -> p k n", p=P)), 4, n_
            s -= 4 * len(FG)
            half, g = s // len(FG), s % len(FG)
            return (A["ffn_w_down"][0, 512 * g:512 * g + FG[g] * P, half * 512:half * 512 + 512]
                    .rearrange("(k p) n -> p k n", p=P)), FG[g], 512

        def visit_piece(e, m):
            kind, c, h = order[m]
            if kind == "d":
                return (A["moe_w_down"][0, e, c * 512 + h * 256:c * 512 + h * 256 + 256, :]
                        .rearrange("a (k p) n -> (a p) k n", p=P)), 2, D
            w = A["moe_w_gate"] if kind == "g" else A["moe_w_up"]
            return (w[0, e, h * 512:h * 512 + 512, c * 512:(c + 1) * 512]
                    .rearrange("a (k p) n -> (a p) k n", p=P)), 4, 512

        last_tile, part_no = {}, {}

        def ends(n, tile):
            last_tile[n] = tile
            if tile is None:
                part_no[n] = len(part_no) + 1

        for l in range(L):
            for s, what in enumerate(IN_ORDER):
                n = mixer_piece(l) + 2 * s
                branch = what[0] == "branch"
                ends(n, ("mix", l, s, 3) if branch else None)
                ends(n + 1, ("mix", l, s, KT - 1 if branch else 3))
            if l == 0:
                for g, nf in enumerate(FG):
                    for i, nm in enumerate(("fg", "fu")):
                        ends(MIX + 4 * g + 2 * i, None)
                        ends(MIX + 4 * g + 2 * i + 1, (nm, g, nf - 1))
                for half in range(2):
                    for g in range(len(FG)):
                        ends(MIX + 4 * len(FG) + half * len(FG) + g,
                             ("fd", 4 * half + 3) if g == len(FG) - 1 else None)
        PART0 = len(part_no)
        part_in_visit = [m for m, (kind, c, h) in enumerate(order) if h == 0 or (kind == "d" and c < NC - 1)]
        NPART = len(part_in_visit)
        OUT_ORDER = [(h, i) for h in range(2) for i in range(3)]
        NSUM = 5
        DT = 3
        GATHER_AT = VISIT - 2

        block = ctx.enter_context(nc.Block())

        @block.sync
        def _(sp):
            rows = A["x_prompt"][0].rearrange("(a p) n -> p a n", p=P)
            sp.dma_start(x_rows[:, :, 0:512], rows[:, :, 0:512]).then_inc(S["ld_x"], 16)
            sp.dma_start(xs_rows[0:NS_, :], A["x_sample"].rearrange("b s n -> (b s) n")).then_inc(S["ld_x"], 16)

            def load(src, tiles, width, slot):
                dst = stage[:, slot, 0:tiles * width].rearrange("p (k n) -> p k n", k=tiles)
                sp.dma_start(dst, src).then_inc(stage_full[slot], 16)

            def small_vectors():
                for i, name in enumerate(VEC_B):
                    sp.dma_start(par_rows[i * L:(i + 1) * L, :], A[name]).then_inc(S["ld_par"], 16)
                r = len(VEC_B) * L
                sp.dma_start(par_rows[r:r + L * CW, :], A["conv_w"].rearrange("l k n -> (l k) n")).then_inc(S["ld_par"], 16)
                r += L * CW
                sp.dma_start(par_rows[r:r + L * LW, :], A["lru_conv_w"].rearrange("l k n -> (l k) n")
                              ).then_inc(S["ld_par"], 16)
                sp.dma_start(pard_rows[0:3 * L, :], A["b_gate"].rearrange("l (b n) -> (l b) n", b=3)
                              ).then_inc(S["ld_par"], 16)
                for i, name in enumerate(VEC_D):
                    sp.dma_start(pard_rows[(3 + i) * L:(4 + i) * L, :], A[name]).then_inc(S["ld_par"], 16)

            for n in range(PRE):
                if n == 3:
                    small_vectors()
                if n >= SLOTS:
                    sp.wait_ge(S["lo_done"], n - SLOTS + 1)
                load(*pre_piece(n), n % SLOTS)
                if n == 0:
                    sp.dma_start(x_rows[:, :, 512:D], rows[:, :, 512:D]).then_inc(S["ld_x2"], 16)

            def visit(v):
                e = v % NE
                for m in range(VISIT):
                    n = PRE + m
                    sp.wait_ge(S["lo_done"], v * VISIT + (n - SLOTS + 1))
                    load(*visit_piece(bass.ds(e, 1), m), n % SLOTS)

            with sp.Fori(0, NE) as v:
                visit(v)
            sp.wait_ge(S["visits_ready"], 1)
            nv = sp.value_load(visits_i[0:1, 0:1], min_val=NE, max_val=3 * NE)
            with sp.If(nv > NE):
                with sp.Fori(NE, nv) as v:
                    visit(v)
            sp.nop()
            sp.wait_ge(S["out_dma"], 16 * 11 * L)
            sp.wait_ge(S["y_out"], 16 * len(OUT_ORDER))

        @block.gpsimd
        def _(pool):
            pool.wait_ge(S["ld_x2"], 16)
            for l in range(L):
                for h in range(2):
                    pool.dma_start(conv_rows[0:4 * (CW - 1), l, h, :],
                                   A["state_conv"][l, 4 * h:4 * h + 4].rearrange("b r n -> (b r) n")
                                   ).then_inc(S["ld_state"], 16)
                pool.dma_start(pool_rows[0:NS_ * (PW - 1), l, :],
                               A["state_pool"][l].rearrange("b r n -> (b r) n")).then_inc(S["ld_state"], 16)
                pool.dma_start(lru_rows[0:NS_ * (LW - 1), l, :],
                               A["state_lru_conv"][l].rearrange("b r n -> (b r) n")).then_inc(S["ld_state"], 16)
                pool.dma_start(lru_rows[24:24 + NS_, l, :], A["state_lru_h"][l]).then_inc(S["ld_state"], 16)
            nc.gpsimd.memset(w_a[:], 0.0).then_inc(S["gates_zeroed"], 1)
            nc.gpsimd.memset(w_x[:], 0.0).then_inc(S["gates_zeroed"], 1)
            pool.wait_ge(S["gates_zeroed"], 2)

            def small(l):
                pool.dma_start(w_pool[:, :, :], A["w_pool"][l].rearrange("g c d -> c g d")).then_inc(S["ld_small"], 16)
                for w, t in ((A["lru_wa"], w_a), (A["lru_wx"], w_x)):
                    for h in range(2):
                        pool.dma_start(t[64 * h:64 * h + 64, :, 64 * h:64 * h + 64],
                                       w[l].rearrange("(j h) c d -> h c j d", h=2)[h]).then_inc(S["ld_small"], 16)

            small(0)
            pool.dma_start(w_rt[:, :, :], A["moe_router"][0].rearrange("(k p) n -> p k n", p=P)
                           ).then_inc(S["ld_small"], 16)
            own = Steps(pool, S["pool"])
            G = nc.gpsimd

            def halve(src, w):
                while w > 1:
                    w //= 2
                    own.then(G.tensor_tensor(prod[:, :, 0:w], src[:, :, 0:w], src[:, :, w:2 * w], ALU.add))
                    src = prod

            def window_conv(win, taps, width, out, bias, done):
                own.then(G.memset(prod[:, :, 31:32], 0.0))
                for j in range(C4):
                    w = taps(l, j, 0, width).unsqueeze(1).to_broadcast([P, NS_, width])
                    own.then(G.tensor_tensor(prod[:, :, 0:width], win[:, l, j, :, :], w, ALU.mult))
                    halve(prod, 32 if width > 16 else width)
                    i = G.tensor_scalar(out[:, j, TP:T], prod[:, :, 0], 1.0, vec(bias, l, j), ALU.mult, ALU.add)
                    i.then_inc(S[done], 1)
                    pool.wait_ge(S[done], l * C4 + j + 1)

            def pool_windows():
                if l:
                    pool.wait_ge(S["x_pool"], 2 * KT)
                for j in range(C4):
                    src, w = upool[:, j, :], 1
                    E_ = PW - 1 + TP
                    while w < WINDOWS[j]:
                        dst = wsum[:, (w.bit_length() - 1) % 2, :]
                        lo_ = 2 * w - 1
                        own.then(G.tensor_tensor(dst[:, lo_:E_], src[:, lo_:E_], src[:, lo_ - w:E_ - w], ALU.add))
                        src, w = dst, 2 * w
                    mean = wsum[:, (w.bit_length() - 1) % 2, 0:TP]
                    own.then(G.tensor_scalar(mean, src[:, PW - 1:], 1.0 / w, None, ALU.mult))
                    own.then(G.tensor_tensor(pooled[:, j, 0:TP], mean, upool[:, j, PW - 1:], ALU.subtract))
                    o2 = mean[:, 0:PW]
                    own.then(G.tensor_tensor(o2, src[:, PW - 1:2 * PW - 1], inv_cnt[:, j, :], ALU.mult))
                    own.then(G.tensor_tensor(pooled[:, j, 0:PW], o2, upool[:, j, PW - 1:2 * PW - 1], ALU.subtract))
                    halve(pool_s[:, l, j, :, PW - w:PW], w)
                    own.then(G.tensor_scalar(prod[:, :, 1], prod[:, :, 0], 1.0 / w, None, ALU.mult))
                    G.tensor_tensor(pooled[:, j, TP:T], prod[:, :, 1], pool_s[:, l, j, :, PW - 1],
                                    ALU.subtract).then_inc(S["pooled_ready"], 1)
                    pool.wait_ge(S["pooled_ready"], l * C4 + j + 1)

            def norm(q, tiles, l, g):
                for j in range(1, NSUM):
                    pool.wait_ge(S["zsq_ready"], q * KT + j + 1)
                    if j > 1:
                        pool.wait_ge(S["zadd"], q * (NSUM - 1) + j - 1)
                    G.tensor_tensor(zsqsum, zsq[:, 0, :] if j == 1 else zsqsum, zsq[:, j, :],
                                    ALU.add).then_inc(S["zadd"], 1)
                if q < 2:
                    for j in range(KT):
                        pool.wait_ge(S["nz_ready"], q * KT + j + 1)
                        nc.gpsimd.tensor_scalar(x[:, j, :], z[:, j, :], 1.0, vec_d(g, l, j), ALU.mult,
                                                ALU.add).then_inc(S["x_pool"], 1)

            for l in range(L):
                for j in range(C4):
                    read_out(pool, ("mix", l, 1, j))
                nc.gpsimd.tensor_copy(so[:, :, 0:30], glu[:, :, TP:TP + 30]).then_inc(S["packed"], 1)
                nc.gpsimd.tensor_copy(so[:, :, 49:57], win_s[:, l, :, :, CW - 1]).then_inc(S["packed"], 1)
                read_out(pool, "par512")
                read_out(pool, ("st_lru", L - 1))
                window_conv(win_s, conv_tap, CW, conv, "conv_b", "cw_ready")
                for j in range(C4):
                    read_out(pool, ("mix", l, 2, j))
                nc.gpsimd.tensor_copy(so[:, :, 45:48], ulru[:, :, TP:TP + 3]).then_inc(S["packed"], 1)
                nc.gpsimd.tensor_copy(so[:, :, 65:73], lru_s[:, l, :, :, LW - 1]).then_inc(S["packed"], 1)
                window_conv(lru_s, lru_tap, LW, xc, "lru_conv_b", "xw_ready")
                for j in range(C4):
                    read_out(pool, ("mix", l, 3, j))
                nc.gpsimd.tensor_copy(so[:, :, 30:45], upool[:, :, TP:TP + 15]).then_inc(S["packed"], 1)
                nc.gpsimd.tensor_copy(so[:, :, 57:65], pool_s[:, l, :, :, PW - 1]).then_inc(S["packed"], 1)
                pool_windows()
                for j in range(DT, C4):
                    for k in range(CW):
                        src, w = glu[:, j, k:k + TP], conv_tap(l, j, k)
                        if k == 0:
                            own.then(G.tensor_scalar(conv[:, j, 0:TP], src, w, vec("conv_b", l, j), ALU.mult, ALU.add))
                        else:
                            tap = stat[:, k % 2, 0:TP]
                            own.then(G.tensor_scalar(tap, src, w, None, ALU.mult))
                            i = G.tensor_tensor(conv[:, j, 0:TP], tap, conv[:, j, 0:TP], ALU.add)
                            if k < CW - 1:
                                own.then(i)
                            else:
                                i.then_inc(S["cp_ready"], 1)
                pool.wait_ge(S["h_ready"], l + 1)
                nc.gpsimd.tensor_copy(so[:, :, 48:49], hseq[:, :, TP - 1:TP]).then_inc(S["packed"], 1)
                nc.gpsimd.tensor_copy(so[:, :, 73:81], hseq[:, :, TP:T]).then_inc(S["packed"], 1)
                if l + 1 < L:
                    filled(pool, ("pm", l, C4 - 1))
                    small(l + 1)
                read_out(pool, ("so", l))
                for dst, r0, r1 in ((O["conv_p"][l, 0], 0, 30), (O["pool_p"][l, 0], 30, 45), (O["lconv_p"][l, 0], 45, 48),
                                    (O["h_p"][l], 48, 49), (O["conv_s"][l, :, CW - 2, :], 49, 57),
                                    (O["pool_s"][l, :, PW - 2, :], 57, 65), (O["lconv_s"][l, :, LW - 2, :], 65, 73),
                                    (O["h_s"][l], 73, 81)):
                    pool.dma_start(dst, so_out[r0:r1, :]).then_inc(S["out_dma"], 16)
                norm(2 * l, [("mix", l, 14 + j // 4, j % 4) for j in range(KT)], l, "ln1_b")
                if l == 1:
                    pool.wait_ge(S["nz_ready"], 3 * KT)
                    for what in (yh[:, :], yl[:, :], onehot_t, gate_slot[:, :], xtl[:, 2, :], xth[:, 2, :]):
                        G.memset(what, 0.0).then_inc(S["rows_zeroed"], 1)
                if l == 0:
                    norm(1, [("fd", j) for j in range(KT)], l, "ln2_b")
                    for l in range(L):
                        pool.dma_start(O["conv_s"][l, :, 0:CW - 2, :], A["state_conv"][l, :, 1:CW - 1, :]
                                       ).then_inc(S["out_dma"], 16)
                        pool.dma_start(O["pool_s"][l, :, 0:PW - 2, :], A["state_pool"][l, :, 1:PW - 1, :]
                                       ).then_inc(S["out_dma"], 16)
                        pool.dma_start(O["lconv_s"][l, :, 0:LW - 2, :], A["state_lru_conv"][l, :, 1:LW - 1, :]
                                       ).then_inc(S["out_dma"], 16)

        @block.tensor
        def _(pe):
            mm = nc.tensor.matmul

            def mm3(out, ah, al, bh, bl, start, stop):
                mm(out, ah, bh, start=start, stop=False, skip_group_check=True)
                mm(out, ah, bl, start=False, stop=False, skip_group_check=True)
                return mm(out, al, bh, start=False, stop=stop, skip_group_check=True)

            pe.wait_ge(S["ld_const"], 16)
            pe.wait_ge(S["ld_x"], 32)
            for k in range(KT):
                if k == 4:
                    pe.wait_ge(S["ld_x2"], 16)
                o = bank(("xT", k))
                for a in range(2):
                    nc.tensor.transpose(o[:, a * P:(a + 1) * P], x_rows[:, a, k * P:(k + 1) * P], ident)
                nc.tensor.transpose(o[:, TP:T], xs_rows[0:NS_, k * P:(k + 1) * P],
                                    ident[0:NS_, 0:NS_]).then_inc(full_of(("xT", k)), 1)
            def params():
                pe.wait_ge(S["ld_par"], 16 * 15)
                empty(pe, "par512")
                for j in range(C4):
                    t = nc.tensor.transpose(bank("par512")[:, j * L * NR:(j + 1) * L * NR],
                                            par_rows[0:L * NR, j * P:(j + 1) * P], ident[0:L * NR, 0:L * NR])
                t.then_inc(full_of("par512"), 1)
                empty(pe, "par1024")
                for j in range(KT):
                    t = nc.tensor.transpose(bank("par1024")[:, j * L * NQ:(j + 1) * L * NQ],
                                            pard_rows[0:L * NQ, j * P:(j + 1) * P], ident[0:L * NQ, 0:L * NQ])
                t.then_inc(full_of("par1024"), 1)

            def states():
                pe.wait_ge(S["ld_state"], 16 * 5 * L)
                for l in range(L):
                    R = 4 * (CW - 1)
                    for h in range(2):
                        n = ("st_conv", l, h)
                        empty(pe, n)
                        for j in range(C4):
                            t = nc.tensor.transpose(bank(n)[:, j * R:(j + 1) * R],
                                                    conv_rows[0:R, l, h, j * P:(j + 1) * P], ident[0:R, 0:R])
                        t.then_inc(full_of(n), 1)
                    R = NS_ * (PW - 1)
                    n = ("st_pool", l)
                    empty(pe, n)
                    for j in range(C4):
                        t = nc.tensor.transpose(bank(n)[:, j * R:(j + 1) * R],
                                                pool_rows[0:R, l, j * P:(j + 1) * P], ident[0:R, 0:R])
                    t.then_inc(full_of(n), 1)
                    n = ("st_lru", l)
                    empty(pe, n)
                    for j in range(C4):
                        t = nc.tensor.transpose(bank(n)[:, j * 32:j * 32 + 32],
                                                lru_rows[0:32, l, j * P:(j + 1) * P], ident[0:32, 0:32])
                    t.then_inc(full_of(n), 1)

            def stats(q, tiles):
                mean, msq = ("mean", q), ("msq", q)
                empty(pe, mean)
                empty(pe, msq)
                for j in range(NSUM, KT):
                    end = j == KT - 1
                    read_out(pe, tiles[j])
                    if end:
                        pe.wait_ge(S["zadd"], (q + 1) * (NSUM - 1))
                        mm(bank(msq)[:, 0:T], ones_d[:, :], zsqsum, start=False, stop=False, skip_group_check=True)
                    t = mm(bank(mean)[:, 0:T], ones_d[:, :], z[:, j, :], start=(j == NSUM), stop=end,
                           skip_group_check=True)
                    if end:
                        t.then_inc(full_of(mean), 1)
                    pe.wait_ge(S["zsq_ready"], q * KT + j + 1)
                    t = mm(bank(msq)[:, 0:T], ones_d[:, :], zsq[:, j, :], start=(j == NSUM), stop=end,
                           skip_group_check=True)
                    if end:
                        t.then_inc(full_of(msq), 1)
                    if j == NSUM:
                        pe.wait_ge(S["zsum_ready"], (q + 1) * (NSUM - 1))
                        mm(bank(mean)[:, 0:T], ones_d[:, :], zsum, start=False, stop=False, skip_group_check=True)

            def rows_half(slot, names_, half, width, ready=None):
                steps = [(j, k) for j in range(len(names_)) for k in range(4)]
                if ready and half == 0:
                    steps.sort(key=lambda jk: jk[1])
                for i, (j, k) in enumerate(steps):
                    kk = 4 * half + k
                    if ready and (half == 0 and j == 0 or half and i < 4):
                        ready(kk)
                    if half == 0 and k == 0:
                        empty(pe, names_[j])
                    t = mm3(bank(names_[j])[:, 0:T], wh(slot, k, j * P, (j + 1) * P, width),
                            wl(slot, k, j * P, (j + 1) * P, width), xh[:, kk, :], xl[:, kk, :],
                            kk == 0, kk == KT - 1)
                    if kk == KT - 1:
                        t.then_inc(full_of(names_[j]), 1)
                if half == 0:
                    t.then_inc(S["part_used"], 1)

            for l in range(L):
                b0 = mixer_piece(l)
                for s, what in enumerate(IN_ORDER):
                    kind = what[0]
                    if kind == "branch":
                        if what[1] == 0:
                            for j in range(C4):
                                read_out(pe, ("pm", l, j))
                        else:
                            pe.wait_ge(S["br_ready"], (2 * l + {2: 1, 1: 2}[what[1]]) * C4)
                    for half in range(2):
                        n = b0 + 2 * s + half
                        slot = n % SLOTS
                        pe.wait_ge(S["lo_done"], n + 1)
                        if kind == "branch":
                            for j in range(4):
                                name = ("mix", l, s, 4 * half + j)
                                empty(pe, name)
                                for k in range(C4):
                                    t = mm3(bank(name)[:, 0:T], wh(slot, k, j * P, (j + 1) * P),
                                            wl(slot, k, j * P, (j + 1) * P), brh[:, k, :], brl[:, k, :],
                                            k == 0, k == C4 - 1)
                                t.then_inc(full_of(name), 1)
                        else:
                            names_ = [("mix", l, s, j) for j in range(4)]
                            if s == 14:
                                rows_half(slot, names_, half, 512, lambda kk: pe.wait_ge(S["mg_split"], l * KT + kk + 1))
                            elif s == 0 and l:
                                rows_half(slot, names_, half, 512, lambda kk: pe.wait_ge(S["x_split"], KT + kk + 1))
                            elif s == 0:
                                rows_half(slot, names_, half, 512, lambda kk: read_out(pe, ("xT", kk)))
                            else:
                                rows_half(slot, names_, half, 512)
                        if s in (4, 5) and half == 0:
                            nm, w = ("ra", w_a) if s == 4 else ("ri", w_x)
                            pe.wait_ge(S["ld_small"], 16 * (6 + 5 * l))
                            for j in range(C4):
                                pe.wait_ge(S["xc_ready"], l * C4 + j + 1)
                                pe.wait_ge(S["xw_ready"], l * C4 + j + 1)
                                empty(pe, (nm, l, j))
                                mm(bank((nm, l, j))[:, 0:T], w[:, j, :], xc[:, j, :], start=True,
                                   stop=True).then_inc(full_of((nm, l, j)), 1)
                        if s == 6 and half == 0:
                            for j in range(C4):
                                pe.wait_ge(S["pooled_ready"], l * C4 + j + 1)
                                empty(pe, ("pm", l, j))
                                mm(bank(("pm", l, j))[:, 0:T], w_pool[:, j, :], pooled[:, j, :], start=True,
                                   stop=True).then_inc(full_of(("pm", l, j)), 1)
                    if s == 0 and l == 0:
                        params()
                    if s == 1 and l == 0:
                        states()
                    if s == 11:
                        pe.wait_ge(S["csq_done"], l + 1)
                        for nm, src in (("cmean", conv), ("csq", conv_sq)):
                            empty(pe, (nm, l))
                            for j in range(C4):
                                t = mm(bank((nm, l))[:, 0:T], ones_b[:, :], src[:, j, :],
                                       start=(j == 0), stop=(j == C4 - 1))
                            t.then_inc(full_of((nm, l)), 1)
                    if s == 13:
                        pe.wait_ge(S["packed"], 8 * (l + 1))
                        empty(pe, ("so", l))
                        for j in range(C4):
                            t = nc.tensor.transpose(bank(("so", l))[0:81, j * P:(j + 1) * P], so[:, j, 0:81],
                                                    ident)
                        t.then_inc(full_of(("so", l)), 1)
                stats(2 * l, [("mix", l, 14 + j // 4, j % 4) for j in range(KT)])
                if l == 0:
                    n = MIX
                    for g, nf in enumerate(FG):
                        for nm in ("fg", "fu"):
                            for half in range(2):
                                pe.wait_ge(S["lo_done"], n + 1)
                                names_ = [(nm, g, j) for j in range(nf)]
                                if n < MIX + 2:
                                    rows_half(n % SLOTS, names_, half, nf * P,
                                              lambda kk: pe.wait_ge(S["x_split"], kk + 1))
                                else:
                                    rows_half(n % SLOTS, names_, half, nf * P)
                                n += 1
                    for half in range(2):
                        for g, nf in enumerate(FG):
                            pe.wait_ge(S["lo_done"], n + 1)
                            pe.wait_ge(S["f_split"], 4 * g + nf)
                            for j in range(4):
                                name = ("fd", half * 4 + j)
                                if g == 0:
                                    empty(pe, name)
                                for k in range(nf):
                                    f = 4 * g + k
                                    t = mm3(bank(name)[:, 0:T], wh(n % SLOTS, k, j * P, (j + 1) * P),
                                            wl(n % SLOTS, k, j * P, (j + 1) * P), hdh[:, f, :],
                                            hdl[:, f, :], f == 0, f == NF - 1)
                                if g == len(FG) - 1:
                                    t.then_inc(full_of(name), 1)
                            if g < len(FG) - 1:
                                t.then_inc(S["part_used"], 1)
                            n += 1
                    stats(1, [("fd", j) for j in range(KT)])

            pe.wait_ge(S["ld_small"], 16 * 11)
            empty(pe, "logits_t")
            for k in range(KT):
                pe.wait_ge(S["norm_ready"], k + 1)
                t = mm(bank("logits_t")[0:NE, 0:T], w_rt[:, k, :], x[:, k, :], start=(k == 0), stop=(k == KT - 1))
            t.then_inc(full_of("logits_t"), 1)
            empty(pe, "logits")
            read_out(pe, "logits_t")
            for i in range(3):
                n = P if i < 2 else NS_
                t = nc.tensor.transpose(bank("logits")[0:n, i * NE:(i + 1) * NE],
                                        logit_rows[:, i * P:i * P + n], ident[0:NE, 0:NE])
            t.then_inc(full_of("logits"), 1)

            def token_rows(i):
                n = P if i < 2 else NS_
                for h in range(2):
                    name = ("xtok", i, h)
                    empty(pe, name)
                    for k in range(4):
                        t = nc.tensor.transpose(bank(name)[0:n, k * P:(k + 1) * P],
                                                x[:, 4 * h + k, i * P:i * P + n], ident)
                    t.then_inc(full_of(name), 1)

            token_rows(0)
            token_rows(1)
            pe.wait_ge(S["mask_ready"], 1)
            empty(pe, "ranks")
            rk = bank("ranks")
            mask = route[:, 0, :, :]
            for i in range(3):
                n = P if i < 2 else NS_
                for q in range(i):
                    mm(rk[0:n, i * NE:(i + 1) * NE], ones_d[:, 0:n], mask[:, q, :], start=(q == 0), stop=False)
                mm(rk[0:n, i * NE:(i + 1) * NE], tri[0:n, 0:n], mask[0:n, i, :], start=(i == 0), stop=True)
            for i in range(3):
                n = P if i < 2 else NS_
                t = mm(rk[:, 3 * NE:4 * NE], ones_d[0:n, :], mask[0:n, i, :], start=(i == 0), stop=(i == 2))
            t.then_inc(full_of("ranks"), 1)
            token_rows(2)

            def gather(v, in_loop):
                pe.wait_ge(S["onehot_ready"], v + 1)
                for part, rows, banks in (("gath_hi", xth, (6, 7)), ("gath_lo", xtl, (1, 3))):
                    if in_loop is None:
                        pe.wait_ge(S["xt_hi"], 6)
                        if part == "gath_lo":
                            for i in range(3):
                                for h in range(2):
                                    read_out(pe, ("xtok", i, h))
                    for h, b in enumerate(banks):
                        if in_loop is None:
                            empty(pe, (part, h))
                        else:
                            pe.wait_ge(*in_visit(bank_free, b, in_loop, PER_VISIT[b] - 2))
                        for k in range(4):
                            for i in range(3):
                                t = mm(ps[:, b, k * CAP:(k + 1) * CAP],
                                       rows[:, i, (4 * h + k) * P:(4 * h + k + 1) * P],
                                       onehot[:, i, :], start=(i == 0), stop=(i == 2))
                        t.then_inc(bank_full[b], 1)

            def scatter(v, batch):
                if batch == 0:
                    for b in (4, 5):
                        pe.wait_ge(*in_visit(bank_free, b, v, -1))
                for b in range(4, 8):
                    d = 4 * batch + b - 4
                    pe.wait_ge(*in_visit(bank_free, b, v, batch - 1))
                    mm(ps[:, b, 0:T], yh[0:CAP, d * P:(d + 1) * P], onehot_t[0:CAP, :], start=True, stop=False)
                    mm(ps[:, b, 0:T], yl[0:CAP, d * P:(d + 1) * P], onehot_t[0:CAP, :], start=False,
                       stop=True).then_inc(bank_full[b], 1)

            gather(0, None)
            pe.wait_ge(S["visits_ready"], 1)
            nv = pe.value_load(visits_i[0:1, 0:1], min_val=NE, max_val=3 * NE)

            with pe.Fori(0, nv) as v:
                def slot_of(m):
                    return (PRE + m) % SLOTS

                def half_piece(c, kind, h):
                    m = order.index((kind, c, h))
                    slot = slot_of(m)
                    b = c % 2 + (0 if kind == "g" else 2)
                    pe.wait_ge(S["lo_done"], v * VISIT + (PRE + m + 1))
                    if h == 0:
                        pe.wait_ge(*in_visit(bank_free, b, v, c // 2 - 1))
                    for j in range(4):
                        for k in range(4):
                            kk = 4 * h + k
                            t = mm3(ps[:, b, j * CAP:(j + 1) * CAP], wh(slot, k, j * P, (j + 1) * P),
                                    wl(slot, k, j * P, (j + 1) * P), xgh[:, kk, :], xgl[:, kk, :],
                                    kk == 0 and j == 0, kk == KT - 1)
                    t.then_inc(bank_full[b] if h else S["part_used"], 1)

                def gate_up(c, kinds="gu"):
                    if c == 0:
                        for b in (6, 7, 1, 3):
                            pe.wait_ge(*in_visit(bank_free, b, v, -1))
                    for kind in kinds:
                        for h in range(2):
                            half_piece(c, kind, h)

                def down(c):
                    pe.wait_ge(S["e_split"], v * NC + (c + 2))
                    for h in range(2):
                        m = order.index(("d", c, h))
                        slot = slot_of(m)
                        pe.wait_ge(S["lo_done"], v * VISIT + (PRE + m + 1))
                        for half in range(2):
                            b = 4 + half
                            if c == 0 and h == 0:
                                pe.wait_ge(*in_visit(bank_free, b, v, 1))
                            for k in range(2):
                                f = 2 * h + k
                                cols = slice(f * CAP, (f + 1) * CAP)
                                t = mm3(ps[0:CAP, b, :], hh[:, c % 2, cols], hl[:, c % 2, cols],
                                        wh(slot, k, half * 512, half * 512 + 512, D),
                                        wl(slot, k, half * 512, half * 512 + 512, D),
                                        c == 0 and f == 0, c == NC - 1 and f == 3)
                            if c == NC - 1 and h:
                                t.then_inc(bank_full[b], 1)
                        if not (c == NC - 1 and h):
                            t.then_inc(S["part_used"], 1)

                gate_up(0)
                scatter(v, 0)
                gate_up(1, "g")
                scatter(v, 1)
                gate_up(1, "u")
                pe.wait_ge(*in_visit(bank_free, 7, v, 1))
                st = ps[:, 7, :].bitcast(F16)
                for i in range(3):
                    n = P if i < 2 else NS_
                    nc.tensor.transpose(st[0:CAP, i * P:i * P + n], onehot[0:n, i, :], ident16[0:n, 0:n])
                for i in range(3):
                    t = mm(ps[0:CAP, 7, 256:258], onehot[:, i, :], gsel[:, i, :], start=(i == 0), stop=(i == 2))
                t.then_inc(bank_full[7], 1)
                down(0)
                for c in range(2, NC):
                    gate_up(c)
                    if c < NC - 1:
                        down(c - 1)
                down(NC - 2)
                with pe.If(v < nv - 1):
                    gather(v + 1, v)
                with pe.If(v > nv - 2):
                    for b in (6, 7, 1, 3):
                        pe.wait_ge(*in_visit(bank_free, b, v, PER_VISIT[b] - 2))
                        mm(ps[0:1, b, 0:1], ident16[:, 0:1], ident16[:, 0:1], start=True, stop=True
                           ).then_inc(bank_full[b], 1)
                down(NC - 1)

            scatter(nv, 0)
            scatter(nv, 1)
            for j in range(KT):
                end = j == KT - 1
                pe.wait_ge(*in_visit(bank_free, 4 + j % 4, nv, j // 4))
                if j == 0:
                    pe.wait_ge(*in_visit(bank_free, 0, nv, -1))
                    pe.wait_ge(*in_visit(bank_free, 1, nv, -1))
                if j >= NSUM:
                    t = mm(ps[:, 0, 0:T], ones_d[:, :], z[:, j, :], start=(j == NSUM), stop=end,
                           skip_group_check=True)
                    if end:
                        t.then_inc(bank_full[0], 1)
                pe.wait_ge(S["zsq_ready"], 3 * KT + j + 1)
                t = mm(ps[:, 1, 0:T], ones_d[:, :], zsq[:, j, :], start=(j == 0), stop=end,
                       skip_group_check=True)
                if end:
                    t.then_inc(bank_full[1], 1)
                if j == NSUM:
                    pe.wait_ge(S["zsum_ready"], 4 * (NSUM - 1))
                    mm(ps[:, 0, 0:T], ones_d[:, :], zsum, start=False, stop=False, skip_group_check=True)
            for o, (h, i) in enumerate(OUT_ORDER):
                n = P if i < 2 else NS_
                b = 2 + o % 2
                pe.wait_ge(S["norm_ready"], KT + 4 * (h + 1))
                pe.wait_ge(*in_visit(bank_free, b, nv, o // 2 - 1))
                for k in range(4):
                    t = nc.tensor.transpose(ps[0:n, b, k * P:(k + 1) * P], x[:, 4 * h + k, i * P:i * P + n],
                                            ident)
                t.then_inc(bank_full[b], 1)

        @block.scalar
        def _(act):
            fn = nc.scalar.activation

            def hi(n):
                tiles, width = pre_piece(n)[1:]
                act.wait_ge(stage_full[n % SLOTS], 16 * (n // SLOTS + 1))
                if n >= SLOTS:
                    piece_done(act, n - SLOTS)
                fn(w_hi[:, n % SLOTS, 0:tiles * width], stage[:, n % SLOTS, 0:tiles * width], ACT.Copy,
                   scale=WS).then_inc(S["hi_done"], 1)

            def norm(q, mean, l, b):
                mean_full(act, mean)
                fn(stat[:, 0, :], mean_ap(mean), ACT.Square).then_inc(S["m2_ready"], 1)
                act.wait_ge(S["var_ready"], q + 1)
                fn(stat[:, 2, :], stat[:, 1, :], ACT.Sqrt).then_inc(S["std_ready"], 1)
                if q == 2:
                    hi(PRE + AHEAD)
                for j in range(KT):
                    act.wait_ge(S["nz_ready"], q * KT + j + 1)
                    if q < 2:
                        fn(xh[:, j, :], z[:, j, :], ACT.Identity, bias=vec_d(b, l, j)).then_inc(S["x_hi"], 1)
                    else:
                        fn(x[:, j, :], z[:, j, :], ACT.Identity, bias=vec_d(b, l, j)).then_inc(S["norm_ready"], 1)

            tables = [0]

            def table(func):
                tables[0] += 1
                fn(warm[:, tables[0] - 1:tables[0]], consts[:, 0:1], func)

            def mean_full(eng, mean):
                if mean[0] == "tail":
                    eng.wait_ge(*in_visit(bank_full, 0, mean[2], 0))
                else:
                    filled(eng, mean)

            def mean_ap(mean):
                return ps[:, mean[1], 0:T] if mean[0] == "tail" else bank(mean)[:, 0:T]

            act.dma_start(consts[:, :], A["consts"]).then_inc(S["ld_const"], 16)
            for k in range(KT):
                filled(act, ("xT", k))
                fn(xh[:, k, :], bank(("xT", k))[:, 0:T], ACT.Copy).then_inc(S["x_hi"], 1)
                if k == 3:
                    hi(0)
            for n in range(1, AHEAD):
                hi(n)

            def params():
                filled(act, "par512")
                fn(par[:, :, :], bank("par512")[:, 0:C4 * L * NR].rearrange("p (j r) -> p j r", j=C4),
                   ACT.Copy).then_inc(free_of("par512"), 1)
                filled(act, "par1024")
                fn(par_d[:, :, :], bank("par1024")[:, 0:KT * L * NQ].rearrange("p (j r) -> p j r", j=KT),
                   ACT.Copy).then_inc(free_of("par1024"), 1)
                read_out(act, "par512")
                read_out(act, "par1024")

            def states():
                for l_ in range(L):
                    for h in range(2):
                        n = ("st_conv", l_, h)
                        filled(act, n)
                        fn(win_s[:, l_, :, 4 * h:4 * h + 4, 0:CW - 1],
                           bank(n)[:, 0:C4 * 4 * (CW - 1)].rearrange("p (j b r) -> p j b r", j=C4, b=4),
                           ACT.Copy).then_inc(free_of(n), 1)
                    n = ("st_pool", l_)
                    filled(act, n)
                    fn(pool_s[:, l_, :, :, 0:PW - 1],
                       bank(n)[:, 0:C4 * NS_ * (PW - 1)].rearrange("p (j b r) -> p j b r", j=C4, b=NS_),
                       ACT.Copy).then_inc(free_of(n), 1)
                    n = ("st_lru", l_)
                    filled(act, n)
                    rows = bank(n)[:, 0:P].rearrange("p (j r) -> p j r", j=C4)
                    for j in range(C4):
                        fn(lru_s[:, l_, j, :, 0:LW - 1], rows[:, j, 0:24].rearrange("p (b r) -> p b r", b=NS_),
                           ACT.Copy)
                    fn(h0_s[:, l_, :, :], rows[:, :, 24:32], ACT.Copy).then_inc(free_of(n), 1)

            for l in range(L):
                b0 = mixer_piece(l)
                for s, what in enumerate(IN_ORDER):
                    start = l == 0 and s == 0
                    if start:
                        table(ACT.Sigmoid)
                    hi(b0 + 2 * s + AHEAD)
                    if not start:
                        hi(b0 + 2 * s + 1 + AHEAD)
                    kind = what[0]
                    if s == 14:
                        table(ACT.Sqrt)
                    if s in (4, 5):
                        if l:
                            act.wait_ge(S["x_pool"], 2 * KT)
                        table(ACT.Sigmoid)
                        nm, w, out = ("ra", "lru_ba", rt) if s == 4 else ("ri", "lru_bx", ig)
                        for j in range(C4):
                            n = (nm, l, j)
                            filled(act, n)
                            fn(out[:, j, :], bank(n)[:, 0:T], ACT.Sigmoid, bias=vec(w, l, j)).then_inc(free_of(n), 1)
                    if s == 4:
                        table(ACT.Gelu_apprx_tanh)
                    if s == 6:
                        for j in range(C4):
                            n = ("pm", l, j)
                            filled(act, n)
                            fn(brh[:, j, :], bank(n)[:, 0:T], ACT.Copy, scale=vec("pool_scale", l, j)
                               ).then_inc(S["bp_hi"], 1)
                    if s == 11:
                        act.wait_ge(S["conv_done"], (l + 1) * DT)
                        act.wait_ge(S["cp_ready"], (l + 1) * (C4 - DT))
                        act.wait_ge(S["cw_ready"], (l + 1) * C4)
                        fn(conv_sq, conv, ACT.Square).then_inc(S["csq_done"], 1)
                    for j in range(4):
                        name = ("mix", l, s, j)
                        o = bank(name)
                        if kind == "glu":
                            filled(act, name)
                            fn(sg[:, j, :], o[:, 0:T], ACT.Sigmoid, scale=1 / WS).then_inc(free_of(name), 1)
                        elif kind == "lru":
                            filled(act, name)
                            if j == 0:
                                act.wait_ge(S["zeroed"], l + 1)
                            fn(ulru[:, j, LW - 1:], o[:, 0:TP], ACT.Copy, scale=1 / WS)
                            fn(lru_s[:, l, j, :, LW - 1], o[:, TP:T], ACT.Copy, scale=1 / WS).then_inc(free_of(name), 1)
                        elif kind == "pool":
                            filled(act, name)
                            fn(upool[:, j, PW - 1:], o[:, 0:TP], ACT.Copy, scale=1 / WS)
                            fn(pool_s[:, l, j, :, PW - 1], o[:, TP:T], ACT.Copy, scale=1 / WS).then_inc(free_of(name), 1)
                        elif kind == "gelu":
                            filled(act, name)
                            fn(gelu[:, j, :], o[:, 0:T], ACT.Gelu_apprx_tanh, scale=1 / WS).then_inc(free_of(name), 1)
                        elif kind == "gate":
                            filled(act, name)
                            turn = {0: 0, 2: 1, 1: 2}[what[2]]
                            d = what[3] * 4 + j
                            if turn == 1:
                                read_out(act, ("mix", l, 7, d))
                            elif turn == 2:
                                act.wait_ge(S["merge_done"], l * KT + d + 1)
                            elif d == 0:
                                act.wait_ge(S["pooled_ready"], (l + 1) * C4)
                            fn(gates[:, d, :], o[:, 0:T], ACT.Sigmoid, bias=gate_bias(l, what[2], d),
                               scale=1 / WS).then_inc(free_of(name), 1)
                    if start:
                        hi(b0 + 1 + AHEAD)
                        params()
                    if l == 0 and s == 1:
                        states()
                        act.wait_ge(S["sp_abs"], 1)
                        fn(spt[:, 1], spt[:, 0], ACT.Exp, scale=-1.0).then_inc(S["sp_exp"], 1)
                    if s == 5:
                        filled(act, ("ri", l, C4 - 1))
                        act.wait_ge(S["sp_done"], 1)
                        for j in range(C4):
                            read_out(act, ("ra", l, j))
                            fn(a_lru[:, j, :], rt[:, j, :], ACT.Exp, scale=sp8n[:, j, l:l + 1])
                            fn(rt[:, j, :], rt[:, j, :], ACT.Tanh, scale=sp4[:, j, l:l + 1]).then_inc(S["tanh_ready"], 1)
                    if s == 6:
                        act.wait_ge(S["tanh_ready"], (l + 1) * C4)
                        fn(rt, rt, ACT.Sqrt).then_inc(S["root_ready"], 1)
                    if s == 8:
                        act.wait_ge(S["hg_ready"], l + 1)
                        piece_done(act, b0 + 15)
                        for j in range(C4):
                            fn(brh[:, j, :], rq[:, j, :], ACT.Copy).then_inc(S["br_hi"], 1)
                    if s == 11:
                        filled(act, ("cmean", l))
                        fn(stat[:, 0, :], bank(("cmean", l))[:, 0:T], ACT.Square).then_inc(S["cm2_ready"], 1)
                        act.wait_ge(S["cvar_ready"], l + 1)
                        fn(stat[:, 2, :], stat[:, 1, :], ACT.Sqrt).then_inc(S["cstd_ready"], 1)
                        for j in range(C4):
                            act.wait_ge(S["cv_ready"], l * C4 + j + 1)
                            fn(conv_sq[:, j, :], conv[:, j, :], ACT.Silu, bias=vec("conv_ln_b", l, j),
                               scale=vec("conv_ln_g", l, j)).then_inc(S["silu_ready"], 1)
                        for j in range(C4):
                            act.wait_ge(S["silu_ready"], l * C4 + j + 1)
                            fn(brh[:, j, :], conv_sq[:, j, :], ACT.Copy).then_inc(S["br_hi"], 1)
                    if s == 13:
                        for d in range(KT):
                            act.wait_ge(S["mg_ready"], l * KT + d + 1)
                            fn(xh[:, d, :], merged[:, d, :], ACT.Copy).then_inc(S["mg_hi"], 1)
                        n = ("so", l)
                        filled(act, n)
                        if l:
                            act.wait_ge(S["out_dma"], 16 * (3 * L + 8 * l))
                        fn(so_out[0:81, :], bank(n)[0:81, :], ACT.Copy).then_inc(free_of(n), 1)
                    if kind == "out":
                        for j in range(4):
                            d = what[1] * 4 + j
                            read_out(act, ("mix", l, s, j))
                            fn(zsq[:, d, :], z[:, d, :], ACT.Square).then_inc(S["zsq_ready"], 1)
                norm(2 * l, ("mean", 2 * l), l, "ln1_b")
                if l == 0:
                    n = MIX
                    f = 0
                    for g, nf in enumerate(FG):
                        hi(n + AHEAD)
                        hi(n + 1 + AHEAD)
                        for j in range(nf):
                            filled(act, ("fg", g, j))
                            if g:
                                read_out(act, ("fu", g - 1, j))
                            fn(silu_d[:, j, :], bank(("fg", g, j))[:, 0:T], ACT.Silu,
                               scale=1 / WS).then_inc(free_of(("fg", g, j)), 1)
                        hi(n + 2 + AHEAD)
                        hi(n + 3 + AHEAD)
                        for j in range(nf):
                            read_out(act, ("fu", g, j))
                            fn(hdh[:, f + j, :], h_d[:, j, :], ACT.Copy).then_inc(S["f_hi"], 1)
                        n += 4
                        f += nf
                    for half in range(2):
                        for g in range(len(FG)):
                            hi(n + AHEAD)
                            n += 1
                        if half == 0:
                            table(ACT.Sqrt)
                        for j in range(4 * half, 4 * half + 4):
                            read_out(act, ("fd", j))
                            fn(zsq[:, j, :], z[:, j, :], ACT.Square).then_inc(S["zsq_ready"], 1)
                    norm(1, ("mean", 1), 0, "ln2_b")

            table(ACT.Sigmoid)        
            filled(act, "logits_t")
            fn(logit_rows, bank("logits_t")[0:NE, 0:T], ACT.Copy).then_inc(free_of("logits_t"), 1)
            for i in range(3):
                n = P if i < 2 else NS_
                if i == 2:
                    act.wait_ge(S["gd_ready"], 1)
                    fn(route1[:, 4, :], route1[:, 3, :], ACT.Sigmoid)
                    fn(route1[:, 5, :], route1[:, 3, :], ACT.Sigmoid, scale=-1.0).then_inc(S["gs_ready"], 1)
                    act.wait_ge(S["rows_zeroed"], 6)
                for h in range(2):
                    name = ("xtok", i, h)
                    filled(act, name)
                    fn(xth[0:n, i, h * 512:(h + 1) * 512], bank(name)[0:n, :], ACT.Copy).then_inc(S["xt_hi"], 1)

            def gather_hi(v, wait):
                for h in range(2):
                    wait(act, "gath_hi", h, 6 + h)
                    fn(xgh[:, 4 * h:4 * h + 4, :], ps[:, 6 + h, 0:4 * CAP].rearrange("p (k c) -> p k c", k=4),
                       ACT.Copy).then_inc(bank_free[6 + h], 1)

            def y_hi(v):
                act.wait_ge(*in_visit(bank_free, 7, v, -2))
                for h in range(2):
                    act.wait_ge(*in_visit(bank_full, 4 + h, v, -1))
                    fn(yh[0:CAP, h * 512:(h + 1) * 512], ps[0:CAP, 4 + h, :], ACT.Copy,
                       scale=gate_slot[0:CAP, 0:1]).then_inc(S["y_hi"], 1)

            gather_hi(0, lambda e, part, h, b: filled(e, (part, h)))
            act.wait_ge(S["visits_ready"], 1)
            nv = act.value_load(visits_i[0:1, 0:1], min_val=NE, max_val=3 * NE)
            def visit_done(m):
                back = 0 if m >= 0 else 1
                m %= VISIT
                kind, c, h = order[m]
                if m in part_in_visit:
                    return S["part_used"], v * NPART + (PART0 - back * NPART + part_in_visit.index(m) + 1)
                b, i = {"g": (c % 2, c // 2), "u": (2 + c % 2, c // 2), "d": (5, 2)}[kind]
                return in_visit(bank_full, b, v, i - back * PER_VISIT[b])

            with act.Fori(0, nv) as v:
                def hi_v(m):
                    n = PRE + m
                    act.wait_ge(stage_full[n % SLOTS], v * (16 * VISIT // SLOTS) + 16 * (n // SLOTS + 1))
                    act.wait_ge(*visit_done(m - SLOTS))
                    fn(w_hi[:, n % SLOTS, :], stage[:, n % SLOTS, :], ACT.Copy, scale=WS).then_inc(S["hi_done"], 1)

                for q, (kind, c, h) in enumerate(order):
                    if q == 0:
                        y_hi(v)
                    if q and order[q - 1] == ("g", order[q - 1][1], 1):
                        c, b = order[q - 1][1], order[q - 1][1] % 2
                        act.wait_ge(*in_visit(bank_full, b, v, c // 2))
                        fn(silu_e[:, b, :], ps[:, b, 0:4 * CAP], ACT.Silu, scale=1 / WS).then_inc(bank_free[b], 1)
                    if q > 1 and order[q - 2] == ("u", order[q - 2][1], 1):
                        c, b = order[q - 2][1], order[q - 2][1] % 2
                        act.wait_ge(*in_visit(bank_free, 2 + b, v, c // 2))
                        fn(hh[:, b, :], h_e[:, b, :], ACT.Copy).then_inc(S["e_hi"], 1)
                    if q == GATHER_AT:
                        gather_hi(v + 1, lambda e, part, hf, bk: e.wait_ge(
                            *in_visit(bank_full, bk, v, PER_VISIT[bk] - 1)))
                    if q + SLOTS < VISIT:
                        hi_v(q + SLOTS)
                    else:
                        with act.If(v < nv - 1):
                            hi_v(q + SLOTS)
            y_hi(nv)
            table(ACT.Sqrt)
            for j in range(KT):
                act.wait_ge(*in_visit(bank_free, 4 + j % 4, nv, j // 4))
                fn(zsq[:, j, :], z[:, j, :], ACT.Square).then_inc(S["zsq_ready"], 1)
            norm(3, ("tail", 0, nv), 1, "ln2_b")
            for o, (h, i) in enumerate(OUT_ORDER):
                n = P if i < 2 else NS_
                b = 2 + o % 2
                act.wait_ge(*in_visit(bank_full, b, nv, o // 2))
                fn(y_rows[0:n, i, h * 512:(h + 1) * 512], ps[0:n, b, :], ACT.Copy).then_inc(bank_free[b], 1)
                act.wait_ge(*in_visit(bank_free, b, nv, o // 2))
                dst = (O["y_prompt"][0, i * P:(i + 1) * P, :] if i < 2 else O["y_sample"].rearrange("b s n -> (b s) n"))
                act.dma_start(dst[:, h * 512:(h + 1) * 512], y_rows[0:n, i, h * 512:(h + 1) * 512]
                              ).then_inc(S["y_out"], 16)

        @block.vector
        def _(dve):
            V = nc.vector
            own = Steps(dve, S["dve"])

            def lo(n):
                tiles, width = pre_piece(n)[1:]
                sl = n % SLOTS
                dve.wait_ge(S["hi_done"], n + 1)
                V.scalar_tensor_tensor(w_lo[:, sl, 0:tiles * width], stage[:, sl, 0:tiles * width], WS,
                                       w_hi[:, sl, 0:tiles * width], ALU.mult, ALU.subtract).then_inc(S["lo_done"], 1)

            def norm(q, mean, msq, scale, l, g, bias):
                if mean[0] == "tail":
                    waits = [in_visit(bank_full, b, mean[2], 0) for b in (0, 1)]
                    read = [in_visit(bank_free, b, mean[2], 0) for b in (0, 1)]
                    mu, sq = ps[:, 0, 0:T], ps[:, 1, 0:T]
                else:
                    waits = [(full_of(n), place[n][1] + 1) for n in (mean, msq)]
                    read = [(free_of(n), place[n][1] + 1) for n in (mean, msq)]
                    mu, sq = bank(mean)[:, 0:T], bank(msq)[:, 0:T]
                for w in waits:
                    dve.wait_ge(*w)
                dve.wait_ge(S["m2_ready"], q + 1)
                V.tensor_tensor(stat[:, 1, :], sq, stat[:, 0, :], ALU.subtract).then_inc(read[1][0], 1)
                dve.wait_ge(*read[1])
                V.tensor_scalar(stat[:, 1, :], stat[:, 1, :], 0.0, EPS * scale * scale, ALU.max,
                                ALU.add).then_inc(S["var_ready"], 1)
                def centre(j):
                    t = V.tensor_tensor(z[:, j, :], z[:, j, :], mu, ALU.subtract)
                    if j == KT - 1:
                        t.then_inc(read[0][0], 1)
                    elif j > 3:
                        own.did(t)

                for j in range(4):
                    centre(j)
                dve.wait_ge(S["std_ready"], q + 1)
                own.then(V.reciprocal(stat[:, 0, :], stat[:, 2, :]))
                for j in range(KT):
                    if j == KT - 1:
                        dve.wait_ge(*read[0])
                    elif j > 3:
                        own.after(own.n)
                    V.scalar_tensor_tensor(z[:, j, :], z[:, j, :], vec_d(g, l, j), stat[:, 0, :], ALU.mult,
                                           ALU.mult).then_inc(S["nz_ready"], 1)
                    if 3 <= j < KT - 1:
                        centre(j + 1)
                    if q < 2 and j:
                        x_lo(q, l, bias, j - 1)
                if q < 2:
                    x_lo(q, l, bias, KT - 1)

            def add_up(q, j, name):
                read_out(dve, name)
                add_sum(q, j)

            def add_sum(q, j):
                if 0 < j < NSUM:
                    if j > 1:
                        dve.wait_ge(S["zsum_ready"], q * (NSUM - 1) + j - 1)
                    V.tensor_tensor(zsum, z[:, 0, :] if j == 1 else zsum, z[:, j, :], ALU.add
                                    ).then_inc(S["zsum_ready"], 1)

            def x_lo(q, l, bias, j):
                dve.wait_ge(S["x_hi"], (q + 1) * KT + j + 1)
                V.scalar_tensor_tensor(xl[:, j, :], z[:, j, :], vec_d(bias, l, j), xh[:, j, :], ALU.add,
                                       ALU.subtract).then_inc(S["x_split"], 1)

            V.memset(ones_d[:], 1.0 / D)
            own.did(V.memset(ones_b[:], 1.0 / DB))
            for k in range(KT):
                n = ("xT", k)
                dve.wait_ge(S["x_hi"], k + 1)
                V.tensor_tensor(xl[:, k, :], bank(n)[:, 0:T], xh[:, k, :], ALU.subtract)
                V.tensor_copy(x[:, k, :], bank(n)[:, 0:T]).then_inc(free_of(n), 1)
                if k == 3:
                    lo(0)
            for n in range(1, AHEAD):
                lo(n)
            dve.wait_ge(S["ld_const"], 16)
            own.did(V.tensor_copy(ident16[:, :], ident))
            def softplus():
                r = VEC_B.index("lru_lambda") * L
                lam = par[:, :, r:r + L]
                read_out(dve, "par512")
                read_out(dve, "par1024")
                V.scalar_tensor_tensor(spt[:, 0], lam, -1.0, lam, ALU.mult, ALU.max).then_inc(S["sp_abs"], 1)
                dve.wait_ge(S["sp_exp"], 1)
                own.then(V.tensor_scalar(spt[:, 2], spt[:, 1], 2.0, None, ALU.add))
                own.then(V.reciprocal(spt[:, 3], spt[:, 2]))
                own.then(V.tensor_tensor(spt[:, 2], spt[:, 1], spt[:, 3], ALU.mult))
                own.then(V.tensor_tensor(spt[:, 3], spt[:, 2], spt[:, 2], ALU.mult))
                own.then(V.tensor_scalar(spt[:, 4], spt[:, 3], 1.0 / 15, 1.0 / 13, ALU.mult, ALU.add))
                for k in (11, 9, 7, 5, 3, 1):
                    own.then(V.tensor_tensor(spt[:, 4], spt[:, 4], spt[:, 3], ALU.mult))
                    own.then(V.tensor_scalar(spt[:, 4], spt[:, 4], 1.0 / k, None, ALU.add))
                own.then(V.tensor_tensor(spt[:, 4], spt[:, 4], spt[:, 2], ALU.mult))
                own.then(V.tensor_scalar(spt[:, 5], lam, -1.0, 0.0, ALU.mult, ALU.max))
                own.then(V.scalar_tensor_tensor(spt[:, 3], spt[:, 4], 2.0, spt[:, 5], ALU.mult, ALU.add))
                V.tensor_scalar(sp8n, spt[:, 3], -8.0, None, ALU.mult)
                V.tensor_scalar(sp4[:, :, :], spt[:, 3], 4.0, None, ALU.mult).then_inc(S["sp_done"], 1)

            for l in range(L):
                b0 = mixer_piece(l)
                tap_at = [0] * C4

                def conv_taps(k0, k1):
                    for k in range(k0, k1):
                        for j in range(DT):
                            w = conv_tap(l, j, k)
                            src = glu[:, j, k:k + TP]
                            if k == 0:
                                i = V.tensor_scalar(conv[:, j, 0:TP], src, w, vec("conv_b", l, j), ALU.mult, ALU.add)
                            else:
                                own.after(tap_at[j])
                                i = V.scalar_tensor_tensor(conv[:, j, 0:TP], src, w, conv[:, j, 0:TP],
                                                           ALU.mult, ALU.add)
                            if k == CW - 1:
                                i.then_inc(S["conv_done"], 1)
                            else:
                                tap_at[j] = own.did(i)

                def merge(s, done, then=None):
                    for d in range(KT):
                        name = ("mix", l, s, d)
                        read_out(dve, ("mix", l, s - 2 + d // 4, d % 4))
                        filled(dve, name)
                        out = gates if done else merged
                        V.scalar_tensor_tensor(out[:, d, :], bank(name)[:, 0:T], 1 / WS, gates[:, d, :], ALU.mult,
                                               ALU.mult).then_inc(free_of(name), 1)
                        if done and d:
                            merge_sum(s, d - 1, done)
                        if then and d > 1:
                            then(d - 2)
                    if done:
                        merge_sum(s, KT - 1, done)
                    if then:
                        then(KT - 2)
                        then(KT - 1)

                def merge_sum(s, d, done):
                    read_out(dve, ("mix", l, s, d))
                    V.tensor_tensor(merged[:, d, :], merged[:, d, :], gates[:, d, :], ALU.add).then_inc(S[done], 1)

                def merged_lo(d):
                    dve.wait_ge(S["mg_hi"], l * KT + d + 1)
                    V.tensor_tensor(xl[:, d, :], merged[:, d, :], xh[:, d, :], ALU.subtract
                                    ).then_inc(S["mg_split"], 1)

                if l:
                    dve.wait_ge(S["packed"], 8 * l)
                V.memset(glu[:, :, 0:CW - 1], 0.0)

                for s, what in enumerate(IN_ORDER):
                    lo(b0 + 2 * s + AHEAD)
                    if s != 1 and (s, l) != (15, 0):
                        lo(b0 + 2 * s + 1 + AHEAD)
                    kind = what[0]
                    if kind == "val":
                        for j in range(4):
                            name = ("mix", l, s, j)
                            gl = ("mix", l, 0, j)
                            read_out(dve, gl)
                            filled(dve, name)
                            o = bank(name)
                            V.scalar_tensor_tensor(glu[:, j, CW - 1:], o[:, 0:TP], 1 / WS, sg[:, j, 0:TP], ALU.mult,
                                                   ALU.mult)
                            V.scalar_tensor_tensor(win_s[:, l, j, :, CW - 1], o[:, TP:T], 1 / WS, sg[:, j, TP:T],
                                                   ALU.mult, ALU.mult).then_inc(free_of(name), 1)
                        lo(b0 + 2 * s + 1 + AHEAD)
                        for j in range(4):
                            read_out(dve, ("mix", l, s, j))
                        filled(dve, ("st_lru", L - 1))
                        V.memset(upool[:, :, 0:PW - 1], 0.0)
                        V.memset(ulru[:, :, 0:LW - 1], 0.0).then_inc(S["zeroed"], 1)
                        if l == 0:
                            softplus()
                    if s == 2:
                        dve.wait_ge(S["zeroed"], l + 1)
                        for k in range(LW):
                            for j in range(C4):
                                src = ulru[:, j, k:k + TP]
                                if k == 0:
                                    read_out(dve, ("mix", l, s, j))
                                    i = V.tensor_scalar(xc[:, j, 0:TP], src, lru_tap(l, j, k), vec("lru_conv_b", l, j),
                                                        ALU.mult, ALU.add)
                                else:
                                    own.after(tap_at[j])
                                    i = V.scalar_tensor_tensor(xc[:, j, 0:TP], src, lru_tap(l, j, k),
                                                               xc[:, j, 0:TP], ALU.mult, ALU.add)
                                if k == LW - 1:
                                    i.then_inc(S["xc_ready"], 1)
                                else:
                                    tap_at[j] = own.did(i)
                    if s not in (6, 10):
                        conv_taps(*TAPS_AT[s])
                    if s == 6:
                        for j in range(C4):
                            n = ("pm", l, j)
                            dve.wait_ge(S["bp_hi"], l * C4 + j + 1)
                            V.scalar_tensor_tensor(brl[:, j, :], bank(n)[:, 0:T], vec("pool_scale", l, j),
                                                   brh[:, j, :], ALU.mult, ALU.subtract).then_inc(free_of(n), 1)
                        conv_taps(*TAPS_AT[s])
                        dve.wait_ge(S["tanh_ready"], (l + 1) * C4)
                        dve.wait_ge(S["packed"], 8 * l + 4)
                        dve.wait_ge(S["xc_ready"], (l + 1) * C4)
                        dve.wait_ge(S["xw_ready"], (l + 1) * C4)
                        own.did(V.tensor_tensor(ig, ig, xc, ALU.mult))
                        dve.wait_ge(S["root_ready"], l + 1)
                        own.then(V.scalar_tensor_tensor(rq, a_lru, 1.0, rt, ALU.add, ALU.mult))
                        own.did(V.memset(a_lru[:, :, 0:1], 0.0))
                        own.then(V.memset(rq[:, :, 0:1], 1.0))
                        own.then(V.tensor_tensor(ig, ig, rq, ALU.mult))
                    if s == 7:
                        merge(s, None)
                        dve.wait_ge(S["packed"], 8 * l + 6)
                        for j in range(C4):
                            V.tensor_tensor_scan(hseq[:, j, 0:TP], a_lru[:, j, 0:TP], ig[:, j, 0:TP], 0.0, ALU.mult,
                                                 ALU.add)
                        own.then(V.tensor_tensor(a_lru[:, :, TP:T], a_lru[:, :, TP:T], h0_s[:, l, :, :], ALU.mult))
                        V.tensor_tensor(hseq[:, :, TP:T], a_lru[:, :, TP:T], ig[:, :, TP:T],
                                        ALU.add).then_inc(S["h_ready"], 1)
                        dve.wait_ge(S["h_ready"], l + 1)
                        for j in range(C4):
                            read_out(dve, ("mix", l, 4, j))
                        V.tensor_tensor(rq, hseq, gelu, ALU.mult).then_inc(S["hg_ready"], 1)
                    if s == 8:
                        for j in range(C4):
                            dve.wait_ge(S["br_hi"], 2 * l * C4 + j + 1)
                            V.tensor_tensor(brl[:, j, :], rq[:, j, :], brh[:, j, :],
                                            ALU.subtract).then_inc(S["br_ready"], 1)
                    if s == 10:
                        merge(s, "merge_done")
                        conv_taps(*TAPS_AT[s])
                    if s == 11:
                        filled(dve, ("cmean", l))
                        filled(dve, ("csq", l))
                        dve.wait_ge(S["cm2_ready"], l + 1)
                        mu = bank(("cmean", l))[:, 0:T]
                        V.tensor_tensor(stat[:, 1, :], bank(("csq", l))[:, 0:T], stat[:, 0, :],
                                        ALU.subtract).then_inc(free_of(("csq", l)), 1)
                        read_out(dve, ("csq", l))
                        V.tensor_scalar(stat[:, 1, :], stat[:, 1, :], 0.0, EPS, ALU.max, ALU.add
                                        ).then_inc(S["cvar_ready"], 1)
                        dve.wait_ge(S["conv_done"], (l + 1) * DT)
                        for j in range(C4):
                            t = V.tensor_tensor(conv[:, j, :], conv[:, j, :], mu, ALU.subtract)
                        t.then_inc(free_of(("cmean", l)), 1)
                        dve.wait_ge(S["cstd_ready"], l + 1)
                        read_out(dve, ("cmean", l))
                        own.then(V.reciprocal(stat[:, 0, :], stat[:, 2, :]))
                        for j in range(C4):
                            V.tensor_tensor(conv[:, j, :], conv[:, j, :], stat[:, 0, :],
                                            ALU.mult).then_inc(S["cv_ready"], 1)
                        for j in range(C4):
                            dve.wait_ge(S["br_hi"], (2 * l + 1) * C4 + j + 1)
                            V.tensor_tensor(brl[:, j, :], conv_sq[:, j, :], brh[:, j, :],
                                            ALU.subtract).then_inc(S["br_ready"], 1)
                    if s == 13:
                        merge(s, "mg_ready", merged_lo)
                    if kind == "out":
                        for j in range(4):
                            name = ("mix", l, s, j)
                            d = what[1] * 4 + j
                            filled(dve, name)
                            if l:
                                dve.wait_ge(S["x_pool"], KT + d + 1)
                            V.scalar_tensor_tensor(z[:, d, :], x[:, d, :], WS * ALPHA, bank(name)[:, 0:T], ALU.mult,
                                                   ALU.add).then_inc(free_of(name), 1)
                            add_up(2 * l, d, name)
                norm(2 * l, ("mean", 2 * l), ("msq", 2 * l), WS, l, "ln1_g", "ln1_b")
                if l == 0:
                    lo(MIX - 1 + AHEAD)
                if l == 0:
                    n = MIX
                    f = 0
                    for g, nf in enumerate(FG):
                        for i in range(4):
                            lo(n + i + AHEAD)
                        for j in range(nf):
                            fg, fu = ("fg", g, j), ("fu", g, j)
                            read_out(dve, fg)
                            if g:
                                dve.wait_ge(S["f_split"], f - 4 + j + 1)
                            filled(dve, fu)
                            V.scalar_tensor_tensor(h_d[:, j, :], bank(fu)[:, 0:T], 1 / WS, silu_d[:, j, :], ALU.mult,
                                                   ALU.mult).then_inc(free_of(fu), 1)
                        for j in range(nf):
                            dve.wait_ge(S["f_hi"], f + j + 1)
                            V.tensor_tensor(hdl[:, f + j, :], h_d[:, j, :], hdh[:, f + j, :],
                                            ALU.subtract).then_inc(S["f_split"], 1)
                        n += 4
                        f += nf
                    for half in range(2):
                        for g in range(len(FG)):
                            if n < MIX + FFN - 1:
                                lo(n + AHEAD)
                            n += 1
                        for j in range(4 * half, 4 * half + 4):
                            name = ("fd", j)
                            filled(dve, name)
                            dve.wait_ge(S["x_pool"], j + 1)
                            V.scalar_tensor_tensor(z[:, j, :], x[:, j, :], WS * ALPHA, bank(name)[:, 0:T], ALU.mult,
                                                   ALU.add).then_inc(free_of(name), 1)
                            add_up(1, j, name)
                    norm(1, ("mean", 1), ("msq", 1), WS, 0, "ln2_g", "ln2_b")
                    lo(n - 1 + AHEAD)

            V.memset(gsel[:, :, :], 0.0).then_inc(S["e_split"], 1)
            lg = route[:, 1]
            own.then(V.memset(lg, 0.0))
            own.did(V.memset(rank[:, :, :], -1.0))
            lo(PRE + AHEAD)
            dve.wait_ge(S["norm_ready"], KT)
            for j in range(KT):
                n = own.did(V.tensor_scalar(z[:, j, :], x[:, j, :], WS * ALPHA, None, ALU.mult))
            filled(dve, "logits")
            own.did(V.tensor_copy(lg[:, 0:2, :], bank("logits")[:, 0:2 * NE].rearrange("p (i e) -> p i e", i=2)))
            V.tensor_copy(lg[0:NS_, 2, :], bank("logits")[0:NS_, 2 * NE:3 * NE]).then_inc(free_of("logits"), 1)
            read_out(dve, "logits")
            big = [P, 3, NE]

            def largest(src, sel, m):
                own.then(V.tensor_reduce(m, src, X, ALU.max))
                own.then(V.tensor_tensor(route[:, 8], src, m.unsqueeze(2).to_broadcast(big), ALU.is_equal))
                own.then(V.tensor_tensor(route[:, 8], route[:, 8], idx_w.unsqueeze(1).to_broadcast(big), ALU.mult))
                own.then(V.tensor_reduce(route1[:, 7, :], route[:, 8], X, ALU.max))
                own.then(V.tensor_tensor(sel, route[:, 8], route1[:, 7, :].unsqueeze(2).to_broadcast(big),
                                         ALU.is_equal))

            largest(lg, route[:, 2], route1[:, 0, :])
            own.then(V.scalar_tensor_tensor(route[:, 3], route[:, 2], -1e30, lg, ALU.mult, ALU.add))
            largest(route[:, 3], route[:, 4], route1[:, 1, :])
            V.tensor_tensor(route[:, 0], route[:, 2], route[:, 4], ALU.add).then_inc(S["mask_ready"], 1)
            V.tensor_tensor(route1[:, 3, :], route1[:, 0, :], route1[:, 1, :], ALU.subtract).then_inc(S["gd_ready"], 1)
            def token_lo(i):
                m = P if i < 2 else NS_
                for h in range(2):
                    name = ("xtok", i, h)
                    dve.wait_ge(S["xt_hi"], 2 * i + h + 1)
                    V.tensor_tensor(xtl[0:m, i, h * 512:(h + 1) * 512], bank(name)[0:m, :],
                                    xth[0:m, i, h * 512:(h + 1) * 512], ALU.subtract).then_inc(free_of(name), 1)

            token_lo(0)
            dve.wait_ge(S["mask_ready"], 1)
            filled(dve, "ranks")
            rk = bank("ranks")
            own.did(V.tensor_tensor(route[:, 9, 0:2, :], rk[:, 0:2 * NE].rearrange("p (i e) -> p i e", i=2),
                                    route[:, 0, 0:2, :], ALU.mult))
            own.then(V.tensor_tensor(route[0:NS_, 9, 2, :], rk[0:NS_, 2 * NE:3 * NE], route[0:NS_, 0, 2, :], ALU.mult))
            own.did(V.tensor_scalar(rank[:, 0:2, :], route[:, 9, 0:2, :], float(D), 1.0, ALU.mult, ALU.subtract))
            own.then(V.tensor_scalar(rank[0:NS_, 2, :], route[0:NS_, 9, 2, :], float(D), 1.0, ALU.mult, ALU.subtract))
            V.tensor_reduce(route1[:, 6, 0:1], rk[:, 3 * NE:4 * NE], X, ALU.max).then_inc(free_of("ranks"), 1)
            read_out(dve, "ranks")
            own.then(V.tensor_scalar(route1[:, 6, 1:2], route1[:, 6, 0:1], CAP / D, float(NE), ALU.is_gt, ALU.mult))
            own.then(V.tensor_scalar(route1[:, 6, 2:3], route1[:, 6, 0:1], 2 * CAP / D, float(NE), ALU.is_gt,
                                     ALU.mult))
            own.then(V.tensor_tensor(route1[:, 6, 1:2], route1[:, 6, 1:2], route1[:, 6, 2:3], ALU.add))
            V.tensor_scalar(visits_i[:, :], route1[:, 6, 1:2], float(NE), None, ALU.add).then_inc(S["visits_ready"], 1)
            dve.wait_ge(S["gs_ready"], 1)
            own.then(V.tensor_tensor(route[:, 5], route[:, 2], route1[:, 4, :].unsqueeze(2).to_broadcast(big), ALU.mult))
            own.then(V.tensor_tensor(route[:, 6], route[:, 4], route1[:, 5, :].unsqueeze(2).to_broadcast(big), ALU.mult))
            own.then(V.tensor_tensor(route[:, 7], route[:, 5], route[:, 6], ALU.add))
            own.then(V.tensor_copy(gate_split[:, :, :, 0], route[:, 7]))
            own.then(V.tensor_tensor(gate_split[:, :, :, 1], route[:, 7], gate_split[:, :, :, 0], ALU.subtract))

            def select(v, col):
                dve.wait_ge(S["rank_next"], v)
                for i in range(3):
                    V.tensor_scalar(onehot[:, i, :], iota, rank[:, i, col], None, ALU.is_equal)
                t = V.tensor_copy(gsel, gate_split[:, :, col, :])
                t.then_inc(S["onehot_ready"], 1)
                dve.wait_ge(S["onehot_ready"], v + 1)
                V.tensor_scalar(rank[:, :, col], rank[:, :, col], float(CAP), None, ALU.subtract
                                ).then_inc(S["rank_next"], 1)

            def gather_lo(wait):
                for h in range(2):
                    b = 1 + 2 * h
                    wait(dve, "gath_lo", h, b)
                    V.tensor_copy(xgl[:, 4 * h:4 * h + 4, :], ps[:, b, 0:4 * CAP].rearrange("p (k c) -> p k c", k=4)
                                  ).then_inc(bank_free[b], 1)

            def y_lo(v):
                for h in range(2):
                    dve.wait_ge(S["y_hi"], 2 * v + (h + 1))
                    V.scalar_tensor_tensor(yl[0:CAP, h * 512:(h + 1) * 512], ps[0:CAP, 4 + h, :], gate_slot[0:CAP, 0:1],
                                           yh[0:CAP, h * 512:(h + 1) * 512], ALU.mult, ALU.subtract
                                           ).then_inc(bank_free[4 + h], 1)

            own.after(own.n)
            select(0, slice(0, 1))
            token_lo(1)
            dve.wait_ge(S["rows_zeroed"], 6)
            token_lo(2)
            for h in range(2):
                empty(dve, ("y_init", h))
                V.memset(ps[:, 4 + h, :], 0.0).then_inc(bank_full[4 + h], 1)
            own.after(n)
            gather_lo(lambda e, part, h, b: filled(e, (part, h)))
            nv = dve.value_load(visits_i[0:1, 0:1], min_val=NE, max_val=3 * NE)

            def scatter_add(v, batch, last=False):
                for b in range(4, 8):
                    d = 4 * batch + b - 4
                    dve.wait_ge(*in_visit(bank_full, b, v, batch))
                    V.tensor_tensor(z[:, d, :], z[:, d, :], ps[:, b, 0:T], ALU.add).then_inc(bank_free[b], 1)
                    if last:
                        dve.wait_ge(*in_visit(bank_free, b, v, batch))
                        add_sum(3, d)

            with dve.Fori(0, nv) as v:
                def lo_v(m):
                    n = PRE + m
                    dve.wait_ge(S["hi_done"], v * VISIT + (n + 1))
                    V.scalar_tensor_tensor(w_lo[:, n % SLOTS, :], stage[:, n % SLOTS, :], WS, w_hi[:, n % SLOTS, :],
                                           ALU.mult, ALU.subtract).then_inc(S["lo_done"], 1)

                for q in range(VISIT):
                    if q == 0:
                        y_lo(v)
                    kind, c, h = order[q - 1] if q else ("", 0, 0)
                    if (kind, h) == ("u", 1):
                        b = 2 + c % 2
                        dve.wait_ge(*in_visit(bank_free, b - 2, v, c // 2))
                        dve.wait_ge(*in_visit(bank_full, b, v, c // 2))
                        dve.wait_ge(S["e_split"], v * NC + max(c, 1))
                        V.scalar_tensor_tensor(h_e[:, c % 2, :], ps[:, b, 0:4 * CAP], 1 / WS, silu_e[:, c % 2, :], ALU.mult,
                                               ALU.mult).then_inc(bank_free[b], 1)
                        if c == 0:
                            scatter_add(v, 0)
                        if c == 1:
                            dve.wait_ge(*in_visit(bank_full, 7, v, 2))
                            V.tensor_copy(onehot_t[0:CAP, :], ps[0:CAP, 7, :].bitcast(F16)[:, 0:T])
                            V.tensor_reduce(gate_slot[0:CAP, 0:1], ps[0:CAP, 7, 256:258], X, ALU.add
                                            ).then_inc(bank_free[7], 1)
                    if (kind, c, h) == ("g", 1, 1):
                        scatter_add(v, 1)
                    if (kind, c, h) == ("d", 3, 0):
                        select(v + 1, bass.ds((v + 1) % NE, 1))
                    kind, c, h = order[q - 2] if q > 1 else ("", 0, 0)
                    if (kind, h) == ("u", 1):
                        dve.wait_ge(S["e_hi"], v * NC + (c + 1))
                        V.tensor_tensor(hl[:, c % 2, :], h_e[:, c % 2, :], hh[:, c % 2, :],
                                        ALU.subtract).then_inc(S["e_split"], 1)
                    if q == GATHER_AT:
                        gather_lo(lambda e, part, hf, bk: e.wait_ge(
                            *in_visit(bank_full, bk, v, PER_VISIT[bk] - 1)))
                    if q + SLOTS < VISIT:
                        lo_v(q + SLOTS)
                    else:
                        with dve.If(v < nv - 1):
                            lo_v(q + SLOTS)
            y_lo(nv)
            scatter_add(nv, 0, True)
            scatter_add(nv, 1, True)
            norm(3, ("tail", 0, nv), None, WS, 1, "ln2_g", "ln2_b")


def constants():
    import numpy as np

    c = np.zeros((P, C_ALL), np.float32)
    c[:, C_ID:C_ID + P] = np.eye(P)
    c[:, C_IO:C_IO + CAP] = np.arange(CAP)
    c[:, C_TR:C_TR + P] = np.triu(np.ones((P, P))) / D
    for g, w in enumerate(WINDOWS):
        c[:, C_IC + g * PW:C_IC + (g + 1) * PW] = 1.0 / np.minimum(w, np.arange(PW) + 1)
    c[:, C_IX:C_IX + NE] = NE - np.arange(NE)
    return c


_INS = ["x_prompt", "x_sample", "state_pool", "state_conv", "state_lru_conv", "state_lru_h", "w_in", "b_gate",
        "w_pool", "pool_scale", "conv_w", "conv_b", "conv_ln_g", "conv_ln_b", "lru_conv_w", "lru_conv_b", "lru_wa",
        "lru_ba", "lru_wx", "lru_bx", "lru_lambda", "w_br_pool", "w_br_conv", "w_br_lru", "w_out", "ln1_g", "ln1_b",
        "ln2_g", "ln2_b", "ffn_w_gate", "ffn_w_up", "ffn_w_down", "moe_router", "moe_w_gate", "moe_w_up",
        "moe_w_down"]
_OUTS = {"y_prompt": (1, TP, D), "y_sample": (NS_, 1, D), "pool_p": (L, 1, PW - 1, DB), "conv_p": (L, 1, CW - 1, DB),
         "lconv_p": (L, 1, LW - 1, DB), "h_p": (L, 1, DB), "pool_s": (L, NS_, PW - 1, DB),
         "conv_s": (L, NS_, CW - 1, DB), "lconv_s": (L, NS_, LW - 1, DB), "h_s": (L, NS_, DB)}


def kernel(**inputs):
    import numpy as np
    import concourse.bacc as bacc
    from concourse.bass_utils import run_bass_kernel_spmd

    nc = bacc.Bacc("TRN2", target_bir_lowering=False, num_devices=1)
    arrays, ins, outs = {}, {}, {}
    for name in _INS:
        arrays[f"in_{name}"] = np.ascontiguousarray(inputs[name])
        ins[name] = nc.dram_tensor(f"in_{name}", arrays[f"in_{name}"].shape, F32, kind="ExternalInput").ap()
    arrays["in_consts"] = constants()
    ins["consts"] = nc.dram_tensor("in_consts", (P, C_ALL), F32, kind="ExternalInput").ap()
    for name, shape in _OUTS.items():
        outs[name] = nc.dram_tensor(f"out_{name}", shape, F32, kind="ExternalOutput").ap()
    trunk_kernel(nc, ins, outs)
    r = run_bass_kernel_spmd(nc, [arrays], core_ids=[0])
    return tuple(r.results[0][f"out_{name}"] for name in _OUTS)
```
